# Optimizing a Trainium2 kernel written in Bass

```python
import math
import jax, jax.numpy as jnp
from jax import lax
import numpy as np

D_MODEL = 2048
BATCH = 1
SEQ = 512
DEPTH = 1

CHUNK = 64
EPS = 1e-6
SSM_WIDTH = D_MODEL // 4
SSM_GROUP = 16
SSM_GROUPS = SSM_WIDTH // SSM_GROUP
SSM_STATE = 64
MLSTM_WIDTH = D_MODEL - SSM_WIDTH
MLSTM_HEADS = 4
MLSTM_HEAD_DIM = MLSTM_WIDTH // MLSTM_HEADS
CONV_WIDTH = 4
PEER_HEADS = 8
PEER_QUERY_DIM = 256
PEER_NKEYS = 128
PEER_TOPK = 16
PEER_EXPERTS = PEER_NKEYS * PEER_NKEYS
PEER_TOKEN_BLOCK = 128
IN_SPLITS = (SSM_WIDTH, MLSTM_WIDTH, MLSTM_WIDTH, MLSTM_HEADS, MLSTM_HEADS, D_MODEL, D_MODEL)
IN_WIDTH = sum(IN_SPLITS)
IN_OFFSETS = tuple(int(o) for o in np.cumsum(IN_SPLITS)[:-1])

kernel_name = 'hybrid_s5_mlstm_peer_block'

def rmsnorm(x, g):
    xf = x.astype(jnp.float32)
    y = xf * lax.rsqrt(jnp.mean(xf * xf, axis=-1, keepdims=True) + EPS)
    return (y * g.astype(jnp.float32)).astype(x.dtype)

def s5_branch(u, lam_re, lam_im, log_dt, b_re, b_im, c_re, c_im, d_skip, w_glu):
    bsz, seq, _ = u.shape
    f32 = jnp.float32
    uf = u.astype(f32).reshape(bsz, seq, SSM_GROUPS, SSM_GROUP)
    lam = lax.complex(lam_re.astype(f32), lam_im.astype(f32))
    dt = jnp.exp(log_dt.astype(f32))[:, None]
    a_bar = jnp.exp(lam * dt)
    b_bar = ((a_bar - 1.0) / lam)[..., None] * lax.complex(b_re.astype(f32), b_im.astype(f32))
    bu = jnp.einsum('gph,bsgh->bsgp', b_bar, uf.astype(jnp.complex64))
    a_full = jnp.broadcast_to(a_bar, bu.shape)

    def combine(left, right):
        a_l, b_l = left
        a_r, b_r = right
        return a_r * a_l, a_r * b_l + b_r

    _, states = lax.associative_scan(combine, (a_full, bu), axis=1)
    c = lax.complex(c_re.astype(f32), c_im.astype(f32))
    y = jnp.real(jnp.einsum('ghp,bsgp->bsgh', c, states)) + d_skip.astype(f32).reshape(SSM_GROUPS, SSM_GROUP) * uf
    y = jax.nn.gelu(y.reshape(bsz, seq, SSM_WIDTH)).astype(u.dtype)
    val, gate = jnp.split(y @ w_glu, 2, axis=-1)
    return val * jax.nn.sigmoid(gate)

def causal_conv(x, w, b):
    seq = x.shape[1]
    xp = jnp.pad(x, ((0, 0), (CONV_WIDTH - 1, 0), (0, 0)))
    out = b
    for j in range(CONV_WIDTH):
        out = out + xp[:, j:j + seq] * w[j]
    return out

def _to_chunks(t):
    b, s = t.shape[:2]
    t = t.reshape((b, s // CHUNK, CHUNK) + t.shape[2:])
    t = jnp.swapaxes(t, 2, 3)
    return jnp.moveaxis(t, 1, 0)

def mlstm_chunkwise(q, k, v, i_pre, logf):
    bsz, seq, nh, dk = q.shape
    dv = v.shape[-1]
    f32 = jnp.float32
    causal = jnp.tril(jnp.ones((CHUNK, CHUNK), dtype=bool))

    def step(carry, inp):
        c_prev, n_prev, m_prev = carry
        qc, kc, vc, ic, fc = inp
        bcum = jnp.cumsum(fc, axis=-1)
        log_w = bcum[..., :, None] - bcum[..., None, :] + ic[..., None, :]
        log_w = jnp.where(causal, log_w, -jnp.inf)
        log_inter = bcum + m_prev[..., None]
        m_t = jnp.maximum(log_inter, jnp.max(log_w, axis=-1))
        w = jnp.exp(log_w - m_t[..., None])
        inter = jnp.exp(log_inter - m_t)
        sw = jnp.einsum('bhtd,bhsd->bhts', qc, kc) * w
        num = jnp.einsum('bhts,bhse->bhte', sw, vc) + inter[..., None] * jnp.einsum('bhed,bhtd->bhte', c_prev, qc)
        den = jnp.sum(sw, axis=-1) + inter * jnp.einsum('bhd,bhtd->bht', n_prev, qc)
        h = num / jnp.maximum(jnp.abs(den), jnp.exp(-m_t))[..., None]
        b_last = bcum[..., -1]
        m_new = m_t[..., -1]
        w_end = jnp.exp(b_last[..., None] - bcum + ic - m_new[..., None])
        decay = jnp.exp(b_last + m_prev - m_new)
        c_new = decay[..., None, None] * c_prev + jnp.einsum('bhs,bhse,bhsd->bhed', w_end, vc, kc)
        n_new = decay[..., None] * n_prev + jnp.einsum('bhs,bhsd->bhd', w_end, kc)
        return (c_new, n_new, m_new), h

    init = (jnp.zeros((bsz, nh, dv, dk), f32), jnp.zeros((bsz, nh, dk), f32), jnp.zeros((bsz, nh), f32))
    xs = (_to_chunks(q), _to_chunks(k), _to_chunks(v), _to_chunks(i_pre), _to_chunks(logf))
    _, hs = lax.scan(step, init, xs)
    hs = jnp.swapaxes(jnp.moveaxis(hs, 0, 1), 2, 3)
    return hs.reshape(bsz, seq, nh, dv)

def mlstm_branch(xm, z, i_raw, f_raw, conv_w, conv_b, w_q, w_k, w_v, b_i, b_f, mh_gain, skip, w_proj):
    bsz, seq, _ = xm.shape
    f32 = jnp.float32
    heads = lambda t: t.reshape(bsz, seq, MLSTM_HEADS, MLSTM_HEAD_DIM)
    xc = jax.nn.silu(causal_conv(xm, conv_w, conv_b))
    q = jnp.einsum('bshd,hde->bshe', heads(xc), w_q).astype(f32)
    k = (jnp.einsum('bshd,hde->bshe', heads(xc), w_k) * MLSTM_HEAD_DIM ** -0.5).astype(f32)
    v = jnp.einsum('bshd,hde->bshe', heads(xm), w_v).astype(f32)
    i_pre = (i_raw + b_i).astype(f32)
    logf = jax.nn.log_sigmoid((f_raw + b_f).astype(f32))
    h = mlstm_chunkwise(q, k, v, i_pre, logf)
    h = jax.nn.sigmoid(heads(z).astype(f32)) * h
    mu = jnp.mean(h, axis=-1, keepdims=True)
    var = jnp.mean(jnp.square(h - mu), axis=-1, keepdims=True)
    h = ((h - mu) * lax.rsqrt(var + EPS)).reshape(bsz, seq, MLSTM_WIDTH)
    h = h * mh_gain.astype(f32) + skip.astype(f32) * xc.astype(f32)
    return h.astype(xm.dtype) @ w_proj

def peer(h, w_query, key1, key2, expert_u, expert_v):
    bsz, seq, d = h.shape
    n_tok = bsz * seq
    hk = PEER_HEADS * PEER_TOPK
    t = h.reshape(n_tok, d)
    qr = (t @ w_query).reshape(n_tok, PEER_HEADS, PEER_QUERY_DIM)
    q1, q2 = jnp.split(qr, 2, axis=-1)
    s1 = jnp.einsum('thd,hnd->thn', q1, key1).astype(jnp.float32)
    s2 = jnp.einsum('thd,hnd->thn', q2, key2).astype(jnp.float32)
    v1, i1 = lax.top_k(s1, PEER_TOPK)
    v2, i2 = lax.top_k(s2, PEER_TOPK)
    cand = (v1[..., :, None] + v2[..., None, :]).reshape(n_tok, PEER_HEADS, PEER_TOPK * PEER_TOPK)
    cand_idx = (i1[..., :, None] * PEER_NKEYS + i2[..., None, :]).reshape(n_tok, PEER_HEADS, PEER_TOPK * PEER_TOPK)
    top_s, pos = lax.top_k(cand, PEER_TOPK)
    experts = jnp.take_along_axis(cand_idx, pos, axis=-1)
    gates = jax.nn.softmax(top_s, axis=-1).astype(h.dtype)

    def block(args):
        tb, eb, gb = args
        u = jnp.take(expert_u, eb, axis=0)
        act = jax.nn.gelu(jnp.einsum('ted,td->te', u, tb)) * gb
        vv = jnp.take(expert_v, eb, axis=0)
        return jnp.einsum('te,ted->td', act, vv)

    nb = n_tok // PEER_TOKEN_BLOCK
    out = lax.map(block, (t.reshape(nb, PEER_TOKEN_BLOCK, d),
                          experts.reshape(nb, PEER_TOKEN_BLOCK, hk),
                          gates.reshape(nb, PEER_TOKEN_BLOCK, hk)))
    return out.reshape(bsz, seq, d)

def setup_inputs(seed: int = 0) -> dict:
    key = jax.random.key(seed)
    keys = jax.random.split(key, 40)
    cnt = [0]
    f32 = jnp.float32

    def nk():
        cnt[0] += 1
        return keys[cnt[0] - 1]

    def nrm(shape, scale):
        return jax.random.normal(nk(), shape, f32) * scale

    L = DEPTH
    G, P, H = SSM_GROUPS, SSM_STATE, SSM_GROUP
    hd = MLSTM_HEAD_DIM
    half = PEER_QUERY_DIM // 2
    return {
        'x': nrm((BATCH, SEQ, D_MODEL), 1.0),
        'norm1_g': 1.0 + nrm((L, D_MODEL), 0.02),
        'w_in': nrm((L, D_MODEL, IN_WIDTH), D_MODEL ** -0.5),
        'lam_re': -0.5 + nrm((L, G, P), 0.01),
        'lam_im': jnp.pi * jnp.arange(P, dtype=f32) + nrm((L, G, P), 0.01),
        'log_dt': jax.random.uniform(nk(), (L, G), f32, math.log(1e-3), math.log(1e-1)),
        'b_re': nrm((L, G, P, H), (2 * H) ** -0.5),
        'b_im': nrm((L, G, P, H), (2 * H) ** -0.5),
        'c_re': nrm((L, G, H, P), (2 * P) ** -0.5),
        'c_im': nrm((L, G, H, P), (2 * P) ** -0.5),
        'd_skip': nrm((L, SSM_WIDTH), 1.0),
        'w_glu': nrm((L, SSM_WIDTH, 2 * D_MODEL), SSM_WIDTH ** -0.5),
        'conv_w': nrm((L, CONV_WIDTH, MLSTM_WIDTH), 0.5),
        'conv_b': nrm((L, MLSTM_WIDTH), 0.02),
        'w_q': nrm((L, MLSTM_HEADS, hd, hd), hd ** -0.5),
        'w_k': nrm((L, MLSTM_HEADS, hd, hd), hd ** -0.5),
        'w_v': nrm((L, MLSTM_HEADS, hd, hd), hd ** -0.5),
        'b_i': nrm((L, MLSTM_HEADS), 0.1),
        'b_f': jnp.linspace(3.0, 6.0, MLSTM_HEADS, dtype=f32) + nrm((L, MLSTM_HEADS), 0.1),
        'mh_gain': 1.0 + nrm((L, MLSTM_WIDTH), 0.02),
        'mlstm_skip': 1.0 + nrm((L, MLSTM_WIDTH), 0.02),
        'w_mlstm_out': nrm((L, MLSTM_WIDTH, D_MODEL), MLSTM_WIDTH ** -0.5),
        'w_out': nrm((L, D_MODEL, D_MODEL), D_MODEL ** -0.5),
        'norm2_g': 1.0 + nrm((L, D_MODEL), 0.02),
        'w_query': nrm((L, D_MODEL, PEER_HEADS * PEER_QUERY_DIM), D_MODEL ** -0.5),
        'key1': nrm((L, PEER_HEADS, PEER_NKEYS, half), half ** -0.5),
        'key2': nrm((L, PEER_HEADS, PEER_NKEYS, half), half ** -0.5),
        'expert_u': nrm((L, PEER_EXPERTS, D_MODEL), D_MODEL ** -0.5),
        'expert_v': nrm((L, PEER_EXPERTS, D_MODEL), (PEER_HEADS * PEER_TOPK) ** -0.5),
        'norm_f_g': 1.0 + nrm((D_MODEL,), 0.02),
    }

def reference(x, norm1_g, w_in, lam_re, lam_im, log_dt, b_re, b_im, c_re, c_im, d_skip, w_glu,
              conv_w, conv_b, w_q, w_k, w_v, b_i, b_f, mh_gain, mlstm_skip, w_mlstm_out, w_out,
              norm2_g, w_query, key1, key2, expert_u, expert_v, norm_f_g):
    h = x
    for l in range(DEPTH):
        hn = rmsnorm(h, norm1_g[l])
        proj = hn @ w_in[l]
        u_ssm, xm, z, i_raw, f_raw, g_a, g_b = jnp.split(proj, IN_OFFSETS, axis=-1)
        y_a = s5_branch(u_ssm, lam_re[l], lam_im[l], log_dt[l], b_re[l], b_im[l],
                        c_re[l], c_im[l], d_skip[l], w_glu[l])
        y_b = mlstm_branch(xm, z, i_raw, f_raw, conv_w[l], conv_b[l], w_q[l], w_k[l], w_v[l],
                           b_i[l], b_f[l], mh_gain[l], mlstm_skip[l], w_mlstm_out[l])
        merged = jax.nn.sigmoid(g_a) * y_a + jax.nn.sigmoid(g_b) * y_b
        h = h + merged @ w_out[l]
        h = h + peer(rmsnorm(h, norm2_g[l]), w_query[l], key1[l], key2[l], expert_u[l], expert_v[l])
    return rmsnorm(h, norm_f_g)


_drawn_inputs = setup_inputs


def setup_inputs(seed=0):
    import zlib

    import numpy as np

    out = dict(_drawn_inputs(seed))
    spreads = {}
    factors = {'lam_re': 64.0,
     'lam_im': 40.656,
     'log_dt': 42.48,
     'b_re': 55.344,
     'b_im': 56.032,
     'c_re': 55.68,
     'c_im': 56.568,
     'conv_b': 3.374,
     'b_i': 200.0,
     'mh_gain': 17.695,
     'mlstm_skip': 31.009,
     'norm2_g': 26.517,
     'norm_f_g': 23.239}
    for name, (base, spread) in spreads.items():
        noise = np.random.default_rng([zlib.crc32(name.encode()), seed]).standard_normal(out[name].shape)
        drawn = base * np.exp(spread * noise) if base else spread * noise
        out[name] = __import__('jax').numpy.asarray(drawn.astype(out[name].dtype))
    for name, factor in factors.items():
        out[name] = (out[name] * factor).astype(out[name].dtype)
    return out
```

```python
from contextlib import ExitStack

import numpy as np

import concourse.bass as bass
from concourse import mybir

ALU = mybir.AluOpType
ACT = mybir.ActivationFunctionType
AX_X = mybir.AxisListType.X
F32 = mybir.dt.float32
F32R = mybir.dt.float32r
I32 = mybir.dt.int32
U32 = mybir.dt.uint32

P = 128
T = 512
D = 2048
KC = D // P
SSM_W, ML_W, HEADS, HD = 512, 1536, 4, 384
SC, MC, HC = SSM_W // P, ML_W // P, HD // P
TB = T // P
STATE, GROUP, GROUPS = 64, 16, 32
PH, NKEY, TOPK = 8, 128, 16
EPS = 1e-6
UNIT = 2048

U_SSM, U_XM, U_Z, U_GA, U_GB = 0, 4, 16, 28, 44
U_GLU, U_QKV, U_YB, U_WO, U_WQ = 60, 68, 76, 92, 108
U_EXP = 124
GROUPS_E = 32
N_STREAM = U_EXP + 8 * GROUPS_E
O_GLU, O_QKV, O_YB, O_WO, O_WQ, O_EXP = 60, 92, 132, 148, 164, 180

V_G1, V_G2, V_GF, V_DSKIP, V_CW, V_CB, V_GAIN, V_SKIP = 0, 16, 32, 48, 52, 100, 112, 124
V_LRE, V_LIM, V_LDT, V_BI, V_BF, N_VEC = 136, 152, 168, 184, 185, 186

LOG2E, LN2_HI, LN2_LO = 1.4426950408889634, 0.693359375, -2.12194440e-4
ROUND = 12582912.0
HALF_PI = (1.5703125, 4.837512969970703125e-4, 7.54978995489188216e-8)
NEG_BIG = -3.0e38
S5_STEPS, ML_STEPS, PK_STEPS = 164, 27, 67


def build(nc, a, out_d):
    ctx = ExitStack()
    with ctx:
        base = (nc.sbuf_base + 63) // 64 * 64
        room = nc.sbuf_usable_end - base

        def S(name, shape, dt, kb):
            size = 4 * int(np.prod(shape[1:]))
            assert kb * 1024 + size <= room, (name, kb * 1024 + size, room)
            return nc.alloc_sbuf_tensor_at(name, shape, dt, offset=base + int(kb * 1024))

        def sem(name):
            return ctx.enter_context(nc.semaphore(name))

        raw = S("raw", [P, 2, UNIT], F32, 0)
        whi = S("whi", [P, 2, UNIT], F32R, 16)
        wlo = S("wlo", [P, 2, UNIT], F32R, 32)
        vec = S("vec", [P, N_VEC], F32, 202)
        ones = S("ones", [P, P], F32, 202.75)
        ones_r = S("ones_r", [P, P], F32R, 203.25)
        ident = S("ident", [P, P], F32, 203.75)
        tri = S("tri", [P, P], F32, 204.25)
        iota = S("iota", [P, P], F32, 204.75)
        rs = S("rs", [P, T], F32, 205.25)
        sq = S("sq", [P, 2, T], F32, 176)
        ms = S("ms", [P, T], F32, 180)
        nt = S("nt", [P, T], F32, 182)
        xt = S("xt", [P, 2, T], F32, 184)
        hn_hi = S("hn_hi", [P, KC, T], F32R, 48)
        hn_lo = S("hn_lo", [P, KC, T], F32R, 80)
        x = S("x", [P, KC, T], F32, 112)
        uT = S("uT", [P, SC, T], F32, 144)
        stage = S("stage", [P, 2, T], F32, 152)
        cp = S("cp", [P, 2, 16, 32], F32, 156)
        craw = S("craw", [P, 2, 16, 32], F32, 160)
        wif = S("wif", [P, KC, 64], F32, 164)
        bc = S("bc", [P, 2, P], F32, 168)
        cc = S("cc", [P, 2, 4, 32], F32, 169)
        pc = S("pc", [P, 2, 9, 4], F32, 170)
        rc = S("rc", [P, 8], F32, 170.5)
        cw = S("cw", [P, 40, 16], F32, 171)
        ptab = S("ptab", [P, 2, 9, 16], F32, 174)
        gt = S("gt", [P, 4, T], F32, 184)
        gout = S("gout", [P, 3, T], F32, 192)
        tab = S("tab", [P, 2, 2, T], F32, 112)
        bus = S("bus", [P, 2, T], F32, 120)
        rin = S("rin", [P, 2, T], F32, 124)
        wst = S("wst", [P, 2, T], F32, 128)
        rout = S("rout", [P, 2, T], F32, 132)
        dtmp = S("dtmp", [P, 2, T], F32, 136)
        ptmp = S("ptmp", [P, 2, T], F32, 140)
        uc = S("uc", [P, T], F32, 198)
        y_hi = S("y_hi", [P, SC, T], F32R, 176)
        y_lo = S("y_lo", [P, SC, T], F32R, 184)
        sgt = S("sgt", [P, 2, T], F32, 112)
        vt = S("vt", [P, 2, T], F32, 116)
        sa = S("sa", [P, 2, T], F32, 132)
        xc_hi = S("xc_hi", [P, MC, T], F32R, 48)
        xc_lo = S("xc_lo", [P, MC, T], F32R, 72)
        q_hi = S("q_hi", [P, HC, T], F32R, 96)
        q_lo = S("q_lo", [P, HC, T], F32R, 102)
        k_hi = S("k_hi", [P, HC, T], F32R, 108)
        k_lo = S("k_lo", [P, HC, T], F32R, 114)
        v_hi = S("v_hi", [P, TB, HD], F32R, 120)
        v_lo = S("v_lo", [P, TB, HD], F32R, 126)
        p_hi = S("p_hi", [P, TB, T], F32R, 132)
        p_lo = S("p_lo", [P, TB, T], F32R, 140)
        m_bc = S("m_bc", [P, T], F32, 148)
        em_bc = S("em_bc", [P, T], F32, 150)
        xmr = S("xmr", [P, HC, T], F32, 152)
        sz = S("sz", [P, HC, T], F32, 158)
        cv = S("cv", [P, 2, T], F32, 164)
        xcf = S("xcf", [P, 2, T], F32, 168)
        pf = S("pf", [P, 2, T], F32, 172)
        xm_hi = S("xm_hi", [P, HC, T], F32R, 176)
        xm_lo = S("xm_lo", [P, HC, T], F32R, 182)
        ex = S("ex", [P, 2, T], F32, 188)
        hh = S("hh", [P, HC, T], F32, 192)
        rd = S("rd", [P, T], F32, 198)
        gcol = S("gcol", [P, TB], F32, 200)
        mg_hi = S("mg_hi", [P, KC, T], F32R, 96)
        mg_lo = S("mg_lo", [P, KC, T], F32R, 128)
        yal = S("yal", [P, 2, T], F32, 160)
        sbl = S("sbl", [P, 2, T], F32, 164)
        mt = S("mt", [P, 2, T], F32, 168)
        xres = S("xres", [P, 2, T], F32, 172)
        h2 = S("h2", [P, KC, T], F32, 48)
        t_hi = S("t_hi", [P, KC, T], F32R, 96)
        t_lo = S("t_lo", [P, KC, T], F32R, 128)
        key_hi = S("key_hi", [P, PH, 2, NKEY], F32R, 160)
        key_lo = S("key_lo", [P, PH, 2, NKEY], F32R, 168)
        key_raw = S("key_raw", [P, PH, 2, NKEY], F32, 188)
        qq_hi = S("qq_hi", [P, 2, T], F32R, 80)
        qq_lo = S("qq_lo", [P, 2, T], F32R, 84)
        tw = S("tw", [P, 256], F32, 196)
        v12 = S("v12", [P, 2, TB, TOPK], F32, 197)
        i12u = S("i12u", [P, 2, TB, TOPK], U32, 197.5)
        i12 = S("i12", [P, 2, TB, TOPK], F32, 198)
        cand = S("cand", [P, TB, TOPK, TOPK], F32, 88)
        eq = S("eq", [P, TB * TOPK, TOPK], F32, 92)
        tv = S("tv", [P, TB, TOPK], F32, 198.5)
        pos = S("pos", [P, TB, TOPK], U32, 198.75)
        ab_u = S("ab_u", [P, 2, TB, TOPK], U32, 199)
        ab = S("ab", [P, 2, TB, TOPK], F32, 199.5)
        ge = S("ge", [P, TB, TOPK], F32, 200)
        gz = S("gz", [P, 2, TB], F32, 200.25)
        slot = S("slot", [P, 3, TB, PH, TOPK], F32, 176)
        slot_t = S("slot_t", [P, 3, T], F32, 80)
        hot_a = S("hot_a", [P, 8, 2, P], F32, 86)
        hot_b = S("hot_b", [P, 8, 2, P], F32, 194)
        gst = S("gst", [P, 2, P, 32], F32, 160)
        gl = S("gl", [P, 2, T], F32, 192)
        af = S("af", [P, 2, T], F32, 196)
        gg = S("gg", [P, 2, 16, P], F32, 80)
        act_hi = S("act_hi", [P, 2, 4, T], F32R, 160)
        act_lo = S("act_lo", [P, 2, 4, T], F32R, 176)
        fin = S("fin", [P, 2, T], F32, 96)

        def bank(name):
            return ctx.enter_context(nc.psum_tensor(name, [P, T], F32))

        mm = [bank("mm0"), bank("mm1")]
        sb_ = [bank("sc0"), bank("sc1")]
        dn, st = bank("dn"), bank("st")
        pv = [bank("pv0"), bank("pv1")]
        vo = [pv[0], pv[1], sb_[0], sb_[1]]

        hsq = (ex[:, 0, :], ex[:, 1, :], pf[:, 0, :])
        eqs = (eq[:], cand[:].rearrange("p b k a -> p (b k) a"))

        spill = nc.dram_tensor("spill", (56, P, T), F32).ap()
        ya_d = nc.dram_tensor("ya_d", (KC, P, T), F32).ap()
        gates_d = nc.dram_tensor("gates_d", (3, HEADS, T), F32).ap()
        g_d = nc.dram_tensor("g_d", (16, P, P, 32), F32).ap()

        raw_in = [sem("raw_in0"), sem("raw_in1")]
        hi_done, lo_done = sem("hi_done"), sem("lo_done")
        proj_done, proj_free = sem("proj_done"), sem("proj_free")
        vec_in, x_in = sem("vec_in"), [sem(f"x_in{i}") for i in range(4)]
        wif_in, craw_in = sem("wif_in"), sem("craw_in")
        const_done, onesr_done = sem("const_done"), sem("onesr_done")
        sq_done, ssq_done, rt_done, rs_done = sem("sq_done"), sem("ssq_done"), sem("rt_done"), sem("rs_done")
        xn_done, ahi_done, alo_done = sem("xn_done"), sem("ahi_done"), sem("alo_done")
        stage_out = [sem("stage_out0"), sem("stage_out1")]
        if_done, ge_sem, gates_done, gates_out = sem("if_done"), sem("ge_sem"), sem("gates_done"), sem("gates_out")
        coef_done, chunk_done, bc_in = sem("coef_done"), sem("chunk_done"), sem("bc_in")
        bu_done, bus_done, tab_done, rot_done = sem("bu_done"), sem("bus_done"), sem("tab_done"), sem("rot_done")
        prot_done, scan_done, out_r_done, out_i_done = sem("prot_done"), sem("scan_done"), sem("out_r_done"), sem("out_i_done")
        cm_done, yp_done, yg_done, yhi_done, ylo_done = sem("cm_done"), sem("yp_done"), sem("yg_done"), sem("yhi_done"), sem("ylo_done")
        sg_done, ya_done = sem("sg_done"), sem("ya_done")
        sa_in, ya_out = [sem("sa_in0"), sem("sa_in1")], [sem("ya_out0"), sem("ya_out1")]
        xm_in, sz_in, bcst_in = sem("xm_in"), sem("sz_in"), sem("bcst_in")
        cv_done, silu_done, xchi_done, xclo_done = sem("cv_done"), sem("silu_done"), sem("xchi_done"), sem("xclo_done")
        xmhi_done, xmlo_done = sem("xmhi_done"), sem("xmlo_done")
        qkv_hi_done = sem("qkv_hi_done")
        s_done, en_done, ex_done = sem("s_done"), sem("en_done"), sem("ex_done")
        pf_done, phi_done, plo_done = sem("pf_done"), sem("phi_done"), sem("plo_done")
        den_done, pv_done, pv_free, hz_done = sem("den_done"), sem("pv_done"), sem("pv_free"), sem("hz_done")
        mu_done, hc_done, hsq_done, var_done = sem("mu_done"), sem("hc_done"), sem("hsq_done"), sem("var_done")
        std_done, xs_done, hf_done, hfhi_done, hflo_done = sem("std_done"), sem("xs_done"), sem("hf_done"), sem("hfhi_done"), sem("hflo_done")
        yl_in = [sem("yl_in0"), sem("yl_in1")]
        mt_done, mghi_done, mglo_done = sem("mt_done"), sem("mghi_done"), sem("mglo_done")
        xr_in = [sem("xr_in0"), sem("xr_in1")]
        key_in, khi_done, klo_done = sem("key_in"), sem("khi_done"), sem("klo_done")
        qhi_done, sco_done, sco_free = sem("qqhi_done"), sem("sco_done"), sem("sco_free")
        gsub_done, gexp_done, eqm_done, slot_done = sem("gsub_done"), sem("gexp_done"), sem("eqm_done"), sem("slot_done")
        eq_done = sem("eq_done")
        tr_done, trc_done = sem("tr_done"), sem("trc_done")
        hot_done, hot_used, gps_free = sem("hot_done"), sem("hot_used"), sem("gps_free")
        gst_out = [sem("gst_out0"), sem("gst_out1")]
        g_in = sem("g_in")
        af_done, acthi_done, actlo_done = sem("af_done"), sem("acthi_done"), sem("actlo_done")
        v_done, v_free = sem("v_done"), sem("v_free")
        fin_done, fin_out = sem("fin_done"), [sem("fin_out0"), sem("fin_out1")]
        dve_step, pool_step = sem("dve_step"), sem("pool_step")
        s5_step, ml_step, pk_step = sem("s5_step"), sem("ml_step"), sem("pk_step")
        waited = sem("waited")
        ms_done, msd_done = sem("ms_done"), sem("msd_done")

        block = ctx.enter_context(nc.Block())

        @block.sync
        def _(sp):
            for i in range(4):
                sp.dma_start(x[:, 4 * i:4 * i + 4, :], a["xT"][:, 4 * i:4 * i + 4, :]).then_inc(x_in[i], 16)
            for k in range(2):
                sp.dma_start(raw[:, k, :], a["stream"][k]).then_inc(raw_in[k], 16)
            with sp.Fori(1, N_STREAM // 2) as m:
                for k in range(2):
                    sp.wait_ge(hi_done, 2 * m + k - 1)
                    sp.wait_ge(lo_done, 2 * m + k - 1)
                    sp.dma_start(raw[:, k, :], a["stream"][2 * m + k]).then_inc(raw_in[k], 16)

        @block.gpsimd
        def _(pool):
            n = [0]

            def step(ins):
                n[0] += 1
                ins.then_inc(pool_step, 1)
                pool.wait_ge(pool_step, n[0])

            pool.dma_start(vec[:], a["vecs"]).then_inc(vec_in, 16)
            pool.memset(ones[:], 1.0).then_inc(const_done, 1)
            pool.dma_start(wif[:], a["wif"]).then_inc(wif_in, 16)
            pool.dma_start(craw[:], a["c_tab"]).then_inc(craw_in, 16)
            pool.dma_start(bc[:], a["b_tab"][0]).then_inc(bc_in, 16)
            step(pool.memset(ident[:], 0.0))
            step(pool.memset(tri[:], 1.0))
            pool.affine_select(out=ident[:], in_=ident[:], compare_op=ALU.not_equal, fill=1.0, base=0,
                               pattern=[[-1, P]], channel_multiplier=1).then_inc(const_done, 1)
            pool.affine_select(out=tri[:], in_=tri[:], compare_op=ALU.is_ge, fill=0.0, base=0,
                               pattern=[[1, P]], channel_multiplier=-1).then_inc(const_done, 1)
            pool.iota(iota[:], [[1, P]], base=0, channel_multiplier=0,
                      allow_small_or_imprecise_dtypes=True).then_inc(const_done, 1)

            pool.wait_ge(gates_done, 1)
            pool.dma_start(gates_d.rearrange("g h t -> h g t"), gout[0:HEADS, :, :]).then_inc(gates_out, 16)

            pool.wait_ge(coef_done, 1)
            pool.wait_ge(proj_free, SC)
            with pool.Fori(0, SC) as c:
                pool.wait_ge(cm_done, 4 * c)
                pool.wait_ge(ylo_done, c)
                pool.tensor_copy(uc[:], uT[:, c, :])
                for r in range(2):
                    pool.tensor_copy(cc[:, r, :, :], cp[:, r, :, :].rearrange("p (c k) h -> p c k h", c=4)[:, c, :, :])
                    pool.tensor_copy(pc[:, r, :, :],
                                     ptab[:, r, :, :].rearrange("p n (c k) -> p c n k", c=4)[:, c, :, :])
                pool.tensor_copy(rc[:, 0:4], cw[:, 0, :].rearrange("p (c k) -> p c k", c=4)[:, c, :])
                pool.tensor_copy(rc[:, 4:5], vec[:, V_DSKIP:V_DSKIP + SC].rearrange("p (c k) -> p c k", k=1)[:, c, :])\
                    .then_inc(chunk_done, 1)
                for k in range(4):
                    pool.wait_ge(bus_done, 8 * c + 2 * k + 2)
                    pool.wait_ge(tab_done, 4 * c + k + 1)
                    pool.tensor_tensor(ptmp[:, 0, :], bus[:, 1, :], tab[:, k % 2, 0, :], ALU.mult).then_inc(pool_step, 1)
                    pool.tensor_tensor(ptmp[:, 1, :], bus[:, 0, :], tab[:, k % 2, 1, :], ALU.mult).then_inc(pool_step, 1)
                    pool.wait_ge(pool_step, 2 + 16 * c + 4 * k + 2)
                    pool.wait_ge(scan_done, 8 * c + 2 * k)
                    pool.tensor_tensor(rin[:, 1, :], ptmp[:, 0, :], ptmp[:, 1, :], ALU.subtract).then_inc(prot_done, 1)
                    pool.wait_ge(prot_done, 4 * c + k + 1)
                    pool.wait_ge(scan_done, 8 * c + 2 * k + 2)
                    pool.tensor_tensor(ptmp[:, 0, :], wst[:, 0, :], tab[:, k % 2, 1, :], ALU.mult).then_inc(pool_step, 1)
                    pool.tensor_tensor(ptmp[:, 1, :], wst[:, 1, :], tab[:, k % 2, 0, :], ALU.mult).then_inc(pool_step, 1)
                    pool.wait_ge(pool_step, 2 + 16 * c + 4 * k + 4)
                    pool.wait_ge(cm_done, 4 * c + k)
                    pool.tensor_tensor(rout[:, 1, :], ptmp[:, 0, :], ptmp[:, 1, :], ALU.add).then_inc(out_i_done, 1)
                pool.wait_ge(bu_done, 8 * c + 8)
                pool.dma_start(bc[:], a["b_tab"][c + 1]).then_inc(bc_in, 16)

            pool.wait_ge(cm_done, 16)
            for b in range(2):
                pool.wait_ge(stage_out[b], 16 * 28)
                pool.dma_start(sa[:, b, :], spill[U_GA - U_XM + b]).then_inc(sa_in[b], 16)

            def glu_block(p, b):
                pool.wait_ge(proj_free, O_GLU + 4 * p + 2 * b + 2)
                pool.wait_ge(sa_in[b], 16 * p + 16)
                pool.tensor_tensor(vt[:, b, :], vt[:, b, :], sa[:, b, :], ALU.mult).then_inc(ya_done, 1)
                pool.wait_ge(ya_done, 2 * p + b + 1)
                pool.dma_start(ya_d[2 * p + b], vt[:, b, :]).then_inc(ya_out[b], 16)

            with pool.Fori(0, KC // 2 - 1) as p:
                for b in range(2):
                    glu_block(p, b)
                    pool.dma_start(sa[:, b, :], spill[U_GA - U_XM + 2 * p + b + 2]).then_inc(sa_in[b], 16)
            for b in range(2):
                glu_block(KC // 2 - 1, b)
            for b in range(2):
                pool.wait_ge(ya_out[b], 16 * 8)

            pool.wait_ge(gates_out, 16)
            with pool.Fori(0, HEADS) as h:
                pool.wait_ge(xmlo_done, 3 * h)
                pool.wait_ge(cv_done, 3 * h)
                pool.dma_start(xmr[:], spill[0:MC].rearrange("(h c) p t -> h p c t", c=HC)[h]).then_inc(xm_in, 16)
                pool.wait_ge(hz_done, 3 * h)
                pool.dma_start(sz[:], spill[MC:2 * MC].rearrange("(h c) p t -> h p c t", c=HC)[h]).then_inc(sz_in, 16)
                pool.wait_ge(en_done, 4 * h)
                pool.wait_ge(pv_free, 3 * h)
                pool.dma_start(m_bc[:], gates_d[1, h].partition_broadcast(P)).then_inc(bcst_in, 16)
                pool.dma_start(em_bc[:], gates_d[2, h].partition_broadcast(P)).then_inc(bcst_in, 16)
                with nc.allow_non_contiguous_dma(reason="one value a partition"):
                    pool.dma_start(gcol[:], gates_d[0, h].rearrange("(s p) -> p s", p=P)).then_inc(bcst_in, 16)
                for c in range(HC):
                    pool.wait_ge(xmhi_done, 3 * h + c + 1)
                    if c == 0:
                        pool.wait_ge(proj_done, O_QKV + 10 * h)
                    pool.tensor_tensor(xm_lo[:, c, :], xmr[:, c, :], xm_hi[:, c, :].bitcast(F32), ALU.subtract)\
                        .then_inc(xmlo_done, 1)
                pool.wait_ge(sz_in, 16 * h + 16)
                for c in range(HC):
                    pool.wait_ge(pv_free, 3 * h + c + 1)
                    pool.tensor_tensor(hh[:, c, :], hh[:, c, :], sz[:, c, :], ALU.mult).then_inc(hz_done, 1)
                pool.wait_ge(xclo_done, 3 * h + 3)
                for c in range(HC):
                    if c >= 2:
                        pool.wait_ge(hf_done, 3 * h + c - 1)
                    pool.tensor_tensor(xcf[:, c % 2, :], xc_hi[:, 3 * h + c, :].bitcast(F32),
                                       xc_lo[:, 3 * h + c, :].bitcast(F32), ALU.add).then_inc(xs_done, 1)

            pool.wait_ge(hf_done, 12)
            for b in range(2):
                pool.dma_start(yal[:, b, :], ya_d[b]).then_inc(yl_in[b], 16)
                pool.dma_start(sbl[:, b, :], spill[U_GB - U_XM + b]).then_inc(yl_in[b], 16)
            with pool.Fori(1, KC // 2) as p:
                for b in range(2):
                    pool.wait_ge(mt_done, 2 * p + b - 1)
                    pool.dma_start(yal[:, b, :], ya_d[2 * p + b]).then_inc(yl_in[b], 16)
                    pool.dma_start(sbl[:, b, :], spill[U_GB - U_XM + 2 * p + b]).then_inc(yl_in[b], 16)
            for b in range(2):
                pool.dma_start(xres[:, b, :], a["xT"][:, b, :]).then_inc(xr_in[b], 16)
            with pool.Fori(1, KC // 2) as p:
                for b in range(2):
                    pool.wait_ge(proj_free, O_WO + 2 * p + b - 1)
                    pool.dma_start(xres[:, b, :], a["xT"][:, 2 * p + b, :]).then_inc(xr_in[b], 16)
            pool.dma_start(key_raw[:], a["keys"]).then_inc(key_in, 16)

            with pool.Fori(0, PH) as hd:
                for k in range(2):
                    nm, nk = (U_WQ // 2 + hd, 1) if k == 0 else (U_WQ // 2 + hd + 1, 0)
                    pool.wait_ge(hi_done, 2 * nm + nk + 1)
                    pool.tensor_tensor(wlo[:, nk, :], raw[:, nk, :], whi[:, nk, :].bitcast(F32), ALU.subtract)\
                        .then_inc(lo_done, 1)
                for r in range(2):
                    pool.wait_ge(eq_done, 2 * hd + r + 1)
                    for tb in range(TB):
                        e = eqs[r][:, tb * TOPK:(tb + 1) * TOPK, :]
                        last = pool.tensor_tensor(
                            e, e, i12[:, r, tb, :].unsqueeze(1).to_broadcast([P, TOPK, TOPK]), ALU.mult)
                    last.then_inc(eqm_done, 1)

            with pool.Fori(0, 8) as r:
                for s in range(2):
                    pool.wait_ge(gps_free, 2 + 16 * r + 8 * s + 8)
                    pool.dma_start(g_d[2 * r + s], gst[:, s, :, :]).then_inc(gst_out[s], 16)
            for s in range(2):
                pool.wait_ge(gst_out[s], 16 * 8)

            gg_src = g_d.rearrange("n i (g j) t -> g i n (j t)", j=4)
            for g in range(2):
                pool.wait_ge(g_in, 16 * g)
                pool.dma_start(gg[:, g, :, :], gg_src[g]).then_inc(g_in, 16)
            with pool.Fori(2, GROUPS_E) as g:
                pool.wait_ge(g_in, 16 * g)
                pool.wait_ge(af_done, 4 * g - 4)
                pool.dma_start(gg[:, g % 2, :, :], gg_src[g]).then_inc(g_in, 16)

            with pool.Fori(0, KC // 2) as p:
                for b in range(2):
                    pool.wait_ge(fin_done, 2 * p + b + 1)
                    pool.dma_start(out_d[:, 2 * p + b, :], fin[:, b, :]).then_inc(fin_out[b], 16)
            for b in range(2):
                pool.wait_ge(fin_out[b], 16 * 8)

        @block.scalar
        def _(act):
            def met():
                act.wait_ge(const_done, 4)

            def split_hi(m, k, free=None):
                act.wait_ge(raw_in[k], 16 * m + 16)
                if free is not None:
                    act.wait_ge(*free)
                act.activation(whi[:, k, :], raw[:, k, :], ACT.Copy).then_inc(hi_done, 1)

            def next_hi(m, k, free):
                nm, nk = (m, 1) if k == 0 else (m + 1, 0)
                split_hi(nm, nk, free)

            def squares(r, src):
                for d in range(KC):
                    if 16 * r + d >= 2:
                        act.wait_ge(ssq_done, 16 * r + d - 1)
                    if r == 0 and d % 4 == 0:
                        act.wait_ge(x_in[d // 4], 16)
                    act.activation(sq[:, d % 2, :], src[:, d, :], ACT.Square).then_inc(sq_done, 1)
                act.wait_ge(ms_done, r + 1)
                act.activation(rs[:], ms[:], ACT.Sqrt).then_inc(rt_done, 1)

            act.wait_ge(const_done, 4)
            act.activation(ones_r[:], ones[:], ACT.Copy).then_inc(onesr_done, 1)
            squares(0, x)
            split_hi(0, 0)
            with act.Fori(0, KC) as d:
                met()
                act.wait_ge(xn_done, d + 1)
                act.activation(hn_hi[:, d, :], x[:, d, :], ACT.Copy).then_inc(ahi_done, 1)

            for nu in range(SC):
                next_hi(nu // 2, nu % 2, (proj_done, nu))
                act.wait_ge(proj_done, nu + 1)
                act.activation(uT[:, nu, :], mm[nu % 2][:], ACT.Copy).then_inc(proj_free, 1)

            def spilled(m, k, func):
                next_hi(m, k, (proj_done, 2 * m + k))
                act.wait_ge(proj_done, 2 * m + k + 1)
                act.wait_ge(stage_out[k], 16 * (m - U_XM // 2))
                act.activation(stage[:, k, :], mm[k][:], func).then_inc(proj_free, 1)
                act.wait_ge(proj_free, 2 * m + k + 1)
                act.dma_start(spill[2 * m + k - U_XM], stage[:, k, :]).then_inc(stage_out[k], 16)

            with act.Fori(U_XM // 2, U_Z // 2) as m:
                for k in range(2):
                    spilled(m, k, ACT.Copy)
            act.wait_ge(ge_sem, 1)
            act.activation(gt[0:HEADS, 2, :], gt[0:HEADS, 1, :], ACT.Exp, scale=-1.0).then_inc(ge_sem, 1)
            with act.Fori(U_Z // 2, U_GA // 2 - 1) as m:
                for k in range(2):
                    spilled(m, k, ACT.Sigmoid)
            act.wait_ge(ge_sem, 3)
            act.activation(gout[0:HEADS, 2, :], gt[0:HEADS, 0, :], ACT.Exp, scale=-1.0).then_inc(gates_done, 1)
            for k in range(2):
                spilled(U_GA // 2 - 1, k, ACT.Sigmoid)

            with act.Fori(0, SC) as c:
                for k in range(4):
                    m = U_GA // 2 + 4 * c + k
                    spilled(m, 0, ACT.Sigmoid)
                    for r in range(2):
                        act.wait_ge(bu_done, 8 * c + 2 * k + r + 1)
                        if r == 0:
                            act.wait_ge(prot_done, 4 * c + k)
                            act.wait_ge(rot_done, 4 * c + k)
                        act.activation(bus[:, r, :], sb_[r][:], ACT.Copy).then_inc(bus_done, 1)
                    spilled(m, 1, ACT.Sigmoid)
                act.wait_ge(yp_done, c + 1)
                act.activation(dtmp[:, 0, :], dtmp[:, 0, :], ACT.Gelu_apprx_tanh).then_inc(yg_done, 1)
                met()
                act.wait_ge(yg_done, c + 1)
                act.activation(y_hi[:, c, :], dtmp[:, 0, :], ACT.Copy).then_inc(yhi_done, 1)

            with act.Fori(0, 4) as q:
                for k in range(2):
                    next_hi(U_GLU // 2 + q, k, (proj_done, O_GLU + 8 * q + 4 * k))
                    for b in range(2):
                        act.wait_ge(proj_done, O_GLU + 8 * q + 4 * k + 2 * b + 2)
                        act.wait_ge(proj_free, O_GLU + 8 * q + 4 * k + 2 * b - 2)
                        act.activation(sgt[:, b, :], mm[1][:], ACT.Sigmoid).then_inc(sg_done, 1)

            with act.Fori(0, HEADS) as h:
                split_hi(U_QKV // 2 + h, 1, (proj_done, O_QKV + 10 * h))
                act.wait_ge(xm_in, 16 * h + 16)
                for c in range(HC):
                    act.activation(xm_hi[:, c, :], xmr[:, c, :], ACT.Copy).then_inc(xmhi_done, 1)
                for c in range(HC):
                    act.wait_ge(cv_done, 3 * h + c + 1)
                    act.wait_ge(hflo_done, 3 * h)
                    if c == 2:
                        act.wait_ge(xclo_done, 3 * h + 1)
                    act.activation(xcf[:, c % 2, :], cv[:, c % 2, :], ACT.Silu).then_inc(silu_done, 1)
                    met()
                    act.wait_ge(silu_done, 3 * h + c + 1)
                    act.activation(xc_hi[:, 3 * h + c, :], xcf[:, c % 2, :], ACT.Copy).then_inc(xchi_done, 1)
                for j in range(10):
                    act.wait_ge(proj_done, O_QKV + 10 * h + j + 1)
                    if j < 3:
                        act.activation(q_hi[:, j, :], mm[j % 2][:], ACT.Copy).then_inc(qkv_hi_done, 1)
                    elif j < 6:
                        act.activation(k_hi[:, j - 3, :], mm[j % 2][:], ACT.Copy, scale=HD ** -0.5)\
                            .then_inc(qkv_hi_done, 1)
                    else:
                        act.activation(v_hi[:, j - 6, :], mm[j % 2][:, 0:HD], ACT.Copy).then_inc(qkv_hi_done, 1)
                split_hi(U_QKV // 2 + h + 1, 0, (proj_done, O_QKV + 10 * h + 10))
                for s in range(TB):
                    w = T - P * s
                    act.wait_ge(en_done, 4 * h + s + 1)
                    act.activation(ex[:, s % 2, 0:w], ex[:, s % 2, 0:w], ACT.Exp).then_inc(ex_done, 1)
                    act.wait_ge(pf_done, 4 * h + s + 1)
                    act.activation(p_hi[:, s, P * s:T], pf[:, s % 2, 0:w], ACT.Copy).then_inc(phi_done, 1)
                for c in range(HC):
                    act.wait_ge(hc_done, 3 * h + c + 1)
                    act.activation(hsq[c], hh[:, c, :], ACT.Square).then_inc(hsq_done, 1)
                act.wait_ge(msd_done, h + 1)
                act.activation(rs[:], cv[:, 0, :], ACT.Sqrt).then_inc(std_done, 1)
                for c in range(HC):
                    met()
                    act.wait_ge(hf_done, 3 * h + c + 1)
                    act.activation(xc_hi[:, 3 * h + c, :], hh[:, c, :], ACT.Copy).then_inc(hfhi_done, 1)

            with act.Fori(0, KC // 2) as p:
                for k in range(2):
                    next_hi(U_YB // 2 + p, k, (proj_done, O_YB + 2 * p + k))
                    met()
                    act.wait_ge(mt_done, 2 * p + k + 1)
                    act.activation(mg_hi[:, 2 * p + k, :], mt[:, k, :], ACT.Copy).then_inc(mghi_done, 1)
            with act.Fori(0, KC // 2) as p:
                for k in range(2):
                    next_hi(U_WO // 2 + p, k, (proj_done, O_WO + 2 * p + k))
            act.wait_ge(proj_free, O_WQ)
            squares(1, h2)
            with act.Fori(0, KC // 2) as p:
                for k in range(2):
                    met()
                    act.wait_ge(xn_done, KC + 2 * p + k + 1)
                    act.activation(t_hi[:, 2 * p + k, :], xt[:, k, :], ACT.Copy).then_inc(ahi_done, 1)
            act.wait_ge(key_in, 16)
            act.activation(key_hi[:], key_raw[:], ACT.Copy).then_inc(khi_done, 1)

            with act.Fori(0, PH) as hd:
                for k in range(2):
                    next_hi(U_WQ // 2 + hd, k, (proj_done, O_WQ + 2 * hd + k))
                    act.wait_ge(proj_done, O_WQ + 2 * hd + k + 1)
                    act.wait_ge(sco_done, 2 * hd)
                    act.activation(qq_hi[:, k, :], mm[k][:], ACT.Copy).then_inc(qhi_done, 1)
                act.wait_ge(gsub_done, hd + 1)
                act.activation(ge[:], ge[:], ACT.Exp).then_inc(gexp_done, 1)

            for v in range(3):
                act.wait_ge(tr_done, v + 1)
                act.activation(slot_t[:, v, :], (dn, pv[0], pv[1])[v][:], ACT.Copy).then_inc(trc_done, 1)
            act.sem_inc(gps_free, 2)
            with act.Fori(0, 8) as r:
                for s in range(2):
                    act.wait_ge(gst_out[s], 16 * r)
                    with act.Fori(0, 2) as q:
                        for b in range(2):
                            for v in range(2):
                                met()
                                act.wait_ge(hot_used, 16 + 64 * r + 32 * s + 16 * q + 8 * b + 4 * v + 4)
                                act.activation(
                                    gst[:, s, :, :].rearrange("p j (q b v t) -> p q b v j t", q=2, b=2, v=2)
                                    [:, q, b, v, :, :],
                                    sb_[v][:].rearrange("p (t j) -> p j t", t=4), ACT.Copy).then_inc(gps_free, 1)

            for jj in range(4):
                next_hi((U_EXP + jj) // 2, jj % 2, (proj_done, O_EXP + jj))
                act.wait_ge(proj_done, O_EXP + jj + 1)
                if jj >= 2:
                    act.wait_ge(af_done, jj - 1)
                act.activation(gl[:, jj % 2, :], mm[jj % 2][:], ACT.Gelu_apprx_tanh).then_inc(proj_free, 1)
                act.wait_ge(af_done, jj + 1)
                act.activation(act_hi[:, 0, jj, :], af[:, jj % 2, :], ACT.Copy).then_inc(acthi_done, 1)
            with act.Fori(0, GROUPS_E - 1) as g:
                for jj in range(4):
                    m = (U_EXP + 4) // 2 + 4 * g + jj
                    if jj == 0:
                        act.wait_ge(proj_done, O_EXP + 4)
                    split_hi(m, 1, (v_done, 16 * g + 4 * jj))
                    act.wait_ge(proj_done, O_EXP + 4 * g + jj + 5)
                    act.wait_ge(af_done, 4 * g + jj + 3)
                    act.activation(gl[:, jj % 2, :], mm[jj % 2][:], ACT.Gelu_apprx_tanh).then_inc(proj_free, 1)
                    split_hi(m + 1, 0, (proj_done, O_EXP + 4 * g + jj + 5))
                    met()
                    if jj == 0:
                        act.wait_ge(v_done, 16 * g)
                    act.wait_ge(af_done, 4 * g + jj + 5)
                    act.activation(act_hi[:, (g + 1) % 2, jj, :], af[:, jj % 2, :], ACT.Copy).then_inc(acthi_done, 1)
            for jj in range(3):
                nu = U_EXP + 4 + 8 * (GROUPS_E - 1) + jj + 1
                split_hi(nu // 2, nu % 2, (v_done, 16 * (GROUPS_E - 1) + 4 * jj))

            act.wait_ge(v_free, 16 * GROUPS_E)
            squares(2, h2)

        @block.vector
        def _(dve):
            n = [0]

            def step(ins):
                n[0] += 1
                ins.then_inc(dve_step, 1)
                dve.wait_ge(dve_step, n[0])

            def stepper(s, at):
                k = [0]

                def one(ins, wait=True, apart=False):
                    k[0] += 1
                    ins.then_inc(s, 1)
                    if wait:
                        dve.wait_ge(s, at + k[0])
                    if apart:
                        carrier()
                return one, k

            def carrier():
                dve.sem_inc(waited, 1)

            def split_lo(m, k):
                dve.wait_ge(hi_done, 2 * m + k + 1)
                dve.tensor_tensor(wlo[:, k, :], raw[:, k, :], whi[:, k, :].bitcast(F32), ALU.subtract)\
                    .then_inc(lo_done, 1)

            def next_lo(m, k):
                nm, nk = (m, 1) if k == 0 else (m + 1, 0)
                split_lo(nm, nk)

            def newton(one, y, ms_, tmp):
                one(dve.tensor_tensor(tmp, y, y, ALU.mult))
                one(dve.tensor_tensor(tmp, tmp, ms_, ALU.mult))
                one(dve.tensor_scalar(tmp, tmp, -0.5, 1.5, ALU.mult, ALU.add))
                one(dve.tensor_tensor(y, y, tmp, ALU.mult))

            def norm_scale(r):
                dve.wait_ge(ssq_done, KC * (r + 1))
                dve.tensor_scalar(ms[:], st[:], 1.0 / D, EPS, ALU.mult, ALU.add).then_inc(ms_done, 1)
                dve.wait_ge(rt_done, r + 1)
                step(dve.reciprocal(rs[:], rs[:]))
                dve.wait_ge(ms_done, r + 1)
                newton(step, rs[:], ms[:], nt[:])

            def cols(v0, nv):
                return vec[:, v0:v0 + nv].rearrange("p (d o) -> p d o", o=1)

            dve.wait_ge(vec_in, 16)
            norm_scale(0)

            def xn(d):
                dve.scalar_tensor_tensor(x[:, d, :], x[:, d, :], cols(V_G1, KC)[:, d, :], rs[:],
                                         ALU.mult, ALU.mult).then_inc(xn_done, 1)

            def xlo(d):
                dve.wait_ge(ahi_done, d + 1)
                dve.tensor_tensor(hn_lo[:, d, :], x[:, d, :], hn_hi[:, d, :].bitcast(F32), ALU.subtract)\
                    .then_inc(alo_done, 1)

            split_lo(0, 0)
            xn(0)
            with dve.Fori(1, KC) as d:
                xn(d)
                xlo(d - 1)
            xlo(KC - 1)

            for nu in range(SC):
                next_lo(nu // 2, nu % 2)

            C = {}

            def col(name):
                if name not in C:
                    C[name] = len(C)
                return cw[:, C[name], :]

            def ts(o, i, s1, s2, o1, o2=None):
                step(dve.tensor_scalar(o, i, s1, s2, o1, o2) if o2 is not None else
                     dve.tensor_scalar(o, i, s1, None, o1))

            def tt(o, i, j, op):
                step(dve.tensor_tensor(o, i, j, op))

            def stt(o, i, s, j, o1, o2):
                step(dve.scalar_tensor_tensor(o, i, s, j, o1, o2))

            radius = col("radius")

            def exp_of(o, i):
                xx, nn, rr, qq = col("xx"), col("nn"), col("rr"), col("qq")
                ts(xx, i, -88.02, 89.0, ALU.max, ALU.min)
                ts(nn, xx, LOG2E, ROUND, ALU.mult, ALU.add)
                ts(nn, nn, -ROUND, None, ALU.add)
                stt(rr, nn, -LN2_HI, xx, ALU.mult, ALU.add)
                stt(rr, nn, -LN2_LO, rr, ALU.mult, ALU.add)
                ts(qq, rr, 1.0 / 5040, None, ALU.mult)
                for c in (1.0 / 720, 1.0 / 120, 1.0 / 24, 1.0 / 6, 0.5, 1.0):
                    stt(qq, qq, c, rr, ALU.add, ALU.mult)
                ts(xx.bitcast(I32), nn, 127.0, 8388608.0, ALU.add, ALU.mult)
                stt(o, qq, 1.0, xx, ALU.add, ALU.mult)

            lre, lim, ldt = (vec[:, v:v + 16] for v in (V_LRE, V_LIM, V_LDT))
            dt, th = col("dt"), col("th")
            exp_of(dt, ldt)
            tt(th, lre, dt, ALU.mult)
            exp_of(radius, th)
            tt(th, lim, dt, ALU.mult)
            nn, rr, zz, ss, co = col("nn"), col("rr"), col("zz"), col("ss"), col("co")
            ts(nn, th, 2.0 / np.pi, ROUND, ALU.mult, ALU.add)
            ts(nn, nn, -ROUND, None, ALU.add)
            stt(rr, nn, -HALF_PI[0], th, ALU.mult, ALU.add)
            stt(rr, nn, -HALF_PI[1], rr, ALU.mult, ALU.add)
            stt(rr, nn, -HALF_PI[2], rr, ALU.mult, ALU.add)
            tt(zz, rr, rr, ALU.mult)
            ts(ss, zz, -1.9515295891e-4, None, ALU.mult)
            stt(ss, ss, 8.3321608736e-3, zz, ALU.add, ALU.mult)
            stt(ss, ss, -1.6666654611e-1, zz, ALU.add, ALU.mult)
            stt(ss, ss, 1.0, rr, ALU.add, ALU.mult)
            ts(co, zz, 2.443315711809948e-5, None, ALU.mult)
            stt(co, co, -1.388731625493765e-3, zz, ALU.add, ALU.mult)
            stt(co, co, 4.166664568298827e-2, zz, ALU.add, ALU.mult)
            stt(co, co, -0.5, zz, ALU.add, ALU.mult)
            ts(co, co, 1.0, None, ALU.add)
            ni, bi, b0, b1 = col("ni").bitcast(I32), col("bi").bitcast(I32), col("b0"), col("b1")
            step(dve.tensor_copy(ni, nn))
            ts(bi, ni, 1, None, ALU.bitwise_and)
            step(dve.tensor_copy(b0, bi))
            ts(bi, ni, 1, 1, ALU.arith_shift_right, ALU.bitwise_and)
            step(dve.tensor_copy(b1, bi))
            ts(b1, b1, -2.0, 1.0, ALU.mult, ALU.add)
            d1, d2, e1, e2 = col("d1"), col("d2"), col("e1"), col("e2")
            ts(d2, b0, -1.0, 1.0, ALU.mult, ALU.add)
            tt(e1, ss, d2, ALU.mult)
            tt(e2, co, b0, ALU.mult)
            tt(e1, e1, e2, ALU.add)
            tt(ptab[:, 1, 0, :], e1, b1, ALU.mult)
            tt(e1, co, d2, ALU.mult)
            tt(e2, ss, b0, ALU.mult)
            tt(e1, e1, e2, ALU.subtract)
            tt(ptab[:, 0, 0, :], e1, b1, ALU.mult)
            for i in range(1, 9):
                c0, s0 = ptab[:, 0, i - 1, :], ptab[:, 1, i - 1, :]
                tt(e1, c0, c0, ALU.mult)
                tt(e2, s0, s0, ALU.mult)
                tt(ptab[:, 0, i, :], e1, e2, ALU.subtract)
                stt(ptab[:, 1, i, :], c0, 2.0, s0, ALU.mult, ALU.mult)
            fr, fi = col("fr"), col("fi")
            tt(d1, radius, ptab[:, 0, 0, :], ALU.mult)
            ts(d1, d1, -1.0, None, ALU.add)
            tt(d2, radius, ptab[:, 1, 0, :], ALU.mult)
            tt(e1, lre, lre, ALU.mult)
            tt(e2, lim, lim, ALU.mult)
            tt(zz, e1, e2, ALU.add)
            step(dve.reciprocal(zz, zz))
            tt(e1, d1, lre, ALU.mult)
            tt(e2, d2, lim, ALU.mult)
            tt(e1, e1, e2, ALU.add)
            tt(fr, e1, zz, ALU.mult)
            tt(e1, d2, lre, ALU.mult)
            tt(e2, d1, lim, ALU.mult)
            tt(e1, e1, e2, ALU.subtract)
            tt(fi, e1, zz, ALU.mult)
            dve.wait_ge(craw_in, 16)
            dve.wait_ge(if_done, 1)
            frb = fr.unsqueeze(2).to_broadcast([P, 16, 32])
            fib = fi.unsqueeze(2).to_broadcast([P, 16, 32])
            cr, ci = craw[:, 0, :, :], craw[:, 1, :, :]
            w0 = dtmp[:, 0, :].rearrange("p (q h) -> p q h", q=16)
            tt(w0, cr, frb, ALU.mult)
            tt(cp[:, 0, :, :], ci, fib, ALU.mult)
            tt(cp[:, 0, :, :], w0, cp[:, 0, :, :], ALU.subtract)
            tt(w0, ci, frb, ALU.mult)
            tt(cp[:, 1, :, :], cr, fib, ALU.mult)
            tt(cp[:, 1, :, :], w0, cp[:, 1, :, :], ALU.add)
            dve.tensor_scalar(cp[:, 1, :, :], cp[:, 1, :, :], -1.0, None, ALU.mult).then_inc(coef_done, 1)

            with dve.Fori(U_XM // 2, U_Z // 2) as m:
                for k in range(2):
                    next_lo(m, k)

            gi, g1, g2, gf = (gt[0:HEADS, i, :] for i in range(4))
            go, gm, g5 = (gout[0:HEADS, i, :] for i in range(3))
            ts(gi, pv[0][0:HEADS, :], vec[0:HEADS, V_BI:V_BI + 1], None, ALU.add)
            ts(gf, pv[0][32:32 + HEADS, :], vec[32:32 + HEADS, V_BF:V_BF + 1], None, ALU.add)
            dve.scalar_tensor_tensor(g1, gf, -1.0, gf, ALU.mult, ALU.max).then_inc(ge_sem, 1)
            with dve.Fori(U_Z // 2, U_GA // 2 - 1) as m:
                for k in range(2):
                    next_lo(m, k)
            dve.wait_ge(ge_sem, 2)
            ts(g1, g2, 2.0, None, ALU.add)
            step(dve.reciprocal(g1, g1))
            tt(g1, g2, g1, ALU.mult)
            tt(go, g1, g1, ALU.mult)
            ts(g2, go, 1.0 / 17, None, ALU.mult)
            for d in (15, 13, 11, 9, 7, 5, 3):
                stt(g2, g2, 1.0 / d, go, ALU.add, ALU.mult)
            stt(g2, g2, 1.0, g1, ALU.add, ALU.mult)
            ts(gf, gf, 0.0, None, ALU.min)
            stt(gf, g2, -2.0, gf, ALU.mult, ALU.add)
            one_b = ones[0:HEADS, 0:1].to_broadcast([HEADS, T])
            step(dve.tensor_tensor_scan(g1, one_b, gf, 0.0, ALU.mult, ALU.add))
            tt(go, gi, g1, ALU.subtract)
            step(dve.tensor_tensor_scan(g2, one_b, go, 0.0, ALU.mult, ALU.max))
            ts(gm, g2, -1.0, None, ALU.mult)
            dve.tensor_tensor(gi, g1, g2, ALU.add).then_inc(ge_sem, 1)
            for k in range(2):
                next_lo(U_GA // 2 - 1, k)

            with dve.Fori(0, SC) as c:
                one, count = stepper(s5_step, S5_STEPS * c)
                dve.wait_ge(chunk_done, c + 1)
                for k in range(4):
                    m = U_GA // 2 + 4 * c + k
                    next_lo(m, 0)
                    dve.wait_ge(out_i_done, 4 * c + k - 1 if k else 4 * c)
                    tc_, ts_ = tab[:, k % 2, 0, :], tab[:, k % 2, 1, :]
                    one(dve.memset(tc_[:, 0:1], 1.0), wait=False)
                    one(dve.memset(ts_[:, 0:1], 0.0))
                    for lv in range(9):
                        w = 1 << lv
                        pcos, psin = pc[:, 0, lv, k:k + 1], pc[:, 1, lv, k:k + 1]
                        one(dve.tensor_scalar(dtmp[:, 0, 0:w], ts_[:, 0:w], psin, None, ALU.mult), wait=False)
                        one(dve.tensor_scalar(dtmp[:, 1, 0:w], ts_[:, 0:w], pcos, None, ALU.mult))
                        one(dve.scalar_tensor_tensor(tc_[:, w:2 * w], tc_[:, 0:w], pcos, dtmp[:, 0, 0:w],
                                                     ALU.mult, ALU.subtract), wait=False)
                        ins = dve.scalar_tensor_tensor(ts_[:, w:2 * w], tc_[:, 0:w], psin, dtmp[:, 1, 0:w],
                                                       ALU.mult, ALU.add)
                        if lv < 8:
                            one(ins)
                        else:
                            ins.then_inc(tab_done, 1)
                    dve.wait_ge(tab_done, 4 * c + k + 1)
                    dve.wait_ge(bus_done, 8 * c + 2 * k + 2)
                    one(dve.tensor_tensor(dtmp[:, 0, :], bus[:, 0, :], tc_, ALU.mult), wait=False)
                    one(dve.tensor_tensor(dtmp[:, 1, :], bus[:, 1, :], ts_, ALU.mult))
                    dve.tensor_tensor(rin[:, 0, :], dtmp[:, 0, :], dtmp[:, 1, :], ALU.add).then_inc(rot_done, 1)
                    dve.wait_ge(rot_done, 4 * c + k + 1)
                    dve.wait_ge(out_i_done, 4 * c + k)
                    rb = rc[:, k:k + 1].to_broadcast([P, T])
                    dve.tensor_tensor_scan(wst[:, 0, :], rb, rin[:, 0, :], 0.0, ALU.mult, ALU.add).then_inc(scan_done, 1)
                    dve.wait_ge(prot_done, 4 * c + k + 1)
                    dve.tensor_tensor_scan(wst[:, 1, :], rb, rin[:, 1, :], 0.0, ALU.mult, ALU.add).then_inc(scan_done, 1)
                    next_lo(m, 1)
                    dve.wait_ge(scan_done, 8 * c + 2 * k + 2)
                    one(dve.tensor_tensor(dtmp[:, 0, :], wst[:, 0, :], tc_, ALU.mult), wait=False)
                    one(dve.tensor_tensor(dtmp[:, 1, :], wst[:, 1, :], ts_, ALU.mult))
                    dve.wait_ge(cm_done, 4 * c + k)
                    dve.tensor_tensor(rout[:, 0, :], dtmp[:, 0, :], dtmp[:, 1, :], ALU.subtract).then_inc(out_r_done, 1)
                dve.wait_ge(out_r_done, 4 * c + 4)
                dve.wait_ge(cm_done, 4 * c + 4)
                dve.scalar_tensor_tensor(dtmp[:, 0, :], uc[:], rc[:, 4:5], dn[:], ALU.mult, ALU.add).then_inc(yp_done, 1)
                dve.wait_ge(yhi_done, c + 1)
                dve.tensor_tensor(y_lo[:, c, :], dtmp[:, 0, :], y_hi[:, c, :].bitcast(F32), ALU.subtract)\
                    .then_inc(ylo_done, 1)
                assert count[0] == S5_STEPS, count

            with dve.Fori(0, 4) as q:
                for k in range(2):
                    next_lo(U_GLU // 2 + q, k)
                    for b in range(2):
                        f = 4 * q + 2 * k + b
                        dve.wait_ge(sg_done, f + 1)
                        dve.wait_ge(ya_out[b], 16 * (2 * q + k))
                        dve.tensor_tensor(vt[:, b, :], mm[0][:], sgt[:, b, :], ALU.mult).then_inc(proj_free, 2)

            for b in range(2):
                dve.wait_ge(ya_out[b], 16 * 8)
            with dve.Fori(0, HEADS) as h:
                one, count = stepper(ml_step, ML_STEPS * h)
                split_lo(U_QKV // 2 + h, 1)
                dve.wait_ge(xm_in, 16 * h + 16)

                def conv(c):
                    dve.wait_ge(silu_done, 3 * h + 1 if c == 2 else 3 * h)
                    o, i = cv[:, c % 2, :], xmr[:, c, :]
                    tap = [cols(V_CW + MC * j, MC)[:, 3 * h + c, :] for j in range(4)]
                    one(dve.tensor_scalar(o, i, tap[3], cols(V_CB, MC)[:, 3 * h + c, :], ALU.mult, ALU.add))
                    for lag in (1, 2, 3):
                        ins = dve.scalar_tensor_tensor(o[:, lag:T], i[:, 0:T - lag], tap[3 - lag], o[:, lag:T],
                                                       ALU.mult, ALU.add)
                        if lag < 3:
                            one(ins)
                        else:
                            ins.then_inc(cv_done, 1)

                def conv_lo(c):
                    dve.wait_ge(xchi_done, 3 * h + c + 1)
                    dve.tensor_tensor(xc_lo[:, 3 * h + c, :], xcf[:, c % 2, :],
                                      xc_hi[:, 3 * h + c, :].bitcast(F32), ALU.subtract).then_inc(xclo_done, 1)

                conv(0)
                conv(1)
                conv_lo(0)
                conv(2)
                conv_lo(1)
                conv_lo(2)
                for j in range(10):
                    dve.wait_ge(qkv_hi_done, 10 * h + j + 1)
                    src = mm[j % 2]
                    if j < 3:
                        dve.tensor_tensor(q_lo[:, j, :], src[:], q_hi[:, j, :].bitcast(F32), ALU.subtract)\
                            .then_inc(proj_free, 1)
                    elif j < 6:
                        dve.scalar_tensor_tensor(k_lo[:, j - 3, :], src[:], HD ** -0.5,
                                                 k_hi[:, j - 3, :].bitcast(F32), ALU.mult, ALU.subtract)\
                            .then_inc(proj_free, 1)
                    else:
                        dve.tensor_tensor(v_lo[:, j - 6, :], src[:, 0:HD], v_hi[:, j - 6, :].bitcast(F32),
                                          ALU.subtract).then_inc(proj_free, 1)
                split_lo(U_QKV // 2 + h + 1, 0)

                def exponent(s):
                    dve.tensor_scalar(ex[:, s % 2, 0:T - P * s], m_bc[:, P * s:T], gcol[:, s:s + 1], 0.0,
                                      ALU.add, ALU.min).then_inc(en_done, 1)

                dve.wait_ge(bcst_in, 48 * h + 48)
                exponent(0)
                for s in range(TB):
                    w = T - P * s
                    if s + 1 < TB:
                        exponent(s + 1)
                    dve.wait_ge(ex_done, 4 * h + s + 1)
                    one(dve.tensor_tensor(ex[:, s % 2, 0:P], ex[:, s % 2, 0:P], tri[:], ALU.mult))
                    dve.wait_ge(s_done, 4 * h + s + 1)
                    dve.tensor_tensor(pf[:, s % 2, 0:w], sb_[s % 2][:, 0:w], ex[:, s % 2, 0:w], ALU.mult)\
                        .then_inc(pf_done, 1)
                    dve.wait_ge(phi_done, 4 * h + s + 1)
                    dve.tensor_tensor(p_lo[:, s, P * s:T], pf[:, s % 2, 0:w], p_hi[:, s, P * s:T].bitcast(F32),
                                      ALU.subtract).then_inc(plo_done, 1)
                dve.wait_ge(den_done, h + 1)
                one(dve.scalar_tensor_tensor(rd[:], dn[:], -1.0, em_bc[:], ALU.mult, ALU.max))
                one(dve.tensor_tensor(rd[:], dn[:], rd[:], ALU.max))
                one(dve.reciprocal(rd[:], rd[:]))
                for c in range(HC):
                    dve.wait_ge(pv_done, 3 * h + c + 1)
                    dve.tensor_tensor(hh[:, c, :], pv[c % 2][:], rd[:], ALU.mult).then_inc(pv_free, 1)
                dve.wait_ge(mu_done, h + 1)
                for c in range(HC):
                    dve.scalar_tensor_tensor(hh[:, c, :], st[:], -1.0 / HD, hh[:, c, :], ALU.mult, ALU.add)\
                        .then_inc(hc_done, 1)
                dve.wait_ge(var_done, h + 1)
                dve.tensor_scalar(cv[:, 0, :], dn[:], 1.0 / HD, EPS, ALU.mult, ALU.add).then_inc(msd_done, 1)
                dve.wait_ge(std_done, h + 1)
                one(dve.reciprocal(rs[:], rs[:]))
                newton(one, rs[:], cv[:, 0, :], cv[:, 1, :])
                for c in range(HC):
                    one(dve.tensor_tensor(hh[:, c, :], hh[:, c, :], rs[:], ALU.mult), wait=False)
                    dve.wait_ge(xs_done, 3 * h + c + 1)
                    one(dve.tensor_scalar(xcf[:, c % 2, :], xcf[:, c % 2, :], cols(V_SKIP, MC)[:, 3 * h + c, :], None,
                                          ALU.mult))
                    dve.scalar_tensor_tensor(hh[:, c, :], hh[:, c, :], cols(V_GAIN, MC)[:, 3 * h + c, :],
                                             xcf[:, c % 2, :], ALU.mult, ALU.add).then_inc(hf_done, 1)
                for c in range(HC):
                    dve.wait_ge(hfhi_done, 3 * h + c + 1)
                    dve.tensor_tensor(xc_lo[:, 3 * h + c, :], hh[:, c, :], xc_hi[:, 3 * h + c, :].bitcast(F32),
                                      ALU.subtract).then_inc(hflo_done, 1)
                assert count[0] == ML_STEPS, count

            with dve.Fori(0, KC // 2) as p:
                for k in range(2):
                    next_lo(U_YB // 2 + p, k)
                    dve.wait_ge(yl_in[k], 32 * p + 32)
                    dve.wait_ge(proj_done, O_YB + 2 * p + k + 1)
                    dve.tensor_tensor(mt[:, k, :], mm[k][:], sbl[:, k, :], ALU.mult).then_inc(proj_free, 1)
                    dve.wait_ge(proj_free, O_YB + 2 * p + k + 1)
                    dve.tensor_tensor(mt[:, k, :], mt[:, k, :], yal[:, k, :], ALU.add).then_inc(mt_done, 1)
                    dve.wait_ge(mghi_done, 2 * p + k + 1)
                    dve.tensor_tensor(mg_lo[:, 2 * p + k, :], mt[:, k, :], mg_hi[:, 2 * p + k, :].bitcast(F32),
                                      ALU.subtract).then_inc(mglo_done, 1)
            with dve.Fori(0, KC // 2) as p:
                for k in range(2):
                    next_lo(U_WO // 2 + p, k)
                    dve.wait_ge(xr_in[k], 16 * p + 16)
                    dve.wait_ge(proj_done, O_WO + 2 * p + k + 1)
                    dve.tensor_tensor(h2[:, 2 * p + k, :], mm[k][:], xres[:, k, :], ALU.add).then_inc(proj_free, 1)

            norm_scale(1)

            def tn(d, k):
                dve.wait_ge(alo_done, KC + d - 1)
                dve.scalar_tensor_tensor(xt[:, k, :], h2[:, d, :], cols(V_G2, KC)[:, d, :], rs[:],
                                         ALU.mult, ALU.mult).then_inc(xn_done, 1)

            def tlo(d, k):
                dve.wait_ge(ahi_done, KC + d + 1)
                dve.tensor_tensor(t_lo[:, d, :], xt[:, k, :], t_hi[:, d, :].bitcast(F32), ALU.subtract)\
                    .then_inc(alo_done, 1)

            tn(0, 0)
            with dve.Fori(0, KC // 2 - 1) as p:
                for k in range(2):
                    tn(2 * p + k + 1, (k + 1) % 2)
                    tlo(2 * p + k, k)
            tn(KC - 1, 1)
            tlo(KC - 2, 0)
            tlo(KC - 1, 1)
            dve.wait_ge(khi_done, 1)
            dve.tensor_tensor(key_lo[:], key_raw[:], key_hi[:].bitcast(F32), ALU.subtract).then_inc(klo_done, 1)

            def top16(one, vals, vo_, io_):
                width = vals.shape[-1]
                one(dve.max(vo_[:, 0:8], vals), apart=True)
                one(dve.max_index(io_[:, 0:8], vo_[:, 0:8], vals), wait=False)
                one(dve.match_replace(tw[:, 0:width], vo_[:, 0:8], vals, NEG_BIG), apart=True)
                one(dve.max(vo_[:, 8:16], tw[:, 0:width]), apart=True)
                one(dve.max_index(io_[:, 8:16], vo_[:, 8:16], tw[:, 0:width]), apart=True)

            with dve.Fori(0, PH) as hd:
                one, count = stepper(pk_step, PK_STEPS * hd)
                for k in range(2):
                    dve.wait_ge(qhi_done, 2 * hd + k + 1)
                    dve.tensor_tensor(qq_lo[:, k, :], mm[k][:], qq_hi[:, k, :].bitcast(F32), ALU.subtract)\
                        .then_inc(proj_free, 1)
                for k in range(2):
                    dve.wait_ge(sco_done, 2 * hd + k + 1)
                    carrier()
                    for tb in range(TB):
                        top16(one, sb_[k][:, tb * NKEY:(tb + 1) * NKEY], v12[:, k, tb, :], i12u[:, k, tb, :])
                    dve.tensor_copy(i12[:, k, :, :], i12u[:, k, :, :]).then_inc(sco_free, 1)
                one(dve.tensor_tensor(cand[:], v12[:, 0, :, :].unsqueeze(3).to_broadcast([P, TB, TOPK, TOPK]),
                                      v12[:, 1, :, :].unsqueeze(2).to_broadcast([P, TB, TOPK, TOPK]), ALU.add),
                    apart=True)
                for tb in range(TB):
                    top16(one, cand[:, tb, :, :].rearrange("p a b -> p (a b)"), tv[:, tb, :], pos[:, tb, :])
                dve.tensor_tensor(ge[:], tv[:], tv[:, :, 0:1].to_broadcast([P, TB, TOPK]), ALU.subtract)\
                    .then_inc(gsub_done, 1)
                one(dve.tensor_scalar(ab_u[:, 0, :, :], pos[:], 4, None, ALU.logical_shift_right), wait=False)
                one(dve.tensor_scalar(ab_u[:, 1, :, :], pos[:], 15, None, ALU.bitwise_and))
                one(dve.tensor_copy(ab[:], ab_u[:]))
                for r in range(2):
                    dve.wait_ge(sco_free, 2 * hd + 2)
                    dve.tensor_tensor(eqs[r], iota[:, 0:TOPK].unsqueeze(1).to_broadcast([P, TB * TOPK, TOPK]),
                                      ab[:, r, :, :].rearrange("p b k -> p (b k)").unsqueeze(2)
                                      .to_broadcast([P, TB * TOPK, TOPK]), ALU.is_equal).then_inc(eq_done, 1)
                dve.wait_ge(gexp_done, hd + 1)
                one(dve.tensor_reduce(gz[:, 0, :], ge[:], AX_X, ALU.add))
                one(dve.reciprocal(gz[:, 1, :], gz[:, 0, :]))
                one(dve.tensor_tensor(slot[:, 0, :, hd, :], ge[:], gz[:, 1, :].unsqueeze(2)
                                      .to_broadcast([P, TB, TOPK]), ALU.mult), wait=False)
                for r in range(2):
                    dve.wait_ge(eqm_done, 2 * hd + r + 1)
                    dve.tensor_reduce(slot[:, 1 + r, :, hd, :], eqs[r].rearrange("p (b k) a -> p b k a", b=TB),
                                      AX_X, ALU.add).then_inc(slot_done, 1)
                assert count[0] == PK_STEPS, count

            dve.wait_ge(trc_done, 3)
            it, jt, gt_ = (slot_t[:, v, :].rearrange("p (t o) -> p t o", o=1) for v in (1, 2, 0))
            with dve.Fori(0, 16) as rs_i:
                with dve.Fori(0, 2) as q:
                    for b, hot in enumerate((hot_a, hot_b)):
                        t0 = 32 * rs_i + 16 * q + 8 * b
                        for w in range(8):
                            dve.wait_ge(hot_used, t0 + w + 1)
                            dve.tensor_scalar(hot[:, w, 0, :], iota[:], it[:, t0 + w, :], gt_[:, t0 + w, :],
                                              ALU.is_equal, ALU.mult).then_inc(hot_done, 1)
                            dve.tensor_scalar(hot[:, w, 1, :], iota[:], jt[:, t0 + w, :], None,
                                              ALU.is_equal).then_inc(hot_done, 1)

            def gated(par, jj, num, slot_af):
                dve.wait_ge(proj_free, O_EXP + num + 1)
                dve.tensor_tensor(af[:, slot_af, :].rearrange("p (n t) -> p n t", n=16),
                                  gl[:, slot_af, :].rearrange("p (n t) -> p n t", n=16),
                                  gg[:, par, :, :].rearrange("p n (j t) -> p n j t", j=4)[:, :, jj, :],
                                  ALU.mult).then_inc(af_done, 1)

            def act_low(par, jj, num, slot_af):
                dve.wait_ge(acthi_done, num + 1)
                dve.tensor_tensor(act_lo[:, par, jj, :], af[:, slot_af, :], act_hi[:, par, jj, :].bitcast(F32),
                                  ALU.subtract).then_inc(actlo_done, 1)

            def add_down(g, jj):
                for b in range(4):
                    dve.wait_ge(v_done, 16 * g + 4 * jj + b + 1)
                    dve.tensor_tensor(h2[:, 4 * jj + b, :], h2[:, 4 * jj + b, :], vo[b][:], ALU.add)\
                        .then_inc(v_free, 1)

            dve.wait_ge(g_in, 16)
            for jj in range(4):
                next_lo((U_EXP + jj) // 2, jj % 2)
                gated(0, jj, jj, jj % 2)
                act_low(0, jj, jj, jj % 2)
            with dve.Fori(0, GROUPS_E - 1) as g:
                dve.wait_ge(g_in, 16 * g + 32)
                for jj in range(4):
                    m = (U_EXP + 4) // 2 + 4 * g + jj
                    split_lo(m, 1)
                    gated((g + 1) % 2, jj, 4 * g + 4 + jj, jj % 2)
                    split_lo(m + 1, 0)
                    act_low((g + 1) % 2, jj, 4 * g + 4 + jj, jj % 2)
                    add_down(g, jj)
            for jj in range(4):
                nu = U_EXP + 4 + 8 * (GROUPS_E - 1) + jj + 1
                if jj < 3:
                    split_lo(nu // 2, nu % 2)
                add_down(GROUPS_E - 1, jj)

            dve.wait_ge(v_free, 16 * GROUPS_E)
            norm_scale(2)
            with dve.Fori(0, KC // 2) as p:
                for b in range(2):
                    dve.wait_ge(fin_out[b], 16 * p)
                    dve.scalar_tensor_tensor(fin[:, b, :], h2[:, 2 * p + b, :], cols(V_GF, KC)[:, 2 * p + b, :],
                                             rs[:], ALU.mult, ALU.mult).then_inc(fin_done, 1)

        @block.tensor
        def _(pe):
            def mm3(out, lh, ll, rh, rl, start, stop):
                pe.matmul(out, lh, rh, start=start, stop=False)
                pe.matmul(out, lh, rl, start=False, stop=False)
                return pe.matmul(out, ll, rh, start=False, stop=stop)

            def w(k, c0, width=P):
                return whi[:, k, c0:c0 + width], wlo[:, k, c0:c0 + width]

            def proj(m, k, o, rh, rl, kc=KC, b=None, c0=0, wait=True):
                if wait:
                    pe.wait_ge(lo_done, 2 * m + k + 1)
                pe.wait_ge(proj_free, o - 1)
                out = mm[k if b is None else b][:]
                for d in range(kc):
                    last = mm3(out, *w(k, c0 + P * d), rh[:, d, :], rl[:, d, :], d == 0, d == kc - 1)
                last.then_inc(proj_done, 1)

            def sum_squares(r):
                for d in range(KC):
                    pe.wait_ge(sq_done, KC * r + d + 1)
                    pe.matmul(st[:], ones[:], sq[:, d % 2, :], start=(d == 0), stop=(d == KC - 1))\
                        .then_inc(ssq_done, 1)

            pe.wait_ge(const_done, 4)
            sum_squares(0)
            pe.wait_ge(lo_done, 1)
            for d in range(KC):
                pe.wait_ge(alo_done, d + 1)
                last = mm3(mm[0][:], *w(0, P * d), hn_hi[:, d, :], hn_lo[:, d, :], d == 0, d == KC - 1)
            last.then_inc(proj_done, 1)
            pe.wait_ge(lo_done, 2)
            for d in range(KC):
                last = mm3(mm[1][:], *w(1, P * d), hn_hi[:, d, :], hn_lo[:, d, :], d == 0, d == KC - 1)
            last.then_inc(proj_done, 1)
            for nu in (2, 3):
                proj(nu // 2, nu % 2, nu, hn_hi, hn_lo)
            pe.wait_ge(wif_in, 16)
            for d in range(KC):
                last = pe.matmul(pv[0][0:64, :], wif[:, d, :], x[:, d, :], start=(d == 0), stop=(d == KC - 1))
            last.then_inc(if_done, 1)
            with pe.Fori(U_XM // 2, U_GA // 2) as m:
                for k in range(2):
                    proj(m, k, 2 * m + k, hn_hi, hn_lo)

            def s5_out(c, k):
                pe.wait_ge(out_r_done, 4 * c + k + 1)
                pe.matmul(dn[32 * k:32 * k + 32, :], cc[:, 0, k, :], rout[:, 0, :], start=True, stop=False)
                pe.wait_ge(out_i_done, 4 * c + k + 1)
                pe.matmul(dn[32 * k:32 * k + 32, :], cc[:, 1, k, :], rout[:, 1, :], start=False, stop=True)\
                    .then_inc(cm_done, 1)

            with pe.Fori(0, SC) as c:
                for k in range(4):
                    m = U_GA // 2 + 4 * c + k
                    proj(m, 0, 2 * m, hn_hi, hn_lo)
                    if k:
                        s5_out(c, k - 1)
                    else:
                        pe.wait_ge(chunk_done, c + 1)
                        pe.wait_ge(bc_in, 16 * c + 16)
                        pe.wait_ge(ylo_done, c)
                    rows = slice(32 * k, 32 * k + 32)
                    pe.wait_ge(bus_done, 8 * c + 2 * k)
                    for r in range(2):
                        pe.matmul(sb_[r][:], bc[rows, r, :], uc[rows, :], start=True, stop=True).then_inc(bu_done, 1)
                    proj(m, 1, 2 * m + 1, hn_hi, hn_lo)
                s5_out(c, 3)

            pe.wait_ge(ylo_done, SC)
            with pe.Fori(0, 4) as q:
                for k in range(2):
                    for j in range(4):
                        proj(U_GLU // 2 + q, k, O_GLU + 8 * q + 4 * k + j, y_hi, y_lo, SC, j % 2, 512 * j, j == 0)

            pe.wait_ge(onesr_done, 1)
            with pe.Fori(0, HEADS) as h:
                ma = U_QKV // 2 + h
                o = O_QKV + 10 * h
                pe.wait_ge(xclo_done, 3 * h + 3)
                for part, k in enumerate((0, 1)):
                    pe.wait_ge(lo_done, 2 * ma + k + 1)
                    for ob in range(HC):
                        j = 3 * part + ob
                        pe.wait_ge(proj_free, o + j - 1)
                        for d in range(HC):
                            last = mm3(mm[j % 2][:], *w(k, HD * d + P * ob), xc_hi[:, 3 * h + d, :],
                                       xc_lo[:, 3 * h + d, :], d == 0, d == HC - 1)
                        last.then_inc(proj_done, 1)
                pe.wait_ge(xmlo_done, 3 * h + 3)
                for s in range(TB):
                    j = 6 + s
                    pe.wait_ge(proj_free, o + j - 1)
                    for d in range(HC):
                        vh, vl = w(0, 3 * HD, HD) if d == 0 else w(1, (2 + d) * HD, HD)
                        ts_ = slice(P * s, P * s + P)
                        last = mm3(mm[j % 2][:, 0:HD], xm_hi[:, d, ts_], xm_lo[:, d, ts_], vh, vl, d == 0, d == HC - 1)
                    last.then_inc(proj_done, 1)

                def scores(s):
                    pe.wait_ge(pf_done, 4 * h + s - 1 if s >= 2 else 4 * h)
                    ks = slice(P * s, P * s + P)
                    for d in range(HC):
                        last = mm3(sb_[s % 2][:, 0:T - P * s], k_hi[:, d, ks], k_lo[:, d, ks],
                                   q_hi[:, d, P * s:T], q_lo[:, d, P * s:T], d == 0, d == HC - 1)
                    last.then_inc(s_done, 1)

                def den(s):
                    pe.wait_ge(plo_done, 4 * h + s + 1)
                    pe.matmul(dn[:, P * s:T], ones_r[:], p_hi[:, s, P * s:T], start=(s == 0), stop=False)
                    return pe.matmul(dn[:, P * s:T], ones_r[:], p_lo[:, s, P * s:T], start=False, stop=(s == TB - 1))

                pe.wait_ge(proj_free, o + 6)
                pe.wait_ge(msd_done, h)
                scores(0)
                scores(1)
                den(0)
                scores(2)
                den(1)
                scores(3)
                den(2)
                den(3).then_inc(den_done, 1)
                pe.wait_ge(proj_free, o + 10)
                for c in range(HC):
                    pe.wait_ge(pv_free, 3 * h + 1 if c == 2 else 3 * h)
                    cs = slice(P * c, P * c + P)
                    for s in range(TB):
                        last = mm3(pv[c % 2][:, P * s:T], v_hi[:, s, cs], v_lo[:, s, cs],
                                   p_hi[:, s, P * s:T], p_lo[:, s, P * s:T], s == 0, s == TB - 1)
                    last.then_inc(pv_done, 1)
                pe.wait_ge(hc_done, 3 * h)
                for c in range(HC):
                    pe.wait_ge(hz_done, 3 * h + c + 1)
                    last = pe.matmul(st[:], ones[:], hh[:, c, :], start=(c == 0), stop=(c == HC - 1))
                last.then_inc(mu_done, 1)
                for c in range(HC):
                    pe.wait_ge(hsq_done, 3 * h + c + 1)
                    last = pe.matmul(dn[:], ones[:], hsq[c], start=(c == 0), stop=(c == HC - 1))
                last.then_inc(var_done, 1)

            pe.wait_ge(hflo_done, MC)
            with pe.Fori(0, KC // 2) as p:
                for k in range(2):
                    proj(U_YB // 2 + p, k, O_YB + 2 * p + k, xc_hi, xc_lo, MC)
            pe.wait_ge(mglo_done, KC)
            with pe.Fori(0, KC // 2) as p:
                for k in range(2):
                    proj(U_WO // 2 + p, k, O_WO + 2 * p + k, mg_hi, mg_lo)

            sum_squares(1)
            pe.wait_ge(alo_done, 2 * KC)
            pe.wait_ge(klo_done, 1)
            with pe.Fori(0, PH) as hd:
                for k in range(2):
                    proj(U_WQ // 2 + hd, k, O_WQ + 2 * hd + k, t_hi, t_lo)
                for k in range(2):
                    pe.wait_ge(proj_free, O_WQ + 2 * hd + k + 1)
                    pe.wait_ge(sco_free, 2 * hd)
                    for tb in range(TB):
                        ts_ = slice(P * tb, P * tb + P)
                        last = mm3(sb_[k][:, ts_], qq_hi[:, k, ts_], qq_lo[:, k, ts_],
                                   key_hi[:, hd, k, :], key_lo[:, hd, k, :], True, True)
                    last.then_inc(sco_done, 1)

            pe.wait_ge(slot_done, 2 * PH)
            pe.wait_ge(pk_step, PK_STEPS * PH)
            for v in range(3):
                for tb in range(TB):
                    last = pe.transpose((dn, pv[0], pv[1])[v][:, P * tb:P * tb + P],
                                        slot[:, v, tb, :, :].rearrange("p h k -> p (h k)"), ident[:])
                last.then_inc(tr_done, 1)
            pe.sem_inc(hot_used, 16)
            with pe.Fori(0, 16) as rs_i:
                with pe.Fori(0, 2) as q:
                    for b, hot in enumerate((hot_a, hot_b)):
                        t0 = 32 * rs_i + 16 * q + 8 * b
                        for v in range(8):
                            pe.wait_ge(hot_done, 2 * t0 + 2 * v + 2)
                            if v % 4 == 0:
                                pe.wait_ge(gps_free, 8 * rs_i + 4 * q + 2 * b + v // 4 + 1)
                            pe.matmul(sb_[v // 4][:, P * (v % 4):P * (v % 4) + P], hot[:, v, 0, :], hot[:, v, 1, :],
                                      start=True, stop=True).then_inc(hot_used, 1)

            def down(k, g, act_par, m, v0):
                pe.wait_ge(lo_done, 2 * m + k + 1)
                pe.wait_ge(actlo_done, 4 * g + 4)
                pe.wait_ge(v_free, v0)
                for b in range(4):
                    for jj in range(4):
                        last = mm3(vo[b][:], *w(k, 512 * jj + P * b), act_hi[:, act_par, jj, :],
                                   act_lo[:, act_par, jj, :], jj == 0, jj == 3)
                    last.then_inc(v_done, 1)

            for jj in range(4):
                proj((U_EXP + jj) // 2, jj % 2, O_EXP + jj, t_hi, t_lo)
            pe.wait_ge(gps_free, 2 + 128)
            with pe.Fori(0, GROUPS_E - 1) as g:
                for jj in range(4):
                    m = (U_EXP + 4) // 2 + 4 * g + jj
                    proj(m, 0, O_EXP + 4 + 4 * g + jj, t_hi, t_lo, b=jj % 2)
                    down(1, g, g % 2, m, 16 * g + 4 * jj)
            for jj in range(4):
                nu = U_EXP + 4 + 8 * (GROUPS_E - 1) + jj
                down(nu % 2, GROUPS_E - 1, (GROUPS_E - 1) % 2, nu // 2, 16 * (GROUPS_E - 1) + 4 * jj)

            sum_squares(2)

def _blocks(w):
    din, f = w.shape
    return w.reshape(din // P, P, f // P, P).transpose(2, 1, 0, 3).reshape(f // P, P, din)


def _stream(i):
    s = np.zeros((N_STREAM, P, UNIT), np.float32)
    w_in = i["w_in"][0]
    z1 = SSM_W + 2 * ML_W
    ga = z1 + 2 * HEADS
    s[U_SSM:U_GA] = _blocks(w_in[:, 0:z1])
    s[U_GA:U_GLU] = _blocks(w_in[:, ga:])
    g = i["w_glu"][0].reshape(SC, P, 2, 8, 2, P).transpose(3, 1, 4, 2, 0, 5)
    s[U_GLU:U_QKV] = g.reshape(8, P, UNIT)
    for h in range(HEADS):
        q, k, v = (i[n][0, h].reshape(HC, P, HD).transpose(1, 0, 2) for n in ("w_q", "w_k", "w_v"))
        a, b = s[U_QKV + 2 * h], s[U_QKV + 2 * h + 1]
        a[:, 0:3 * HD], a[:, 3 * HD:4 * HD] = q.reshape(P, -1), v[:, 0]
        b[:, 0:3 * HD], b[:, 3 * HD:5 * HD] = k.reshape(P, -1), v[:, 1:3].reshape(P, -1)
    s[U_YB:U_WO, :, 0:ML_W] = _blocks(i["w_mlstm_out"][0])
    s[U_WO:U_WQ] = _blocks(i["w_out"][0])
    s[U_WQ:U_EXP] = _blocks(i["w_query"][0])
    up = i["expert_u"][0].reshape(P, P, KC, P).transpose(1, 3, 2, 0).reshape(P, P, UNIT)
    down = i["expert_v"][0].reshape(P, GROUPS_E, 4, 4, 512).transpose(1, 3, 0, 2, 4).reshape(4 * GROUPS_E, P, UNIT)
    s[U_EXP:U_EXP + 4] = up[0:4]
    s[U_EXP + 4:N_STREAM - 4:2] = up[4:]
    s[U_EXP + 5:N_STREAM - 4:2] = down[:-4]
    s[N_STREAM - 4:] = down[-4:]
    return s


def _vectors(i):
    v = np.zeros((P, N_VEC), np.float32)

    def put(at, x):
        x = x.reshape(-1, P).T
        v[:, at:at + x.shape[1]] = x

    put(V_G1, i["norm1_g"][0])
    put(V_G2, i["norm2_g"][0])
    put(V_GF, i["norm_f_g"])
    put(V_DSKIP, i["d_skip"][0])
    put(V_CW, i["conv_w"][0])
    put(V_CB, i["conv_b"][0])
    put(V_GAIN, i["mh_gain"][0])
    put(V_SKIP, i["mlstm_skip"][0])
    put(V_LRE, i["lam_re"][0])
    put(V_LIM, i["lam_im"][0])
    put(V_LDT, np.repeat(i["log_dt"][0], STATE))
    v[0:HEADS, V_BI] = i["b_i"][0]
    v[32:32 + HEADS, V_BF] = i["b_f"][0]
    return v


def _s5_tables(i):
    b_tab = np.zeros((SC + 1, P, 2, P), np.float32)
    c_tab = np.zeros((P, 2, 16, 32), np.float32)
    for g in range(GROUPS):
        c, k, half = g // 8, g // 2 % 4, g % 2
        ch, st = 32 * k + GROUP * half, STATE * half
        for r, (b, cm) in enumerate((("b_re", "c_re"), ("b_im", "c_im"))):
            b_tab[c, ch:ch + GROUP, r, st:st + STATE] = i[b][0, g].T
            c_tab[st:st + STATE, r, g // 2, GROUP * half:GROUP * half + GROUP] = i[cm][0, g].T
    return b_tab, c_tab


def kernel(**inputs):
    import concourse.bacc as _bacc
    from concourse.bass_utils import run_bass_kernel_spmd as _run

    i = {k: np.asarray(v) for k, v in inputs.items()}
    w_in = i["w_in"][0]
    z1 = SSM_W + 2 * ML_W
    wif = np.zeros((P, KC, 64), np.float32)
    wif[:, :, 0:HEADS] = w_in[:, z1:z1 + HEADS].reshape(KC, P, HEADS).transpose(1, 0, 2)
    wif[:, :, 32:32 + HEADS] = w_in[:, z1 + HEADS:z1 + 2 * HEADS].reshape(KC, P, HEADS).transpose(1, 0, 2)
    b_tab, c_tab = _s5_tables(i)
    keys = np.stack([i["key1"][0], i["key2"][0]], 1)
    arrays = {
        "xT": np.ascontiguousarray(i["x"][0].reshape(T, KC, P).transpose(2, 1, 0)),
        "stream": _stream(i), "vecs": _vectors(i), "wif": wif, "b_tab": b_tab, "c_tab": c_tab,
        "keys": np.ascontiguousarray(keys.transpose(3, 0, 1, 2)),
    }
    nc = _bacc.Bacc("TRN2", target_bir_lowering=False, num_devices=1)
    args = {n: nc.dram_tensor(n, v.shape, F32, kind="ExternalInput").ap() for n, v in arrays.items()}
    out = nc.dram_tensor("out", (P, KC, T), F32, kind="ExternalOutput").ap()
    build(nc, args, out)
    r = _run(nc, [arrays], core_ids=[0])
    y = r.results[0]["out"]
    return np.ascontiguousarray(y.transpose(2, 1, 0)).reshape(1, T, D)
```

```python
from contextlib import ExitStack

import numpy as np

import concourse.bass as bass
from concourse import mybir

ALU = mybir.AluOpType
ACT = mybir.ActivationFunctionType
AX_X = mybir.AxisListType.X
F32 = mybir.dt.float32
F32R = mybir.dt.float32r
I32 = mybir.dt.int32
U32 = mybir.dt.uint32

P = 128
T = 512
D = 2048
KC = D // P
SSM_W, ML_W, HEADS, HD = 512, 1536, 4, 384
SC, MC, HC = SSM_W // P, ML_W // P, HD // P
TB = T // P
STATE, GROUP, GROUPS = 64, 16, 32
PH, NKEY, TOPK = 8, 128, 16
EPS = 1e-6
UNIT = 2048

U_SSM, U_XM, U_Z, U_GA, U_GB = 0, 4, 16, 28, 44
U_GLU, U_QKV, U_YB, U_WO = 60, 68, 76, 92
U_HEAD = 108
U_FILL = U_HEAD + 6 * PH
U_GATE = U_FILL + 4
U_LAST = U_GATE + 32
U_DOWN = U_LAST + 4
GROUPS_E = 32
N_FILL, N_GATE, N_LAST = 4 * PH, 4 * PH + 4, 4 * PH + 36
EARLY = (N_LAST + 4) // 4
U_PAIR = U_DOWN + 4 * (EARLY - 1)
N_STREAM = U_PAIR + 8 * (GROUPS_E - EARLY) + 4
O_GLU, O_QKV, O_YB, O_WO, O_UP = 60, 92, 132, 148, 164

V_G1, V_G2, V_GF, V_DSKIP, V_CW, V_CB, V_GAIN, V_SKIP = 0, 16, 32, 48, 52, 100, 112, 124
V_LRE, V_LIM, V_LDT, V_BI, V_BF, N_VEC = 136, 152, 168, 184, 185, 186

LOG2E, LN2_HI, LN2_LO = 1.4426950408889634, 0.693359375, -2.12194440e-4
ROUND = 12582912.0
HALF_PI = (1.5703125, 4.837512969970703125e-4, 7.54978995489188216e-8)
NEG_BIG = -3.0e38
S5_STEPS, ML_STEPS, PK_STEPS, PICK_STEPS = 164, 27, 67, 64


def build(nc, a, out_d):
    ctx = ExitStack()
    with ctx:
        base = (nc.sbuf_base + 63) // 64 * 64
        room = nc.sbuf_usable_end - base

        def S(name, shape, dt, kb):
            size = 4 * int(np.prod(shape[1:]))
            assert kb * 1024 + size <= room, (name, kb * 1024 + size, room)
            return nc.alloc_sbuf_tensor_at(name, shape, dt, offset=base + int(kb * 1024))

        def sem(name):
            return ctx.enter_context(nc.semaphore(name))

        raw = S("raw", [P, 2, UNIT], F32, 0)
        whi = S("whi", [P, 2, UNIT], F32R, 16)
        wlo = S("wlo", [P, 2, UNIT], F32R, 32)
        vec = S("vec", [P, N_VEC], F32, 202)
        ones = S("ones", [P, P], F32, 202.75)
        ones_r = S("ones_r", [P, P], F32R, 203.25)
        ident = S("ident", [P, P], F32, 203.75)
        tri = S("tri", [P, P], F32, 204.25)
        iota = S("iota", [P, P], F32, 204.75)
        rs = S("rs", [P, T], F32, 205.25)
        sq = S("sq", [P, 2, T], F32, 176)
        ms = S("ms", [P, T], F32, 180)
        nt = S("nt", [P, T], F32, 182)
        xt = S("xt", [P, 2, T], F32, 184)
        hn_hi = S("hn_hi", [P, KC, T], F32R, 48)
        hn_lo = S("hn_lo", [P, KC, T], F32R, 80)
        x = S("x", [P, KC, T], F32, 112)
        uT = S("uT", [P, SC, T], F32, 144)
        stage = S("stage", [P, 2, T], F32, 152)
        cp = S("cp", [P, 2, 16, 32], F32, 156)
        craw = S("craw", [P, 2, 16, 32], F32, 160)
        wif = S("wif", [P, KC, 64], F32, 164)
        bc = S("bc", [P, 2, P], F32, 168)
        cc = S("cc", [P, 2, 4, 32], F32, 169)
        pc = S("pc", [P, 2, 9, 4], F32, 170)
        rc = S("rc", [P, 8], F32, 170.5)
        cw = S("cw", [P, 40, 16], F32, 171)
        ptab = S("ptab", [P, 2, 9, 16], F32, 174)
        gt = S("gt", [P, 4, T], F32, 184)
        gout = S("gout", [P, 3, T], F32, 192)
        tab = S("tab", [P, 2, 2, T], F32, 112)
        bus = S("bus", [P, 2, T], F32, 120)
        rin = S("rin", [P, 2, T], F32, 124)
        wst = S("wst", [P, 2, T], F32, 128)
        rout = S("rout", [P, 2, T], F32, 132)
        dtmp = S("dtmp", [P, 2, T], F32, 136)
        ptmp = S("ptmp", [P, 2, T], F32, 140)
        uc = S("uc", [P, T], F32, 198)
        y_hi = S("y_hi", [P, SC, T], F32R, 176)
        y_lo = S("y_lo", [P, SC, T], F32R, 184)
        sgt = S("sgt", [P, 2, T], F32, 112)
        vt = S("vt", [P, 2, T], F32, 116)
        sa = S("sa", [P, 2, T], F32, 132)
        xc_hi = S("xc_hi", [P, MC, T], F32R, 48)
        xc_lo = S("xc_lo", [P, MC, T], F32R, 72)
        q_hi = S("q_hi", [P, HC, T], F32R, 96)
        q_lo = S("q_lo", [P, HC, T], F32R, 102)
        k_hi = S("k_hi", [P, HC, T], F32R, 108)
        k_lo = S("k_lo", [P, HC, T], F32R, 114)
        v_hi = S("v_hi", [P, TB, HD], F32R, 120)
        v_lo = S("v_lo", [P, TB, HD], F32R, 126)
        p_hi = S("p_hi", [P, TB, T], F32R, 132)
        p_lo = S("p_lo", [P, TB, T], F32R, 140)
        m_bc = S("m_bc", [P, T], F32, 148)
        em_bc = S("em_bc", [P, T], F32, 150)
        xmr = S("xmr", [P, HC, T], F32, 152)
        sz = S("sz", [P, HC, T], F32, 158)
        cv = S("cv", [P, 2, T], F32, 164)
        xcf = S("xcf", [P, 2, T], F32, 168)
        pf = S("pf", [P, 2, T], F32, 172)
        xm_hi = S("xm_hi", [P, HC, T], F32R, 176)
        xm_lo = S("xm_lo", [P, HC, T], F32R, 182)
        ex = S("ex", [P, 2, T], F32, 188)
        hh = S("hh", [P, HC, T], F32, 192)
        rd = S("rd", [P, T], F32, 198)
        gcol = S("gcol", [P, TB], F32, 200)
        mg_hi = S("mg_hi", [P, KC, T], F32R, 96)
        mg_lo = S("mg_lo", [P, KC, T], F32R, 128)
        yal = S("yal", [P, 2, T], F32, 160)
        sbl = S("sbl", [P, 2, T], F32, 164)
        mt = S("mt", [P, 2, T], F32, 168)
        xres = S("xres", [P, 2, T], F32, 172)
        h2 = S("h2", [P, KC, T], F32, 48)
        t_hi = S("t_hi", [P, KC, T], F32R, 96)
        t_lo = S("t_lo", [P, KC, T], F32R, 128)
        key_hi = S("key_hi", [P, PH, 2, NKEY], F32R, 160)
        key_lo = S("key_lo", [P, PH, 2, NKEY], F32R, 168)
        key_raw = S("key_raw", [P, PH, 2, NKEY], F32, 188)
        qq_hi = S("qq_hi", [P, 2, T], F32R, 80)
        qq_lo = S("qq_lo", [P, 2, T], F32R, 84)
        tw = S("tw", [P, 256], F32, 196)
        v12 = S("v12", [P, 2, TB, TOPK], F32, 197)
        i12u = S("i12u", [P, 2, TB, TOPK], U32, 197.5)
        i12 = S("i12", [P, 2, TB, TOPK], F32, 198)
        cand = S("cand", [P, TB, TOPK, TOPK], F32, 88)
        eq = S("eq", [P, TB * TOPK, TOPK], F32, 92)
        tv = S("tv", [P, TB, TOPK], F32, 198.5)
        pos = S("pos", [P, TB, TOPK], U32, 198.75)
        ab_u = S("ab_u", [P, 2, TB, TOPK], U32, 199)
        ab = S("ab", [P, 2, TB, TOPK], F32, 199.5)
        ge = S("ge", [P, TB, TOPK], F32, 200)
        gz = S("gz", [P, 2, TB], F32, 200.25)
        slot = S("slot", [P, 3, TB, PH, TOPK], F32, 176)
        sgl = S("sgl", [P, 2, T], F32, 192)
        slot_t = S("slot_t", [P, 2, T], F32, 82)
        gate_hi = S("gate_hi", [P, T], F32R, 80)
        gate_lo = S("gate_lo", [P, T], F32, 86)
        hot_i = S("hot_i", [P, 2, 8, P], F32R, 48)
        hot_j = S("hot_j", [P, 2, 8, P], F32, 56)
        hot_jh = S("hot_jh", [P, 2, 8, P], F32R, 64)
        hot_jl = S("hot_jl", [P, 2, 8, P], F32R, 72)
        gst = S("gst", [P, 2, P, 32], F32, 160)
        gl = S("gl", [P, 2, T], F32, 196)
        gg = S("gg", [P, 2, 16, P], F32, 80)
        act_hi = S("act_hi", [P, 2, 4, T], F32R, 160)
        act_lo = S("act_lo", [P, 2, 4, T], F32R, 176)
        fin = S("fin", [P, 2, T], F32, 96)

        def bank(name):
            return ctx.enter_context(nc.psum_tensor(name, [P, T], F32))

        mm = [bank("mm0"), bank("mm1")]
        sb_ = [bank("sc0"), bank("sc1")]
        dn, st = bank("dn"), bank("st")
        pv = [bank("pv0"), bank("pv1")]
        vo = [pv[0], pv[1], sb_[0], sb_[1]]

        hsq = (ex[:, 0, :], ex[:, 1, :], pf[:, 0, :])
        eqs = (eq[:], cand[:].rearrange("p b k a -> p (b k) a"))

        spill = nc.dram_tensor("spill", (56, P, T), F32).ap()
        ya_d = nc.dram_tensor("ya_d", (KC, P, T), F32).ap()
        gates_d = nc.dram_tensor("gates_d", (3, HEADS, T), F32).ap()
        h2_d = nc.dram_tensor("h2_d", (P, KC, T), F32).ap()
        up_d = nc.dram_tensor("up_d", (4 * EARLY, P, T), F32).ap()
        g_d = nc.dram_tensor("g_d", (16, P, P, 32), F32).ap()

        raw_in = [sem("raw_in0"), sem("raw_in1")]
        hi_done, lo_done = sem("hi_done"), sem("lo_done")
        proj_done, proj_free = sem("proj_done"), sem("proj_free")
        vec_in, x_in = sem("vec_in"), [sem(f"x_in{i}") for i in range(4)]
        wif_in, craw_in = sem("wif_in"), sem("craw_in")
        const_done, onesr_done = sem("const_done"), sem("onesr_done")
        sq_done, ssq_done, rt_done, rs_done = sem("sq_done"), sem("ssq_done"), sem("rt_done"), sem("rs_done")
        xn_done, ahi_done, alo_done = sem("xn_done"), sem("ahi_done"), sem("alo_done")
        stage_out = [sem("stage_out0"), sem("stage_out1")]
        if_done, ge_sem, gates_done, gates_out = sem("if_done"), sem("ge_sem"), sem("gates_done"), sem("gates_out")
        coef_done, chunk_done, bc_in = sem("coef_done"), sem("chunk_done"), sem("bc_in")
        bu_done, bus_done, tab_done, rot_done = sem("bu_done"), sem("bus_done"), sem("tab_done"), sem("rot_done")
        prot_done, scan_done, out_r_done, out_i_done = sem("prot_done"), sem("scan_done"), sem("out_r_done"), sem("out_i_done")
        cm_done, yp_done, yg_done, yhi_done, ylo_done = sem("cm_done"), sem("yp_done"), sem("yg_done"), sem("yhi_done"), sem("ylo_done")
        sg_done, ya_done = sem("sg_done"), sem("ya_done")
        sa_in, ya_out = [sem("sa_in0"), sem("sa_in1")], [sem("ya_out0"), sem("ya_out1")]
        xm_in, sz_in, bcst_in = sem("xm_in"), sem("sz_in"), sem("bcst_in")
        cv_done, silu_done, xchi_done, xclo_done = sem("cv_done"), sem("silu_done"), sem("xchi_done"), sem("xclo_done")
        xmhi_done, xmlo_done = sem("xmhi_done"), sem("xmlo_done")
        qkv_hi_done = sem("qkv_hi_done")
        s_done, en_done, ex_done = sem("s_done"), sem("en_done"), sem("ex_done")
        pf_done, phi_done, plo_done = sem("pf_done"), sem("phi_done"), sem("plo_done")
        den_done, pv_done, pv_free, hz_done = sem("den_done"), sem("pv_done"), sem("pv_free"), sem("hz_done")
        mu_done, hc_done, hsq_done, var_done = sem("mu_done"), sem("hc_done"), sem("hsq_done"), sem("var_done")
        std_done, xs_done, hf_done, hfhi_done, hflo_done = sem("std_done"), sem("xs_done"), sem("hf_done"), sem("hfhi_done"), sem("hflo_done")
        yl_in = [sem("yl_in0"), sem("yl_in1")]
        mt_done, mghi_done, mglo_done = sem("mt_done"), sem("mghi_done"), sem("mglo_done")
        xr_in = [sem("xr_in0"), sem("xr_in1")]
        key_in, khi_done, klo_done = sem("key_in"), sem("khi_done"), sem("klo_done")
        qp_done, qhi_done, qlo_done = sem("qp_done"), sem("qhi_done"), sem("qlo_done")
        sco_done, sco_free = sem("sco_done"), sem("sco_free")
        gsub_done, gexp_done, eqm_done, slot_done = sem("gsub_done"), sem("gexp_done"), sem("eqm_done"), sem("slot_done")
        eq_done = sem("eq_done")
        tr_done, trc_done = sem("tr_done"), sem("trc_done")
        glo_done, hotj_done, hoth_done, hotl_done = sem("glo_done"), sem("hotj_done"), sem("hoth_done"), sem("hotl_done")
        hot_used, gps_free = sem("hot_used"), sem("gps_free")
        gst_out = [sem("gst_out0"), sem("gst_out1")]
        up_out, up_in = [sem("up_out0"), sem("up_out1")], [sem("up_in0"), sem("up_in1")]
        h2_out, h2_in, g_in = sem("h2_out"), sem("h2_in"), sem("g_in")
        gated_done, acthi_done, actlo_done = sem("gated_done"), sem("acthi_done"), sem("actlo_done")
        v_done, v_free = sem("v_done"), sem("v_free")
        fin_done, fin_out = sem("fin_done"), [sem("fin_out0"), sem("fin_out1")]
        dve_step, pool_step = sem("dve_step"), sem("pool_step")
        s5_step, ml_step, pk_step = sem("s5_step"), sem("ml_step"), sem("pk_step")
        waited = sem("waited")
        ms_done, msd_done = sem("ms_done"), sem("msd_done")

        block = ctx.enter_context(nc.Block())

        @block.sync
        def _(sp):
            for i in range(4):
                sp.dma_start(x[:, 4 * i:4 * i + 4, :], a["xT"][:, 4 * i:4 * i + 4, :]).then_inc(x_in[i], 16)
            for k in range(2):
                sp.dma_start(raw[:, k, :], a["stream"][k]).then_inc(raw_in[k], 16)
            with sp.Fori(1, N_STREAM // 2) as m:
                for k in range(2):
                    sp.wait_ge(hi_done, 2 * m + k - 1)
                    sp.wait_ge(lo_done, 2 * m + k - 1)
                    sp.dma_start(raw[:, k, :], a["stream"][2 * m + k]).then_inc(raw_in[k], 16)

        @block.gpsimd
        def _(pool):
            n = [0]

            def step(ins):
                n[0] += 1
                ins.then_inc(pool_step, 1)
                pool.wait_ge(pool_step, n[0])

            pool.dma_start(vec[:], a["vecs"]).then_inc(vec_in, 16)
            pool.memset(ones[:], 1.0).then_inc(const_done, 1)
            pool.dma_start(wif[:], a["wif"]).then_inc(wif_in, 16)
            pool.dma_start(craw[:], a["c_tab"]).then_inc(craw_in, 16)
            pool.dma_start(bc[:], a["b_tab"][0]).then_inc(bc_in, 16)
            step(pool.memset(ident[:], 0.0))
            step(pool.memset(tri[:], 1.0))
            pool.affine_select(out=ident[:], in_=ident[:], compare_op=ALU.not_equal, fill=1.0, base=0,
                               pattern=[[-1, P]], channel_multiplier=1).then_inc(const_done, 1)
            pool.affine_select(out=tri[:], in_=tri[:], compare_op=ALU.is_ge, fill=0.0, base=0,
                               pattern=[[1, P]], channel_multiplier=-1).then_inc(const_done, 1)
            pool.iota(iota[:], [[1, P]], base=0, channel_multiplier=0,
                      allow_small_or_imprecise_dtypes=True).then_inc(const_done, 1)

            pool.wait_ge(gates_done, 1)
            pool.dma_start(gates_d.rearrange("g h t -> h g t"), gout[0:HEADS, :, :]).then_inc(gates_out, 16)

            pool.wait_ge(coef_done, 1)
            pool.wait_ge(proj_free, SC)
            with pool.Fori(0, SC) as c:
                pool.wait_ge(cm_done, 4 * c)
                pool.wait_ge(ylo_done, c)
                pool.tensor_copy(uc[:], uT[:, c, :])
                for r in range(2):
                    pool.tensor_copy(cc[:, r, :, :], cp[:, r, :, :].rearrange("p (c k) h -> p c k h", c=4)[:, c, :, :])
                    pool.tensor_copy(pc[:, r, :, :],
                                     ptab[:, r, :, :].rearrange("p n (c k) -> p c n k", c=4)[:, c, :, :])
                pool.tensor_copy(rc[:, 0:4], cw[:, 0, :].rearrange("p (c k) -> p c k", c=4)[:, c, :])
                pool.tensor_copy(rc[:, 4:5], vec[:, V_DSKIP:V_DSKIP + SC].rearrange("p (c k) -> p c k", k=1)[:, c, :])\
                    .then_inc(chunk_done, 1)
                for k in range(4):
                    pool.wait_ge(bus_done, 8 * c + 2 * k + 2)
                    pool.wait_ge(tab_done, 4 * c + k + 1)
                    pool.tensor_tensor(ptmp[:, 0, :], bus[:, 1, :], tab[:, k % 2, 0, :], ALU.mult).then_inc(pool_step, 1)
                    pool.tensor_tensor(ptmp[:, 1, :], bus[:, 0, :], tab[:, k % 2, 1, :], ALU.mult).then_inc(pool_step, 1)
                    pool.wait_ge(pool_step, 2 + 16 * c + 4 * k + 2)
                    pool.wait_ge(scan_done, 8 * c + 2 * k)
                    pool.tensor_tensor(rin[:, 1, :], ptmp[:, 0, :], ptmp[:, 1, :], ALU.subtract).then_inc(prot_done, 1)
                    pool.wait_ge(prot_done, 4 * c + k + 1)
                    pool.wait_ge(scan_done, 8 * c + 2 * k + 2)
                    pool.tensor_tensor(ptmp[:, 0, :], wst[:, 0, :], tab[:, k % 2, 1, :], ALU.mult).then_inc(pool_step, 1)
                    pool.tensor_tensor(ptmp[:, 1, :], wst[:, 1, :], tab[:, k % 2, 0, :], ALU.mult).then_inc(pool_step, 1)
                    pool.wait_ge(pool_step, 2 + 16 * c + 4 * k + 4)
                    pool.wait_ge(cm_done, 4 * c + k)
                    pool.tensor_tensor(rout[:, 1, :], ptmp[:, 0, :], ptmp[:, 1, :], ALU.add).then_inc(out_i_done, 1)
                pool.wait_ge(bu_done, 8 * c + 8)
                pool.dma_start(bc[:], a["b_tab"][c + 1]).then_inc(bc_in, 16)

            pool.wait_ge(cm_done, 16)
            for b in range(2):
                pool.wait_ge(stage_out[b], 16 * 28)
                pool.dma_start(sa[:, b, :], spill[U_GA - U_XM + b]).then_inc(sa_in[b], 16)

            def glu_block(p, b):
                pool.wait_ge(proj_free, O_GLU + 4 * p + 2 * b + 2)
                pool.wait_ge(sa_in[b], 16 * p + 16)
                pool.tensor_tensor(vt[:, b, :], vt[:, b, :], sa[:, b, :], ALU.mult).then_inc(ya_done, 1)
                pool.wait_ge(ya_done, 2 * p + b + 1)
                pool.dma_start(ya_d[2 * p + b], vt[:, b, :]).then_inc(ya_out[b], 16)

            with pool.Fori(0, KC // 2 - 1) as p:
                for b in range(2):
                    glu_block(p, b)
                    pool.dma_start(sa[:, b, :], spill[U_GA - U_XM + 2 * p + b + 2]).then_inc(sa_in[b], 16)
            for b in range(2):
                glu_block(KC // 2 - 1, b)
            for b in range(2):
                pool.wait_ge(ya_out[b], 16 * 8)

            pool.wait_ge(gates_out, 16)
            with pool.Fori(0, HEADS) as h:
                pool.wait_ge(xmlo_done, 3 * h)
                pool.wait_ge(cv_done, 3 * h)
                pool.dma_start(xmr[:], spill[0:MC].rearrange("(h c) p t -> h p c t", c=HC)[h]).then_inc(xm_in, 16)
                pool.wait_ge(hz_done, 3 * h)
                pool.dma_start(sz[:], spill[MC:2 * MC].rearrange("(h c) p t -> h p c t", c=HC)[h]).then_inc(sz_in, 16)
                pool.wait_ge(en_done, 4 * h)
                pool.wait_ge(pv_free, 3 * h)
                pool.dma_start(m_bc[:], gates_d[1, h].partition_broadcast(P)).then_inc(bcst_in, 16)
                pool.dma_start(em_bc[:], gates_d[2, h].partition_broadcast(P)).then_inc(bcst_in, 16)
                with nc.allow_non_contiguous_dma(reason="one value a partition"):
                    pool.dma_start(gcol[:], gates_d[0, h].rearrange("(s p) -> p s", p=P)).then_inc(bcst_in, 16)
                for c in range(HC):
                    pool.wait_ge(xmhi_done, 3 * h + c + 1)
                    if c == 0:
                        pool.wait_ge(proj_done, O_QKV + 10 * h)
                    pool.tensor_tensor(xm_lo[:, c, :], xmr[:, c, :], xm_hi[:, c, :].bitcast(F32), ALU.subtract)\
                        .then_inc(xmlo_done, 1)
                pool.wait_ge(sz_in, 16 * h + 16)
                for c in range(HC):
                    pool.wait_ge(pv_free, 3 * h + c + 1)
                    pool.tensor_tensor(hh[:, c, :], hh[:, c, :], sz[:, c, :], ALU.mult).then_inc(hz_done, 1)
                pool.wait_ge(xclo_done, 3 * h + 3)
                for c in range(HC):
                    if c >= 2:
                        pool.wait_ge(hf_done, 3 * h + c - 1)
                    pool.tensor_tensor(xcf[:, c % 2, :], xc_hi[:, 3 * h + c, :].bitcast(F32),
                                       xc_lo[:, 3 * h + c, :].bitcast(F32), ALU.add).then_inc(xs_done, 1)

            pool.wait_ge(hf_done, 12)
            for b in range(2):
                pool.dma_start(yal[:, b, :], ya_d[b]).then_inc(yl_in[b], 16)
                pool.dma_start(sbl[:, b, :], spill[U_GB - U_XM + b]).then_inc(yl_in[b], 16)
            with pool.Fori(1, KC // 2) as p:
                for b in range(2):
                    pool.wait_ge(mt_done, 2 * p + b - 1)
                    pool.dma_start(yal[:, b, :], ya_d[2 * p + b]).then_inc(yl_in[b], 16)
                    pool.dma_start(sbl[:, b, :], spill[U_GB - U_XM + 2 * p + b]).then_inc(yl_in[b], 16)
            for b in range(2):
                pool.dma_start(xres[:, b, :], a["xT"][:, b, :]).then_inc(xr_in[b], 16)
            with pool.Fori(1, KC // 2) as p:
                for b in range(2):
                    pool.wait_ge(proj_free, O_WO + 2 * p + b - 1)
                    pool.dma_start(xres[:, b, :], a["xT"][:, 2 * p + b, :]).then_inc(xr_in[b], 16)
            pool.dma_start(key_raw[:], a["keys"]).then_inc(key_in, 16)
            pool.wait_ge(proj_free, O_UP)
            pool.dma_start(h2_d, h2[:]).then_inc(h2_out, 16)

            def next_lo(m, k):
                nm, nk = (m, 1) if k == 0 else (m + 1, 0)
                pool.wait_ge(hi_done, 2 * nm + nk + 1)
                pool.tensor_tensor(wlo[:, nk, :], raw[:, nk, :], whi[:, nk, :].bitcast(F32), ALU.subtract)\
                    .then_inc(lo_done, 1)

            def indices(hd):
                for r in range(2):
                    pool.wait_ge(eq_done, 2 * hd + r + 1)
                    for tb in range(TB):
                        e = eqs[r][:, tb * TOPK:(tb + 1) * TOPK, :]
                        last = pool.tensor_tensor(
                            e, e, i12[:, r, tb, :].unsqueeze(1).to_broadcast([P, TOPK, TOPK]), ALU.mult)
                    last.then_inc(eqm_done, 1)

            def head_lo(hd, units):
                for n in units:
                    next_lo(U_HEAD // 2 + 3 * hd + n // 2, n % 2)

            head_lo(0, range(6))
            with pool.Fori(1, PH) as hd:
                head_lo(hd, (0, 1))
                indices(hd - 1)
                head_lo(hd, (2, 3, 4, 5))
            next_lo(U_FILL // 2, 0)
            indices(PH - 1)
            for jj in (1, 2, 3):
                next_lo((U_FILL + jj) // 2, jj % 2)

            pool.wait_ge(glo_done, 1)
            lo_cols = gate_lo[:].rearrange("p (n w) -> p n w", w=8)

            def hot_low(n, b):
                pool.wait_ge(hotj_done, n + 1)
                pool.tensor_tensor(hot_jl[:, b, :, :], hot_j[:, b, :, :],
                                   lo_cols[:, n, :].unsqueeze(2).to_broadcast([P, 8, P]), ALU.mult)\
                    .then_inc(hotl_done, 1)

            with pool.Fori(0, 16) as r:
                for s in range(2):
                    for q in range(2):
                        hot_low(4 * r + 2 * s + q, q)
                    next_lo(U_GATE // 2 + r, s)

            pool.wait_ge(hot_used, 4 + 128)
            pool.dma_start(h2[:], h2_d).then_inc(h2_in, 16)
            for s in range(2):
                pool.wait_ge(gst_out[s], 16 * 8)
            gg_src = g_d.rearrange("n i (g j) t -> g i n (j t)", j=4)
            for k in range(2):
                pool.wait_ge(up_out[k], 16)
                pool.dma_start(gl[:, k, :], up_d[k]).then_inc(up_in[k], 16)
            pool.dma_start(gg[:, 0, :, :], gg_src[0]).then_inc(g_in, 16)
            pool.wait_ge(g_in, 16)
            pool.dma_start(gg[:, 1, :, :], gg_src[1]).then_inc(g_in, 16)
            for k in range(2):
                pool.wait_ge(actlo_done, k + 1)
                pool.dma_start(gl[:, k, :], up_d[2 + k]).then_inc(up_in[k], 16)
            for k in range(2):
                pool.wait_ge(up_out[k], 16 * 2 * EARLY)
            with pool.Fori(1, EARLY) as g:
                for jj in range(4):
                    pool.wait_ge(actlo_done, 4 * g + jj - 1)
                    pool.dma_start(gl[:, jj % 2, :], up_d[4 * g + jj]).then_inc(up_in[jj % 2], 16)
                    if jj == 1:
                        pool.wait_ge(g_in, 16 * g + 16)
                        pool.wait_ge(gated_done, 4 * g)
                        pool.dma_start(gg[:, (g + 1) % 2, :, :], gg_src[g + 1]).then_inc(g_in, 16)
            with pool.Fori(EARLY, GROUPS_E - 1) as g:
                pool.wait_ge(g_in, 16 * g + 16)
                pool.wait_ge(gated_done, 4 * g)
                pool.dma_start(gg[:, (g + 1) % 2, :, :], gg_src[g + 1]).then_inc(g_in, 16)

            with pool.Fori(0, KC // 2) as p:
                for b in range(2):
                    pool.wait_ge(fin_done, 2 * p + b + 1)
                    pool.dma_start(out_d[:, 2 * p + b, :], fin[:, b, :]).then_inc(fin_out[b], 16)
            for b in range(2):
                pool.wait_ge(fin_out[b], 16 * 8)

        @block.scalar
        def _(act):
            def met():
                act.wait_ge(const_done, 4)

            def split_hi(m, k, free=None):
                act.wait_ge(raw_in[k], 16 * m + 16)
                if free is not None:
                    act.wait_ge(*free)
                act.activation(whi[:, k, :], raw[:, k, :], ACT.Copy).then_inc(hi_done, 1)

            def next_hi(m, k, free):
                nm, nk = (m, 1) if k == 0 else (m + 1, 0)
                split_hi(nm, nk, free)

            def squares(r, src):
                for d in range(KC):
                    if 16 * r + d >= 2:
                        act.wait_ge(ssq_done, 16 * r + d - 1)
                    if r == 0 and d % 4 == 0:
                        act.wait_ge(x_in[d // 4], 16)
                    act.activation(sq[:, d % 2, :], src[:, d, :], ACT.Square).then_inc(sq_done, 1)
                act.wait_ge(ms_done, r + 1)
                act.activation(rs[:], ms[:], ACT.Sqrt).then_inc(rt_done, 1)

            act.wait_ge(const_done, 4)
            act.activation(ones_r[:], ones[:], ACT.Copy).then_inc(onesr_done, 1)
            squares(0, x)
            split_hi(0, 0)
            with act.Fori(0, KC) as d:
                met()
                act.wait_ge(xn_done, d + 1)
                act.activation(hn_hi[:, d, :], x[:, d, :], ACT.Copy).then_inc(ahi_done, 1)

            for nu in range(SC):
                next_hi(nu // 2, nu % 2, (proj_done, nu))
                act.wait_ge(proj_done, nu + 1)
                act.activation(uT[:, nu, :], mm[nu % 2][:], ACT.Copy).then_inc(proj_free, 1)

            def spilled(m, k, func):
                next_hi(m, k, (proj_done, 2 * m + k))
                act.wait_ge(proj_done, 2 * m + k + 1)
                act.wait_ge(stage_out[k], 16 * (m - U_XM // 2))
                act.activation(stage[:, k, :], mm[k][:], func).then_inc(proj_free, 1)
                act.wait_ge(proj_free, 2 * m + k + 1)
                act.dma_start(spill[2 * m + k - U_XM], stage[:, k, :]).then_inc(stage_out[k], 16)

            with act.Fori(U_XM // 2, U_Z // 2) as m:
                for k in range(2):
                    spilled(m, k, ACT.Copy)
            act.wait_ge(ge_sem, 1)
            act.activation(gt[0:HEADS, 2, :], gt[0:HEADS, 1, :], ACT.Exp, scale=-1.0).then_inc(ge_sem, 1)
            with act.Fori(U_Z // 2, U_GA // 2 - 1) as m:
                for k in range(2):
                    spilled(m, k, ACT.Sigmoid)
            act.wait_ge(ge_sem, 3)
            act.activation(gout[0:HEADS, 2, :], gt[0:HEADS, 0, :], ACT.Exp, scale=-1.0).then_inc(gates_done, 1)
            for k in range(2):
                spilled(U_GA // 2 - 1, k, ACT.Sigmoid)

            with act.Fori(0, SC) as c:
                for k in range(4):
                    m = U_GA // 2 + 4 * c + k
                    spilled(m, 0, ACT.Sigmoid)
                    for r in range(2):
                        act.wait_ge(bu_done, 8 * c + 2 * k + r + 1)
                        if r == 0:
                            act.wait_ge(prot_done, 4 * c + k)
                            act.wait_ge(rot_done, 4 * c + k)
                        act.activation(bus[:, r, :], sb_[r][:], ACT.Copy).then_inc(bus_done, 1)
                    spilled(m, 1, ACT.Sigmoid)
                act.wait_ge(yp_done, c + 1)
                act.activation(dtmp[:, 0, :], dtmp[:, 0, :], ACT.Gelu_apprx_tanh).then_inc(yg_done, 1)
                met()
                act.wait_ge(yg_done, c + 1)
                act.activation(y_hi[:, c, :], dtmp[:, 0, :], ACT.Copy).then_inc(yhi_done, 1)

            with act.Fori(0, 4) as q:
                for k in range(2):
                    next_hi(U_GLU // 2 + q, k, (proj_done, O_GLU + 8 * q + 4 * k))
                    for b in range(2):
                        act.wait_ge(proj_done, O_GLU + 8 * q + 4 * k + 2 * b + 2)
                        act.wait_ge(proj_free, O_GLU + 8 * q + 4 * k + 2 * b - 2)
                        act.activation(sgt[:, b, :], (mm, pv)[b][1][:], ACT.Sigmoid).then_inc(sg_done, 1)

            with act.Fori(0, HEADS) as h:
                split_hi(U_QKV // 2 + h, 1, (proj_done, O_QKV + 10 * h))
                act.wait_ge(xm_in, 16 * h + 16)
                for c in range(HC):
                    act.activation(xm_hi[:, c, :], xmr[:, c, :], ACT.Copy).then_inc(xmhi_done, 1)
                for c in range(HC):
                    act.wait_ge(cv_done, 3 * h + c + 1)
                    act.wait_ge(hflo_done, 3 * h)
                    if c == 2:
                        act.wait_ge(xclo_done, 3 * h + 1)
                    act.activation(xcf[:, c % 2, :], cv[:, c % 2, :], ACT.Silu).then_inc(silu_done, 1)
                    met()
                    act.wait_ge(silu_done, 3 * h + c + 1)
                    act.activation(xc_hi[:, 3 * h + c, :], xcf[:, c % 2, :], ACT.Copy).then_inc(xchi_done, 1)
                for j in range(10):
                    act.wait_ge(proj_done, O_QKV + 10 * h + j + 1)
                    if j < 3:
                        act.activation(q_hi[:, j, :], mm[j % 2][:], ACT.Copy).then_inc(qkv_hi_done, 1)
                    elif j < 6:
                        act.activation(k_hi[:, j - 3, :], mm[j % 2][:], ACT.Copy, scale=HD ** -0.5)\
                            .then_inc(qkv_hi_done, 1)
                    else:
                        act.activation(v_hi[:, j - 6, :], mm[j % 2][:, 0:HD], ACT.Copy).then_inc(qkv_hi_done, 1)
                split_hi(U_QKV // 2 + h + 1, 0, (proj_done, O_QKV + 10 * h + 10))
                for s in range(TB):
                    w = T - P * s
                    act.wait_ge(en_done, 4 * h + s + 1)
                    act.activation(ex[:, s % 2, 0:w], ex[:, s % 2, 0:w], ACT.Exp).then_inc(ex_done, 1)
                    act.wait_ge(pf_done, 4 * h + s + 1)
                    act.activation(p_hi[:, s, P * s:T], pf[:, s % 2, 0:w], ACT.Copy).then_inc(phi_done, 1)
                for c in range(HC):
                    act.wait_ge(hc_done, 3 * h + c + 1)
                    act.activation(hsq[c], hh[:, c, :], ACT.Square).then_inc(hsq_done, 1)
                act.wait_ge(msd_done, h + 1)
                act.activation(rs[:], cv[:, 0, :], ACT.Sqrt).then_inc(std_done, 1)
                for c in range(HC):
                    met()
                    act.wait_ge(hf_done, 3 * h + c + 1)
                    act.activation(xc_hi[:, 3 * h + c, :], hh[:, c, :], ACT.Copy).then_inc(hfhi_done, 1)

            with act.Fori(0, KC // 2) as p:
                for k in range(2):
                    next_hi(U_YB // 2 + p, k, (proj_done, O_YB + 2 * p + k))
                    met()
                    act.wait_ge(mt_done, 2 * p + k + 1)
                    act.activation(mg_hi[:, 2 * p + k, :], mt[:, k, :], ACT.Copy).then_inc(mghi_done, 1)
            with act.Fori(0, KC // 2) as p:
                for k in range(2):
                    next_hi(U_WO // 2 + p, k, (proj_done, O_WO + 2 * p + k))
            act.wait_ge(proj_free, O_UP)
            squares(1, h2)
            with act.Fori(0, KC // 2) as p:
                for k in range(2):
                    met()
                    act.wait_ge(xn_done, KC + 2 * p + k + 1)
                    act.activation(t_hi[:, 2 * p + k, :], xt[:, k, :], ACT.Copy).then_inc(ahi_done, 1)
            act.wait_ge(key_in, 16)
            act.activation(key_hi[:], key_raw[:], ACT.Copy).then_inc(khi_done, 1)

            act.wait_ge(klo_done, 1)

            def stored_up(half, k):
                n = 2 * half + k
                act.wait_ge(proj_done, O_UP + n + 1)
                act.wait_ge(up_out[k], 16 * half)
                act.activation(sgl[:, k, :], mm[k][:], ACT.Gelu_apprx_tanh).then_inc(proj_free, 1)
                act.wait_ge(proj_free, O_UP + n + 1)
                act.dma_start(up_d[n], sgl[:, k, :]).then_inc(up_out[k], 16)

            def queries(hd):
                m = U_HEAD // 2 + 3 * hd
                for k in range(2):
                    next_hi(m, k, (proj_done, O_UP + 4 * hd) if k == 0 else (qp_done, 2 * hd + 1))
                    act.wait_ge(qp_done, 2 * hd + k + 1)
                    act.wait_ge(sco_done, 2 * hd)
                    act.activation(qq_hi[:, k, :], pv[k][:], ACT.Copy).then_inc(qhi_done, 1)

            def ups(hd):
                m = U_HEAD // 2 + 3 * hd
                for jj in range(4):
                    next_hi(m + 1 + jj // 2, jj % 2,
                            (qp_done, 2 * hd + 2) if jj == 0 else (proj_done, O_UP + 4 * hd + jj))
                    stored_up(2 * hd + jj // 2, jj % 2)

            def softmax_exp(hd):
                act.wait_ge(gsub_done, hd + 1)
                act.activation(ge[:], ge[:], ACT.Exp).then_inc(gexp_done, 1)

            queries(0)
            ups(0)
            with act.Fori(1, PH) as hd:
                queries(hd)
                softmax_exp(hd - 1)
                ups(hd)
            for jj in range(4):
                next_hi((U_FILL + jj) // 2, jj % 2, (proj_done, O_UP + N_FILL + jj))
                stored_up((N_FILL + jj) // 2, jj % 2)
                if jj == 1:
                    softmax_exp(PH - 1)
                if jj == 2:
                    for v in range(3):
                        act.wait_ge(tr_done, v + 1)
                        act.activation(gate_hi[:] if v == 0 else slot_t[:, v - 1, :], (dn, pv[0], pv[1])[v][:],
                                       ACT.Copy).then_inc(trc_done, 1)

            act.wait_ge(trc_done, 3)
            act.sem_inc(gps_free, 4)
            with act.Fori(0, 8) as r2:
                for s2 in range(2):
                    block_no = 2 * r2 + s2
                    m = U_GATE // 2 + block_no
                    act.wait_ge(gst_out[s2], 16 * r2)
                    for s in range(2):
                        next_hi(m, s, (proj_done, O_UP + N_GATE + 2 * block_no + s))
                        for b in range(4 * s, 4 * s + 4):
                            act.wait_ge(hot_used, 4 + 8 * block_no + b + 1)
                            act.activation(gst[:, s2, :, 4 * b:4 * b + 4],
                                           vo[b % 4][:].rearrange("p (t j) -> p j t", t=4), ACT.Copy)\
                                .then_inc(gps_free, 1)
                        stored_up(N_GATE // 2 + block_no, s)
                    act.wait_ge(gps_free, 4 + 8 * block_no + 8)
                    act.dma_start(g_d[block_no], gst[:, s2, :, :]).then_inc(gst_out[s2], 16)

            def act_high(g, par, jj):
                act.activation(act_hi[:, par, jj, :], gl[:, jj % 2, :], ACT.Copy).then_inc(acthi_done, 1)

            for jj in range(4):
                next_hi((U_LAST + jj) // 2, jj % 2, (proj_done, O_UP + N_LAST + jj))
                stored_up((N_LAST + jj) // 2, jj % 2)
                if jj == 2:
                    for j0 in range(4):
                        act.wait_ge(gated_done, j0 + 1)
                        act_high(0, 0, j0)
            with act.Fori(0, EARLY - 1) as g:
                for jj in range(4):
                    m, k = U_DOWN // 2 + 2 * g + jj // 2, jj % 2
                    act.wait_ge(proj_done, O_UP + 4 * EARLY)
                    next_hi(m, k, (v_done, 16 * g + 4 * jj))
                    met()
                    if jj == 0:
                        act.wait_ge(v_done, 16 * g)
                    act.wait_ge(gated_done, 4 * g + jj + 5)
                    act_high(g + 1, (g + 1) % 2, jj)
            with act.Fori(EARLY - 1, GROUPS_E - 1) as g:
                for jj in range(4):
                    m = U_PAIR // 2 + 4 * (g - (EARLY - 1)) + jj
                    split_hi(m, 1, (v_done, 16 * g + 4 * jj))
                    act.wait_ge(proj_done, O_UP + 4 * g + jj + 5)
                    act.wait_ge(actlo_done, 4 * g + jj + 3)
                    act.activation(gl[:, jj % 2, :], mm[jj % 2][:], ACT.Gelu_apprx_tanh).then_inc(proj_free, 1)
                    split_hi(m + 1, 0, (proj_done, O_UP + 4 * g + jj + 5))
                    met()
                    if jj == 0:
                        act.wait_ge(v_done, 16 * g)
                    act.wait_ge(gated_done, 4 * g + jj + 5)
                    act_high(g + 1, (g + 1) % 2, jj)
            for jj in range(3):
                nu = N_STREAM - 4 + jj + 1
                split_hi(nu // 2, nu % 2, (v_done, 16 * (GROUPS_E - 1) + 4 * jj))

            act.wait_ge(v_free, 4 + 16 * GROUPS_E)
            squares(2, h2)

        @block.vector
        def _(dve):
            n = [0]

            def step(ins):
                n[0] += 1
                ins.then_inc(dve_step, 1)
                dve.wait_ge(dve_step, n[0])

            def stepper(s, at):
                k = [0]

                def one(ins, wait=True, apart=False):
                    k[0] += 1
                    ins.then_inc(s, 1)
                    if wait:
                        dve.wait_ge(s, at + k[0])
                    if apart:
                        carrier()
                return one, k

            def carrier():
                dve.sem_inc(waited, 1)

            def split_lo(m, k):
                dve.wait_ge(hi_done, 2 * m + k + 1)
                dve.tensor_tensor(wlo[:, k, :], raw[:, k, :], whi[:, k, :].bitcast(F32), ALU.subtract)\
                    .then_inc(lo_done, 1)

            def next_lo(m, k):
                nm, nk = (m, 1) if k == 0 else (m + 1, 0)
                split_lo(nm, nk)

            def newton(one, y, ms_, tmp):
                one(dve.tensor_tensor(tmp, y, y, ALU.mult))
                one(dve.tensor_tensor(tmp, tmp, ms_, ALU.mult))
                one(dve.tensor_scalar(tmp, tmp, -0.5, 1.5, ALU.mult, ALU.add))
                one(dve.tensor_tensor(y, y, tmp, ALU.mult))

            def norm_scale(r):
                dve.wait_ge(ssq_done, KC * (r + 1))
                dve.tensor_scalar(ms[:], st[:], 1.0 / D, EPS, ALU.mult, ALU.add).then_inc(ms_done, 1)
                dve.wait_ge(rt_done, r + 1)
                step(dve.reciprocal(rs[:], rs[:]))
                dve.wait_ge(ms_done, r + 1)
                newton(step, rs[:], ms[:], nt[:])

            def cols(v0, nv):
                return vec[:, v0:v0 + nv].rearrange("p (d o) -> p d o", o=1)

            dve.wait_ge(vec_in, 16)
            norm_scale(0)

            def xn(d):
                dve.scalar_tensor_tensor(x[:, d, :], x[:, d, :], cols(V_G1, KC)[:, d, :], rs[:],
                                         ALU.mult, ALU.mult).then_inc(xn_done, 1)

            def xlo(d):
                dve.wait_ge(ahi_done, d + 1)
                dve.tensor_tensor(hn_lo[:, d, :], x[:, d, :], hn_hi[:, d, :].bitcast(F32), ALU.subtract)\
                    .then_inc(alo_done, 1)

            split_lo(0, 0)
            xn(0)
            with dve.Fori(1, KC) as d:
                xn(d)
                xlo(d - 1)
            xlo(KC - 1)

            for nu in range(SC):
                next_lo(nu // 2, nu % 2)

            C = {}

            def col(name):
                if name not in C:
                    C[name] = len(C)
                return cw[:, C[name], :]

            def ts(o, i, s1, s2, o1, o2=None):
                step(dve.tensor_scalar(o, i, s1, s2, o1, o2) if o2 is not None else
                     dve.tensor_scalar(o, i, s1, None, o1))

            def tt(o, i, j, op):
                step(dve.tensor_tensor(o, i, j, op))

            def stt(o, i, s, j, o1, o2):
                step(dve.scalar_tensor_tensor(o, i, s, j, o1, o2))

            radius = col("radius")

            def exp_of(o, i):
                xx, nn, rr, qq = col("xx"), col("nn"), col("rr"), col("qq")
                ts(xx, i, -88.02, 89.0, ALU.max, ALU.min)
                ts(nn, xx, LOG2E, ROUND, ALU.mult, ALU.add)
                ts(nn, nn, -ROUND, None, ALU.add)
                stt(rr, nn, -LN2_HI, xx, ALU.mult, ALU.add)
                stt(rr, nn, -LN2_LO, rr, ALU.mult, ALU.add)
                ts(qq, rr, 1.0 / 5040, None, ALU.mult)
                for c in (1.0 / 720, 1.0 / 120, 1.0 / 24, 1.0 / 6, 0.5, 1.0):
                    stt(qq, qq, c, rr, ALU.add, ALU.mult)
                ts(xx.bitcast(I32), nn, 127.0, 8388608.0, ALU.add, ALU.mult)
                stt(o, qq, 1.0, xx, ALU.add, ALU.mult)

            lre, lim, ldt = (vec[:, v:v + 16] for v in (V_LRE, V_LIM, V_LDT))
            dt, th = col("dt"), col("th")
            exp_of(dt, ldt)
            tt(th, lre, dt, ALU.mult)
            exp_of(radius, th)
            tt(th, lim, dt, ALU.mult)
            nn, rr, zz, ss, co = col("nn"), col("rr"), col("zz"), col("ss"), col("co")
            ts(nn, th, 2.0 / np.pi, ROUND, ALU.mult, ALU.add)
            ts(nn, nn, -ROUND, None, ALU.add)
            stt(rr, nn, -HALF_PI[0], th, ALU.mult, ALU.add)
            stt(rr, nn, -HALF_PI[1], rr, ALU.mult, ALU.add)
            stt(rr, nn, -HALF_PI[2], rr, ALU.mult, ALU.add)
            tt(zz, rr, rr, ALU.mult)
            ts(ss, zz, -1.9515295891e-4, None, ALU.mult)
            stt(ss, ss, 8.3321608736e-3, zz, ALU.add, ALU.mult)
            stt(ss, ss, -1.6666654611e-1, zz, ALU.add, ALU.mult)
            stt(ss, ss, 1.0, rr, ALU.add, ALU.mult)
            ts(co, zz, 2.443315711809948e-5, None, ALU.mult)
            stt(co, co, -1.388731625493765e-3, zz, ALU.add, ALU.mult)
            stt(co, co, 4.166664568298827e-2, zz, ALU.add, ALU.mult)
            stt(co, co, -0.5, zz, ALU.add, ALU.mult)
            ts(co, co, 1.0, None, ALU.add)
            ni, bi, b0, b1 = col("ni").bitcast(I32), col("bi").bitcast(I32), col("b0"), col("b1")
            step(dve.tensor_copy(ni, nn))
            ts(bi, ni, 1, None, ALU.bitwise_and)
            step(dve.tensor_copy(b0, bi))
            ts(bi, ni, 1, 1, ALU.arith_shift_right, ALU.bitwise_and)
            step(dve.tensor_copy(b1, bi))
            ts(b1, b1, -2.0, 1.0, ALU.mult, ALU.add)
            d1, d2, e1, e2 = col("d1"), col("d2"), col("e1"), col("e2")
            ts(d2, b0, -1.0, 1.0, ALU.mult, ALU.add)
            tt(e1, ss, d2, ALU.mult)
            tt(e2, co, b0, ALU.mult)
            tt(e1, e1, e2, ALU.add)
            tt(ptab[:, 1, 0, :], e1, b1, ALU.mult)
            tt(e1, co, d2, ALU.mult)
            tt(e2, ss, b0, ALU.mult)
            tt(e1, e1, e2, ALU.subtract)
            tt(ptab[:, 0, 0, :], e1, b1, ALU.mult)
            for i in range(1, 9):
                c0, s0 = ptab[:, 0, i - 1, :], ptab[:, 1, i - 1, :]
                tt(e1, c0, c0, ALU.mult)
                tt(e2, s0, s0, ALU.mult)
                tt(ptab[:, 0, i, :], e1, e2, ALU.subtract)
                stt(ptab[:, 1, i, :], c0, 2.0, s0, ALU.mult, ALU.mult)
            fr, fi = col("fr"), col("fi")
            tt(d1, radius, ptab[:, 0, 0, :], ALU.mult)
            ts(d1, d1, -1.0, None, ALU.add)
            tt(d2, radius, ptab[:, 1, 0, :], ALU.mult)
            tt(e1, lre, lre, ALU.mult)
            tt(e2, lim, lim, ALU.mult)
            tt(zz, e1, e2, ALU.add)
            step(dve.reciprocal(zz, zz))
            tt(e1, d1, lre, ALU.mult)
            tt(e2, d2, lim, ALU.mult)
            tt(e1, e1, e2, ALU.add)
            tt(fr, e1, zz, ALU.mult)
            tt(e1, d2, lre, ALU.mult)
            tt(e2, d1, lim, ALU.mult)
            tt(e1, e1, e2, ALU.subtract)
            tt(fi, e1, zz, ALU.mult)
            dve.wait_ge(craw_in, 16)
            dve.wait_ge(if_done, 1)
            frb = fr.unsqueeze(2).to_broadcast([P, 16, 32])
            fib = fi.unsqueeze(2).to_broadcast([P, 16, 32])
            cr, ci = craw[:, 0, :, :], craw[:, 1, :, :]
            w0 = dtmp[:, 0, :].rearrange("p (q h) -> p q h", q=16)
            tt(w0, cr, frb, ALU.mult)
            tt(cp[:, 0, :, :], ci, fib, ALU.mult)
            tt(cp[:, 0, :, :], w0, cp[:, 0, :, :], ALU.subtract)
            tt(w0, ci, frb, ALU.mult)
            tt(cp[:, 1, :, :], cr, fib, ALU.mult)
            tt(cp[:, 1, :, :], w0, cp[:, 1, :, :], ALU.add)
            dve.tensor_scalar(cp[:, 1, :, :], cp[:, 1, :, :], -1.0, None, ALU.mult).then_inc(coef_done, 1)

            with dve.Fori(U_XM // 2, U_Z // 2) as m:
                for k in range(2):
                    next_lo(m, k)

            gi, g1, g2, gf = (gt[0:HEADS, i, :] for i in range(4))
            go, gm, g5 = (gout[0:HEADS, i, :] for i in range(3))
            ts(gi, pv[0][0:HEADS, :], vec[0:HEADS, V_BI:V_BI + 1], None, ALU.add)
            ts(gf, pv[0][32:32 + HEADS, :], vec[32:32 + HEADS, V_BF:V_BF + 1], None, ALU.add)
            dve.scalar_tensor_tensor(g1, gf, -1.0, gf, ALU.mult, ALU.max).then_inc(ge_sem, 1)
            with dve.Fori(U_Z // 2, U_GA // 2 - 1) as m:
                for k in range(2):
                    next_lo(m, k)
            dve.wait_ge(ge_sem, 2)
            ts(g1, g2, 2.0, None, ALU.add)
            step(dve.reciprocal(g1, g1))
            tt(g1, g2, g1, ALU.mult)
            tt(go, g1, g1, ALU.mult)
            ts(g2, go, 1.0 / 17, None, ALU.mult)
            for d in (15, 13, 11, 9, 7, 5, 3):
                stt(g2, g2, 1.0 / d, go, ALU.add, ALU.mult)
            stt(g2, g2, 1.0, g1, ALU.add, ALU.mult)
            ts(gf, gf, 0.0, None, ALU.min)
            stt(gf, g2, -2.0, gf, ALU.mult, ALU.add)
            one_b = ones[0:HEADS, 0:1].to_broadcast([HEADS, T])
            step(dve.tensor_tensor_scan(g1, one_b, gf, 0.0, ALU.mult, ALU.add))
            tt(go, gi, g1, ALU.subtract)
            step(dve.tensor_tensor_scan(g2, one_b, go, 0.0, ALU.mult, ALU.max))
            ts(gm, g2, -1.0, None, ALU.mult)
            dve.tensor_tensor(gi, g1, g2, ALU.add).then_inc(ge_sem, 1)
            for k in range(2):
                next_lo(U_GA // 2 - 1, k)

            with dve.Fori(0, SC) as c:
                one, count = stepper(s5_step, S5_STEPS * c)
                dve.wait_ge(chunk_done, c + 1)
                for k in range(4):
                    m = U_GA // 2 + 4 * c + k
                    next_lo(m, 0)
                    dve.wait_ge(out_i_done, 4 * c + k - 1 if k else 4 * c)
                    tc_, ts_ = tab[:, k % 2, 0, :], tab[:, k % 2, 1, :]
                    one(dve.memset(tc_[:, 0:1], 1.0), wait=False)
                    one(dve.memset(ts_[:, 0:1], 0.0))
                    for lv in range(9):
                        w = 1 << lv
                        pcos, psin = pc[:, 0, lv, k:k + 1], pc[:, 1, lv, k:k + 1]
                        one(dve.tensor_scalar(dtmp[:, 0, 0:w], ts_[:, 0:w], psin, None, ALU.mult), wait=False)
                        one(dve.tensor_scalar(dtmp[:, 1, 0:w], ts_[:, 0:w], pcos, None, ALU.mult))
                        one(dve.scalar_tensor_tensor(tc_[:, w:2 * w], tc_[:, 0:w], pcos, dtmp[:, 0, 0:w],
                                                     ALU.mult, ALU.subtract), wait=False)
                        ins = dve.scalar_tensor_tensor(ts_[:, w:2 * w], tc_[:, 0:w], psin, dtmp[:, 1, 0:w],
                                                       ALU.mult, ALU.add)
                        if lv < 8:
                            one(ins)
                        else:
                            ins.then_inc(tab_done, 1)
                    dve.wait_ge(tab_done, 4 * c + k + 1)
                    dve.wait_ge(bus_done, 8 * c + 2 * k + 2)
                    one(dve.tensor_tensor(dtmp[:, 0, :], bus[:, 0, :], tc_, ALU.mult), wait=False)
                    one(dve.tensor_tensor(dtmp[:, 1, :], bus[:, 1, :], ts_, ALU.mult))
                    dve.tensor_tensor(rin[:, 0, :], dtmp[:, 0, :], dtmp[:, 1, :], ALU.add).then_inc(rot_done, 1)
                    dve.wait_ge(rot_done, 4 * c + k + 1)
                    dve.wait_ge(out_i_done, 4 * c + k)
                    rb = rc[:, k:k + 1].to_broadcast([P, T])
                    dve.tensor_tensor_scan(wst[:, 0, :], rb, rin[:, 0, :], 0.0, ALU.mult, ALU.add).then_inc(scan_done, 1)
                    dve.wait_ge(prot_done, 4 * c + k + 1)
                    dve.tensor_tensor_scan(wst[:, 1, :], rb, rin[:, 1, :], 0.0, ALU.mult, ALU.add).then_inc(scan_done, 1)
                    next_lo(m, 1)
                    dve.wait_ge(scan_done, 8 * c + 2 * k + 2)
                    one(dve.tensor_tensor(dtmp[:, 0, :], wst[:, 0, :], tc_, ALU.mult), wait=False)
                    one(dve.tensor_tensor(dtmp[:, 1, :], wst[:, 1, :], ts_, ALU.mult))
                    dve.wait_ge(cm_done, 4 * c + k)
                    dve.tensor_tensor(rout[:, 0, :], dtmp[:, 0, :], dtmp[:, 1, :], ALU.subtract).then_inc(out_r_done, 1)
                dve.wait_ge(out_r_done, 4 * c + 4)
                dve.wait_ge(cm_done, 4 * c + 4)
                dve.scalar_tensor_tensor(dtmp[:, 0, :], uc[:], rc[:, 4:5], dn[:], ALU.mult, ALU.add).then_inc(yp_done, 1)
                dve.wait_ge(yhi_done, c + 1)
                dve.tensor_tensor(y_lo[:, c, :], dtmp[:, 0, :], y_hi[:, c, :].bitcast(F32), ALU.subtract)\
                    .then_inc(ylo_done, 1)
                assert count[0] == S5_STEPS, count

            with dve.Fori(0, 4) as q:
                for k in range(2):
                    next_lo(U_GLU // 2 + q, k)
                    for b in range(2):
                        f = 4 * q + 2 * k + b
                        dve.wait_ge(sg_done, f + 1)
                        dve.wait_ge(ya_out[b], 16 * (2 * q + k))
                        dve.tensor_tensor(vt[:, b, :], (mm, pv)[b][0][:], sgt[:, b, :], ALU.mult).then_inc(proj_free, 2)

            for b in range(2):
                dve.wait_ge(ya_out[b], 16 * 8)
            with dve.Fori(0, HEADS) as h:
                one, count = stepper(ml_step, ML_STEPS * h)
                split_lo(U_QKV // 2 + h, 1)
                dve.wait_ge(xm_in, 16 * h + 16)

                def conv(c):
                    dve.wait_ge(silu_done, 3 * h + 1 if c == 2 else 3 * h)
                    o, i = cv[:, c % 2, :], xmr[:, c, :]
                    tap = [cols(V_CW + MC * j, MC)[:, 3 * h + c, :] for j in range(4)]
                    one(dve.tensor_scalar(o, i, tap[3], cols(V_CB, MC)[:, 3 * h + c, :], ALU.mult, ALU.add))
                    for lag in (1, 2, 3):
                        ins = dve.scalar_tensor_tensor(o[:, lag:T], i[:, 0:T - lag], tap[3 - lag], o[:, lag:T],
                                                       ALU.mult, ALU.add)
                        if lag < 3:
                            one(ins)
                        else:
                            ins.then_inc(cv_done, 1)

                def conv_lo(c):
                    dve.wait_ge(xchi_done, 3 * h + c + 1)
                    dve.tensor_tensor(xc_lo[:, 3 * h + c, :], xcf[:, c % 2, :],
                                      xc_hi[:, 3 * h + c, :].bitcast(F32), ALU.subtract).then_inc(xclo_done, 1)

                conv(0)
                conv(1)
                conv_lo(0)
                conv(2)
                conv_lo(1)
                conv_lo(2)
                for j in range(10):
                    dve.wait_ge(qkv_hi_done, 10 * h + j + 1)
                    src = mm[j % 2]
                    if j < 3:
                        dve.tensor_tensor(q_lo[:, j, :], src[:], q_hi[:, j, :].bitcast(F32), ALU.subtract)\
                            .then_inc(proj_free, 1)
                    elif j < 6:
                        dve.scalar_tensor_tensor(k_lo[:, j - 3, :], src[:], HD ** -0.5,
                                                 k_hi[:, j - 3, :].bitcast(F32), ALU.mult, ALU.subtract)\
                            .then_inc(proj_free, 1)
                    else:
                        dve.tensor_tensor(v_lo[:, j - 6, :], src[:, 0:HD], v_hi[:, j - 6, :].bitcast(F32),
                                          ALU.subtract).then_inc(proj_free, 1)
                split_lo(U_QKV // 2 + h + 1, 0)

                def exponent(s):
                    dve.tensor_scalar(ex[:, s % 2, 0:T - P * s], m_bc[:, P * s:T], gcol[:, s:s + 1], 0.0,
                                      ALU.add, ALU.min).then_inc(en_done, 1)

                dve.wait_ge(bcst_in, 48 * h + 48)
                exponent(0)
                for s in range(TB):
                    w = T - P * s
                    if s + 1 < TB:
                        exponent(s + 1)
                    dve.wait_ge(ex_done, 4 * h + s + 1)
                    one(dve.tensor_tensor(ex[:, s % 2, 0:P], ex[:, s % 2, 0:P], tri[:], ALU.mult))
                    dve.wait_ge(s_done, 4 * h + s + 1)
                    dve.tensor_tensor(pf[:, s % 2, 0:w], sb_[s % 2][:, 0:w], ex[:, s % 2, 0:w], ALU.mult)\
                        .then_inc(pf_done, 1)
                    dve.wait_ge(phi_done, 4 * h + s + 1)
                    dve.tensor_tensor(p_lo[:, s, P * s:T], pf[:, s % 2, 0:w], p_hi[:, s, P * s:T].bitcast(F32),
                                      ALU.subtract).then_inc(plo_done, 1)
                dve.wait_ge(den_done, h + 1)
                one(dve.scalar_tensor_tensor(rd[:], dn[:], -1.0, em_bc[:], ALU.mult, ALU.max))
                one(dve.tensor_tensor(rd[:], dn[:], rd[:], ALU.max))
                one(dve.reciprocal(rd[:], rd[:]))
                for c in range(HC):
                    dve.wait_ge(pv_done, 3 * h + c + 1)
                    dve.tensor_tensor(hh[:, c, :], pv[c % 2][:], rd[:], ALU.mult).then_inc(pv_free, 1)
                dve.wait_ge(mu_done, h + 1)
                for c in range(HC):
                    dve.scalar_tensor_tensor(hh[:, c, :], st[:], -1.0 / HD, hh[:, c, :], ALU.mult, ALU.add)\
                        .then_inc(hc_done, 1)
                dve.wait_ge(var_done, h + 1)
                dve.tensor_scalar(cv[:, 0, :], dn[:], 1.0 / HD, EPS, ALU.mult, ALU.add).then_inc(msd_done, 1)
                dve.wait_ge(std_done, h + 1)
                one(dve.reciprocal(rs[:], rs[:]))
                newton(one, rs[:], cv[:, 0, :], cv[:, 1, :])
                for c in range(HC):
                    one(dve.tensor_tensor(hh[:, c, :], hh[:, c, :], rs[:], ALU.mult), wait=False)
                    dve.wait_ge(xs_done, 3 * h + c + 1)
                    one(dve.tensor_scalar(xcf[:, c % 2, :], xcf[:, c % 2, :], cols(V_SKIP, MC)[:, 3 * h + c, :], None,
                                          ALU.mult))
                    dve.scalar_tensor_tensor(hh[:, c, :], hh[:, c, :], cols(V_GAIN, MC)[:, 3 * h + c, :],
                                             xcf[:, c % 2, :], ALU.mult, ALU.add).then_inc(hf_done, 1)
                for c in range(HC):
                    dve.wait_ge(hfhi_done, 3 * h + c + 1)
                    dve.tensor_tensor(xc_lo[:, 3 * h + c, :], hh[:, c, :], xc_hi[:, 3 * h + c, :].bitcast(F32),
                                      ALU.subtract).then_inc(hflo_done, 1)
                assert count[0] == ML_STEPS, count

            with dve.Fori(0, KC // 2) as p:
                for k in range(2):
                    next_lo(U_YB // 2 + p, k)
                    dve.wait_ge(yl_in[k], 32 * p + 32)
                    dve.wait_ge(proj_done, O_YB + 2 * p + k + 1)
                    dve.tensor_tensor(mt[:, k, :], mm[k][:], sbl[:, k, :], ALU.mult).then_inc(proj_free, 1)
                    dve.wait_ge(proj_free, O_YB + 2 * p + k + 1)
                    dve.tensor_tensor(mt[:, k, :], mt[:, k, :], yal[:, k, :], ALU.add).then_inc(mt_done, 1)
                    dve.wait_ge(mghi_done, 2 * p + k + 1)
                    dve.tensor_tensor(mg_lo[:, 2 * p + k, :], mt[:, k, :], mg_hi[:, 2 * p + k, :].bitcast(F32),
                                      ALU.subtract).then_inc(mglo_done, 1)
            with dve.Fori(0, KC // 2) as p:
                for k in range(2):
                    next_lo(U_WO // 2 + p, k)
                    dve.wait_ge(xr_in[k], 16 * p + 16)
                    dve.wait_ge(proj_done, O_WO + 2 * p + k + 1)
                    dve.tensor_tensor(h2[:, 2 * p + k, :], mm[k][:], xres[:, k, :], ALU.add).then_inc(proj_free, 1)

            norm_scale(1)

            def tn(d, k):
                dve.wait_ge(alo_done, KC + d - 1)
                dve.scalar_tensor_tensor(xt[:, k, :], h2[:, d, :], cols(V_G2, KC)[:, d, :], rs[:],
                                         ALU.mult, ALU.mult).then_inc(xn_done, 1)

            def tlo(d, k):
                dve.wait_ge(ahi_done, KC + d + 1)
                dve.tensor_tensor(t_lo[:, d, :], xt[:, k, :], t_hi[:, d, :].bitcast(F32), ALU.subtract)\
                    .then_inc(alo_done, 1)

            tn(0, 0)
            with dve.Fori(0, KC // 2 - 1) as p:
                for k in range(2):
                    tn(2 * p + k + 1, (k + 1) % 2)
                    tlo(2 * p + k, k)
            tn(KC - 1, 1)
            tlo(KC - 2, 0)
            tlo(KC - 1, 1)
            dve.wait_ge(khi_done, 1)
            dve.tensor_tensor(key_lo[:], key_raw[:], key_hi[:].bitcast(F32), ALU.subtract).then_inc(klo_done, 1)

            def top16(one, vals, vo_, io_):
                width = vals.shape[-1]
                one(dve.max(vo_[:, 0:8], vals), apart=True)
                one(dve.max_index(io_[:, 0:8], vo_[:, 0:8], vals), wait=False)
                one(dve.match_replace(tw[:, 0:width], vo_[:, 0:8], vals, NEG_BIG), apart=True)
                one(dve.max(vo_[:, 8:16], tw[:, 0:width]), apart=True)
                one(dve.max_index(io_[:, 8:16], vo_[:, 8:16], tw[:, 0:width]), apart=True)

            def query_lo(hd):
                for k in range(2):
                    dve.wait_ge(qhi_done, 2 * hd + k + 1)
                    dve.tensor_tensor(qq_lo[:, k, :], pv[k][:], qq_hi[:, k, :].bitcast(F32), ALU.subtract)\
                        .then_inc(qlo_done, 1)

            def picks(one, hd):
                for k in range(2):
                    dve.wait_ge(sco_done, 2 * hd + k + 1)
                    carrier()
                    for tb in range(TB):
                        top16(one, sb_[k][:, tb * NKEY:(tb + 1) * NKEY], v12[:, k, tb, :], i12u[:, k, tb, :])
                    dve.tensor_copy(i12[:, k, :, :], i12u[:, k, :, :]).then_inc(sco_free, 1)
                one(dve.tensor_tensor(cand[:], v12[:, 0, :, :].unsqueeze(3).to_broadcast([P, TB, TOPK, TOPK]),
                                      v12[:, 1, :, :].unsqueeze(2).to_broadcast([P, TB, TOPK, TOPK]), ALU.add),
                    apart=True)
                for tb in range(TB):
                    top16(one, cand[:, tb, :, :].rearrange("p a b -> p (a b)"), tv[:, tb, :], pos[:, tb, :])
                dve.tensor_tensor(ge[:], tv[:], tv[:, :, 0:1].to_broadcast([P, TB, TOPK]), ALU.subtract)\
                    .then_inc(gsub_done, 1)
                one(dve.tensor_scalar(ab_u[:, 0, :, :], pos[:], 4, None, ALU.logical_shift_right), wait=False)
                one(dve.tensor_scalar(ab_u[:, 1, :, :], pos[:], 15, None, ALU.bitwise_and))
                one(dve.tensor_copy(ab[:], ab_u[:]))
                for r in range(2):
                    dve.wait_ge(sco_free, 2 * hd + 2)
                    dve.tensor_tensor(eqs[r], iota[:, 0:TOPK].unsqueeze(1).to_broadcast([P, TB * TOPK, TOPK]),
                                      ab[:, r, :, :].rearrange("p b k -> p (b k)").unsqueeze(2)
                                      .to_broadcast([P, TB * TOPK, TOPK]), ALU.is_equal).then_inc(eq_done, 1)

            def gates(one, hd):
                dve.wait_ge(gexp_done, hd + 1)
                one(dve.tensor_reduce(gz[:, 0, :], ge[:], AX_X, ALU.add))
                one(dve.reciprocal(gz[:, 1, :], gz[:, 0, :]))
                one(dve.tensor_tensor(slot[:, 0, :, hd, :], ge[:], gz[:, 1, :].unsqueeze(2)
                                      .to_broadcast([P, TB, TOPK]), ALU.mult), wait=False)
                for r in range(2):
                    dve.wait_ge(eqm_done, 2 * hd + r + 1)
                    dve.tensor_reduce(slot[:, 1 + r, :, hd, :], eqs[r].rearrange("p (b k) a -> p b k a", b=TB),
                                      AX_X, ALU.add).then_inc(slot_done, 1)

            one, count = stepper(pk_step, 0)
            query_lo(0)
            picks(one, 0)
            assert count[0] == PICK_STEPS, count
            with dve.Fori(1, PH) as hd:
                one, count = stepper(pk_step, PICK_STEPS + PK_STEPS * (hd - 1))
                query_lo(hd)
                gates(one, hd - 1)
                picks(one, hd)
                assert count[0] == PK_STEPS, count
            one, count = stepper(pk_step, PICK_STEPS + PK_STEPS * (PH - 1))
            gates(one, PH - 1)

            dve.wait_ge(trc_done, 3)
            dve.tensor_tensor(gate_lo[:], dn[:], gate_hi[:].bitcast(F32), ALU.subtract).then_inc(glo_done, 1)
            i_cols, j_cols = (slot_t[:, v, :].rearrange("p (n w) -> p n w", w=8) for v in range(2))
            g_cols = gate_hi[:].bitcast(F32).rearrange("p (n w) -> p n w", w=8)
            iota_b = iota[:].unsqueeze(1).to_broadcast([P, 8, P])
            dve.wait_ge(h2_out, 16)
            with dve.Fori(0, 32) as r:
                for b in range(2):
                    n8 = 2 * r + b
                    dve.wait_ge(hot_used, 2 * n8 + 2)
                    dve.tensor_tensor(hot_j[:, b, :, :], iota_b, j_cols[:, n8, :].unsqueeze(2).to_broadcast([P, 8, P]),
                                      ALU.is_equal).then_inc(hotj_done, 1)
                    dve.tensor_tensor(hot_i[:, b, :, :], iota_b, i_cols[:, n8, :].unsqueeze(2).to_broadcast([P, 8, P]),
                                      ALU.is_equal)
                    dve.wait_ge(hotj_done, n8 + 1)
                    dve.tensor_tensor(hot_jh[:, b, :, :], hot_j[:, b, :, :],
                                      g_cols[:, n8, :].unsqueeze(2).to_broadcast([P, 8, P]), ALU.mult)\
                        .then_inc(hoth_done, 1)

            def gate(par, jj, num):
                g3 = gl[:, jj % 2, :].rearrange("p (n t) -> p n t", n=16)
                dve.tensor_tensor(g3, g3, gg[:, par, :, :].rearrange("p n (j t) -> p n j t", j=4)[:, :, jj, :],
                                  ALU.mult).then_inc(gated_done, 1)

            def act_low(par, jj, num):
                dve.wait_ge(acthi_done, num + 1)
                dve.tensor_tensor(act_lo[:, par, jj, :], gl[:, jj % 2, :], act_hi[:, par, jj, :].bitcast(F32),
                                  ALU.subtract).then_inc(actlo_done, 1)

            def add_down(g, jj):
                for b in range(4):
                    dve.wait_ge(v_done, 16 * g + 4 * jj + b + 1)
                    dve.tensor_tensor(h2[:, 4 * jj + b, :], h2[:, 4 * jj + b, :], vo[b][:], ALU.add)\
                        .then_inc(v_free, 1)

            dve.wait_ge(lo_done, U_LAST + 1)
            for jj in range(4):
                next_lo((U_LAST + jj) // 2, jj % 2)
                if jj == 2:
                    dve.wait_ge(g_in, 16)
                    for j0 in range(4):
                        dve.wait_ge(up_in[j0 % 2], 16 * (j0 // 2) + 16)
                        gate(0, j0, j0)
                        act_low(0, j0, j0)
            dve.wait_ge(h2_in, 16)
            for k in range(2):
                dve.wait_ge(up_out[k], 16 * 2 * EARLY)
            with dve.Fori(0, EARLY - 1) as g:
                dve.wait_ge(g_in, 16 * g + 32)
                for jj in range(4):
                    m, k = U_DOWN // 2 + 2 * g + jj // 2, jj % 2
                    next_lo(m, k)
                    dve.wait_ge(up_in[k], 16 * (2 * g + jj // 2) + 48)
                    gate((g + 1) % 2, jj, 4 * g + 4 + jj)
                    act_low((g + 1) % 2, jj, 4 * g + 4 + jj)
                    add_down(g, jj)
            with dve.Fori(EARLY - 1, GROUPS_E - 1) as g:
                dve.wait_ge(g_in, 16 * g + 32)
                for jj in range(4):
                    m = U_PAIR // 2 + 4 * (g - (EARLY - 1)) + jj
                    split_lo(m, 1)
                    dve.wait_ge(proj_free, O_UP + 4 * g + jj + 5)
                    gate((g + 1) % 2, jj, 4 * g + 4 + jj)
                    split_lo(m + 1, 0)
                    act_low((g + 1) % 2, jj, 4 * g + 4 + jj)
                    add_down(g, jj)
            for jj in range(4):
                nu = N_STREAM - 4 + jj + 1
                if jj < 3:
                    split_lo(nu // 2, nu % 2)
                add_down(GROUPS_E - 1, jj)

            dve.wait_ge(v_free, 4 + 16 * GROUPS_E)
            norm_scale(2)
            with dve.Fori(0, KC // 2) as p:
                for b in range(2):
                    dve.wait_ge(fin_out[b], 16 * p)
                    dve.scalar_tensor_tensor(fin[:, b, :], h2[:, 2 * p + b, :], cols(V_GF, KC)[:, 2 * p + b, :],
                                             rs[:], ALU.mult, ALU.mult).then_inc(fin_done, 1)

        @block.tensor
        def _(pe):
            def mm3(out, lh, ll, rh, rl, start, stop):
                pe.matmul(out, lh, rh, start=start, stop=False)
                pe.matmul(out, lh, rl, start=False, stop=False)
                return pe.matmul(out, ll, rh, start=False, stop=stop)

            def w(k, c0, width=P):
                return whi[:, k, c0:c0 + width], wlo[:, k, c0:c0 + width]

            def proj(m, k, o, rh, rl, kc=KC, b=None, c0=0, wait=True):
                if wait:
                    pe.wait_ge(lo_done, 2 * m + k + 1)
                pe.wait_ge(proj_free, o - 1)
                out = mm[k if b is None else b][:]
                for d in range(kc):
                    last = mm3(out, *w(k, c0 + P * d), rh[:, d, :], rl[:, d, :], d == 0, d == kc - 1)
                last.then_inc(proj_done, 1)

            def sum_squares(r):
                for d in range(KC):
                    pe.wait_ge(sq_done, KC * r + d + 1)
                    pe.matmul(st[:], ones[:], sq[:, d % 2, :], start=(d == 0), stop=(d == KC - 1))\
                        .then_inc(ssq_done, 1)

            pe.wait_ge(const_done, 4)
            sum_squares(0)
            pe.wait_ge(lo_done, 1)
            for d in range(KC):
                pe.wait_ge(alo_done, d + 1)
                last = mm3(mm[0][:], *w(0, P * d), hn_hi[:, d, :], hn_lo[:, d, :], d == 0, d == KC - 1)
            last.then_inc(proj_done, 1)
            pe.wait_ge(lo_done, 2)
            for d in range(KC):
                last = mm3(mm[1][:], *w(1, P * d), hn_hi[:, d, :], hn_lo[:, d, :], d == 0, d == KC - 1)
            last.then_inc(proj_done, 1)
            for nu in (2, 3):
                proj(nu // 2, nu % 2, nu, hn_hi, hn_lo)
            pe.wait_ge(wif_in, 16)
            for d in range(KC):
                last = pe.matmul(pv[0][0:64, :], wif[:, d, :], x[:, d, :], start=(d == 0), stop=(d == KC - 1))
            last.then_inc(if_done, 1)
            with pe.Fori(U_XM // 2, U_GA // 2) as m:
                for k in range(2):
                    proj(m, k, 2 * m + k, hn_hi, hn_lo)

            def s5_out(c, k):
                pe.wait_ge(out_r_done, 4 * c + k + 1)
                pe.matmul(dn[32 * k:32 * k + 32, :], cc[:, 0, k, :], rout[:, 0, :], start=True, stop=False)
                pe.wait_ge(out_i_done, 4 * c + k + 1)
                pe.matmul(dn[32 * k:32 * k + 32, :], cc[:, 1, k, :], rout[:, 1, :], start=False, stop=True)\
                    .then_inc(cm_done, 1)

            with pe.Fori(0, SC) as c:
                for k in range(4):
                    m = U_GA // 2 + 4 * c + k
                    proj(m, 0, 2 * m, hn_hi, hn_lo)
                    if k:
                        s5_out(c, k - 1)
                    else:
                        pe.wait_ge(chunk_done, c + 1)
                        pe.wait_ge(bc_in, 16 * c + 16)
                        pe.wait_ge(ylo_done, c)
                    rows = slice(32 * k, 32 * k + 32)
                    pe.wait_ge(bus_done, 8 * c + 2 * k)
                    for r in range(2):
                        pe.matmul(sb_[r][:], bc[rows, r, :], uc[rows, :], start=True, stop=True).then_inc(bu_done, 1)
                    proj(m, 1, 2 * m + 1, hn_hi, hn_lo)
                s5_out(c, 3)

            pe.wait_ge(ylo_done, SC)
            pe.wait_ge(proj_free, O_GLU)
            with pe.Fori(0, 4) as q:
                for k in range(2):
                    pe.wait_ge(lo_done, U_GLU + 2 * q + k + 1)
                    for j in range(4):
                        pe.wait_ge(proj_free, O_GLU + 8 * q + 4 * k + 2 * (j // 2) - 2)
                        for d in range(SC):
                            last = mm3((mm, pv)[j // 2][j % 2][:], *w(k, 512 * j + P * d), y_hi[:, d, :], y_lo[:, d, :],
                                       d == 0, d == SC - 1)
                        last.then_inc(proj_done, 1)

            pe.wait_ge(onesr_done, 1)
            with pe.Fori(0, HEADS) as h:
                ma = U_QKV // 2 + h
                o = O_QKV + 10 * h
                pe.wait_ge(xclo_done, 3 * h + 3)
                for part, k in enumerate((0, 1)):
                    pe.wait_ge(lo_done, 2 * ma + k + 1)
                    for ob in range(HC):
                        j = 3 * part + ob
                        pe.wait_ge(proj_free, o + j - 1)
                        for d in range(HC):
                            last = mm3(mm[j % 2][:], *w(k, HD * d + P * ob), xc_hi[:, 3 * h + d, :],
                                       xc_lo[:, 3 * h + d, :], d == 0, d == HC - 1)
                        last.then_inc(proj_done, 1)
                pe.wait_ge(xmlo_done, 3 * h + 3)
                for s in range(TB):
                    j = 6 + s
                    pe.wait_ge(proj_free, o + j - 1)
                    for d in range(HC):
                        vh, vl = w(0, 3 * HD, HD) if d == 0 else w(1, (2 + d) * HD, HD)
                        ts_ = slice(P * s, P * s + P)
                        last = mm3(mm[j % 2][:, 0:HD], xm_hi[:, d, ts_], xm_lo[:, d, ts_], vh, vl, d == 0, d == HC - 1)
                    last.then_inc(proj_done, 1)

                def scores(s):
                    pe.wait_ge(pf_done, 4 * h + s - 1 if s >= 2 else 4 * h)
                    ks = slice(P * s, P * s + P)
                    for d in range(HC):
                        last = mm3(sb_[s % 2][:, 0:T - P * s], k_hi[:, d, ks], k_lo[:, d, ks],
                                   q_hi[:, d, P * s:T], q_lo[:, d, P * s:T], d == 0, d == HC - 1)
                    last.then_inc(s_done, 1)

                def den(s):
                    pe.wait_ge(plo_done, 4 * h + s + 1)
                    pe.matmul(dn[:, P * s:T], ones_r[:], p_hi[:, s, P * s:T], start=(s == 0), stop=False)
                    return pe.matmul(dn[:, P * s:T], ones_r[:], p_lo[:, s, P * s:T], start=False, stop=(s == TB - 1))

                pe.wait_ge(proj_free, o + 6)
                pe.wait_ge(msd_done, h)
                scores(0)
                scores(1)
                den(0)
                scores(2)
                den(1)
                scores(3)
                den(2)
                den(3).then_inc(den_done, 1)
                pe.wait_ge(proj_free, o + 10)
                for c in range(HC):
                    pe.wait_ge(pv_free, 3 * h + 1 if c == 2 else 3 * h)
                    cs = slice(P * c, P * c + P)
                    for s in range(TB):
                        last = mm3(pv[c % 2][:, P * s:T], v_hi[:, s, cs], v_lo[:, s, cs],
                                   p_hi[:, s, P * s:T], p_lo[:, s, P * s:T], s == 0, s == TB - 1)
                    last.then_inc(pv_done, 1)
                pe.wait_ge(hc_done, 3 * h)
                for c in range(HC):
                    pe.wait_ge(hz_done, 3 * h + c + 1)
                    last = pe.matmul(st[:], ones[:], hh[:, c, :], start=(c == 0), stop=(c == HC - 1))
                last.then_inc(mu_done, 1)
                for c in range(HC):
                    pe.wait_ge(hsq_done, 3 * h + c + 1)
                    last = pe.matmul(dn[:], ones[:], hsq[c], start=(c == 0), stop=(c == HC - 1))
                last.then_inc(var_done, 1)

            pe.wait_ge(hflo_done, MC)
            with pe.Fori(0, KC // 2) as p:
                for k in range(2):
                    proj(U_YB // 2 + p, k, O_YB + 2 * p + k, xc_hi, xc_lo, MC)
            pe.wait_ge(mglo_done, KC)
            with pe.Fori(0, KC // 2) as p:
                for k in range(2):
                    proj(U_WO // 2 + p, k, O_WO + 2 * p + k, mg_hi, mg_lo)

            sum_squares(1)
            pe.wait_ge(alo_done, 2 * KC)
            pe.wait_ge(klo_done, 1)
            with pe.Fori(0, PH) as hd:
                m = U_HEAD // 2 + 3 * hd
                for k in range(2):
                    pe.wait_ge(lo_done, 2 * m + k + 1)
                    pe.wait_ge(qlo_done, 2 * hd)
                    for d in range(KC):
                        last = mm3(pv[k][:], *w(k, P * d), t_hi[:, d, :], t_lo[:, d, :], d == 0, d == KC - 1)
                    last.then_inc(qp_done, 1)
                proj(m + 1, 0, O_UP + 4 * hd, t_hi, t_lo)
                for k in range(2):
                    pe.wait_ge(qlo_done, 2 * hd + k + 1)
                    pe.wait_ge(sco_free, 2 * hd)
                    for tb in range(TB):
                        ts_ = slice(P * tb, P * tb + P)
                        last = mm3(sb_[k][:, ts_], qq_hi[:, k, ts_], qq_lo[:, k, ts_],
                                   key_hi[:, hd, k, :], key_lo[:, hd, k, :], True, True)
                    last.then_inc(sco_done, 1)
                for jj in (1, 2, 3):
                    proj(m + 1 + jj // 2, jj % 2, O_UP + 4 * hd + jj, t_hi, t_lo)
            for jj in range(4):
                if jj == 3:
                    pe.wait_ge(slot_done, 2 * PH)
                    pe.wait_ge(qlo_done, 2 * PH)
                    for v in range(3):
                        for tb in range(TB):
                            last = pe.transpose((dn, pv[0], pv[1])[v][:, P * tb:P * tb + P],
                                                slot[:, v, tb, :, :].rearrange("p h k -> p (h k)"), ident[:])
                        last.then_inc(tr_done, 1)
                proj((U_FILL + jj) // 2, jj % 2, O_UP + N_FILL + jj, t_hi, t_lo)

            pe.sem_inc(hot_used, 4)
            with pe.Fori(0, 16) as r:
                for s in range(2):
                    m, n = U_GATE // 2 + r, 2 * r + s
                    pe.wait_ge(lo_done, 2 * m + s + 1)
                    pe.wait_ge(proj_free, O_UP + N_GATE + n - 1)
                    for q in range(2):
                        for d in range(8 * q, 8 * q + 8):
                            last = mm3(mm[s][:], *w(s, P * d), t_hi[:, d, :], t_lo[:, d, :], d == 0, d == KC - 1)
                        if q == 1:
                            last.then_inc(proj_done, 1)
                        pe.wait_ge(hoth_done, 2 * n + q + 1)
                        pe.wait_ge(hotl_done, 2 * n + q + 1)
                        for v in range(8):
                            b = 2 * q + v // 4
                            if v % 4 == 0:
                                pe.wait_ge(gps_free, 4 * n + b + 1)
                            o = vo[b % 4][:, P * (v % 4):P * (v % 4) + P]
                            pe.matmul(o, hot_i[:, q, v, :], hot_jh[:, q, v, :], start=True, stop=False)
                            last = pe.matmul(o, hot_i[:, q, v, :], hot_jl[:, q, v, :], start=False, stop=True)
                            if v % 4 == 3:
                                last.then_inc(hot_used, 1)
            for jj in range(4):
                proj((U_LAST + jj) // 2, jj % 2, O_UP + N_LAST + jj, t_hi, t_lo)

            def down(k, g, par, m, v0):
                pe.wait_ge(lo_done, 2 * m + k + 1)
                pe.wait_ge(actlo_done, 4 * g + 4)
                for b in range(4):
                    pe.wait_ge(v_free, v0 + b + 1)
                    for jj in range(4):
                        last = mm3(vo[b][:], *w(k, 512 * jj + P * b), act_hi[:, par, jj, :],
                                   act_lo[:, par, jj, :], jj == 0, jj == 3)
                    last.then_inc(v_done, 1)

            pe.wait_ge(gps_free, 4 + 128)
            pe.sem_inc(v_free, 4)
            with pe.Fori(0, EARLY - 1) as g:
                for jj in range(4):
                    down(jj % 2, g, g % 2, U_DOWN // 2 + 2 * g + jj // 2, 16 * g + 4 * jj)
            with pe.Fori(EARLY - 1, GROUPS_E - 1) as g:
                for jj in range(4):
                    m = U_PAIR // 2 + 4 * (g - (EARLY - 1)) + jj
                    proj(m, 0, O_UP + 4 * (g + 1) + jj, t_hi, t_lo, b=jj % 2)
                    down(1, g, g % 2, m, 16 * g + 4 * jj)
            for jj in range(4):
                nu = N_STREAM - 4 + jj
                down(nu % 2, GROUPS_E - 1, (GROUPS_E - 1) % 2, nu // 2, 16 * (GROUPS_E - 1) + 4 * jj)

            sum_squares(2)

def _blocks(w):
    din, f = w.shape
    return w.reshape(din // P, P, f // P, P).transpose(2, 1, 0, 3).reshape(f // P, P, din)


def _stream(i):
    s = np.zeros((N_STREAM, P, UNIT), np.float32)
    w_in = i["w_in"][0]
    z1 = SSM_W + 2 * ML_W
    ga = z1 + 2 * HEADS
    s[U_SSM:U_GA] = _blocks(w_in[:, 0:z1])
    s[U_GA:U_GLU] = _blocks(w_in[:, ga:])
    g = i["w_glu"][0].reshape(SC, P, 2, 8, 2, P).transpose(3, 1, 4, 2, 0, 5)
    s[U_GLU:U_QKV] = g.reshape(8, P, UNIT)
    for h in range(HEADS):
        q, k, v = (i[n][0, h].reshape(HC, P, HD).transpose(1, 0, 2) for n in ("w_q", "w_k", "w_v"))
        a, b = s[U_QKV + 2 * h], s[U_QKV + 2 * h + 1]
        a[:, 0:3 * HD], a[:, 3 * HD:4 * HD] = q.reshape(P, -1), v[:, 0]
        b[:, 0:3 * HD], b[:, 3 * HD:5 * HD] = k.reshape(P, -1), v[:, 1:3].reshape(P, -1)
    s[U_YB:U_WO, :, 0:ML_W] = _blocks(i["w_mlstm_out"][0])
    s[U_WO:U_HEAD] = _blocks(i["w_out"][0])
    up = i["expert_u"][0].reshape(P, P, KC, P).transpose(1, 3, 2, 0).reshape(P, P, UNIT)
    down = i["expert_v"][0].reshape(P, GROUPS_E, 4, 4, 512).transpose(1, 3, 0, 2, 4).reshape(4 * GROUPS_E, P, UNIT)
    heads = s[U_HEAD:U_FILL].reshape(PH, 6, P, UNIT)
    heads[:, 0:2] = _blocks(i["w_query"][0]).reshape(PH, 2, P, UNIT)
    heads[:, 2:6] = up[0:N_FILL].reshape(PH, 4, P, UNIT)
    s[U_FILL:U_DOWN] = up[N_FILL:4 * EARLY]
    s[U_DOWN:U_PAIR] = down[0:4 * (EARLY - 1)]
    s[U_PAIR:N_STREAM - 4:2] = up[4 * EARLY:]
    s[U_PAIR + 1:N_STREAM - 4:2] = down[4 * (EARLY - 1):-4]
    s[N_STREAM - 4:] = down[-4:]
    return s


def _vectors(i):
    v = np.zeros((P, N_VEC), np.float32)

    def put(at, x):
        x = x.reshape(-1, P).T
        v[:, at:at + x.shape[1]] = x

    put(V_G1, i["norm1_g"][0])
    put(V_G2, i["norm2_g"][0])
    put(V_GF, i["norm_f_g"])
    put(V_DSKIP, i["d_skip"][0])
    put(V_CW, i["conv_w"][0])
    put(V_CB, i["conv_b"][0])
    put(V_GAIN, i["mh_gain"][0])
    put(V_SKIP, i["mlstm_skip"][0])
    put(V_LRE, i["lam_re"][0])
    put(V_LIM, i["lam_im"][0])
    put(V_LDT, np.repeat(i["log_dt"][0], STATE))
    v[0:HEADS, V_BI] = i["b_i"][0]
    v[32:32 + HEADS, V_BF] = i["b_f"][0]
    return v


def _s5_tables(i):
    b_tab = np.zeros((SC + 1, P, 2, P), np.float32)
    c_tab = np.zeros((P, 2, 16, 32), np.float32)
    for g in range(GROUPS):
        c, k, half = g // 8, g // 2 % 4, g % 2
        ch, st = 32 * k + GROUP * half, STATE * half
        for r, (b, cm) in enumerate((("b_re", "c_re"), ("b_im", "c_im"))):
            b_tab[c, ch:ch + GROUP, r, st:st + STATE] = i[b][0, g].T
            c_tab[st:st + STATE, r, g // 2, GROUP * half:GROUP * half + GROUP] = i[cm][0, g].T
    return b_tab, c_tab


def kernel(**inputs):
    import concourse.bacc as _bacc
    from concourse.bass_utils import run_bass_kernel_spmd as _run

    i = {k: np.asarray(v) for k, v in inputs.items()}
    w_in = i["w_in"][0]
    z1 = SSM_W + 2 * ML_W
    wif = np.zeros((P, KC, 64), np.float32)
    wif[:, :, 0:HEADS] = w_in[:, z1:z1 + HEADS].reshape(KC, P, HEADS).transpose(1, 0, 2)
    wif[:, :, 32:32 + HEADS] = w_in[:, z1 + HEADS:z1 + 2 * HEADS].reshape(KC, P, HEADS).transpose(1, 0, 2)
    b_tab, c_tab = _s5_tables(i)
    keys = np.stack([i["key1"][0], i["key2"][0]], 1)
    arrays = {
        "xT": np.ascontiguousarray(i["x"][0].reshape(T, KC, P).transpose(2, 1, 0)),
        "stream": _stream(i), "vecs": _vectors(i), "wif": wif, "b_tab": b_tab, "c_tab": c_tab,
        "keys": np.ascontiguousarray(keys.transpose(3, 0, 1, 2)),
    }
    nc = _bacc.Bacc("TRN2", target_bir_lowering=False, num_devices=1)
    args = {n: nc.dram_tensor(n, v.shape, F32, kind="ExternalInput").ap() for n, v in arrays.items()}
    out = nc.dram_tensor("out", (P, KC, T), F32, kind="ExternalOutput").ap()
    build(nc, args, out)
    r = _run(nc, [arrays], core_ids=[0])
    y = r.results[0]["out"]
    return np.ascontiguousarray(y.transpose(2, 1, 0)).reshape(1, T, D)
```

```python
from contextlib import ExitStack

import numpy as np

import concourse.bass as bass
from concourse import mybir

ALU = mybir.AluOpType
ACT = mybir.ActivationFunctionType
AX_X = mybir.AxisListType.X
F32 = mybir.dt.float32
F32R = mybir.dt.float32r
I32 = mybir.dt.int32
U32 = mybir.dt.uint32

P = 128
T = 512
D = 2048
KC = D // P
SSM_W, ML_W, HEADS, HD = 512, 1536, 4, 384
SC, MC, HC = SSM_W // P, ML_W // P, HD // P
TB = T // P
STATE, GROUP, GROUPS = 64, 16, 32
PH, NKEY, TOPK = 8, 128, 16
EPS = 1e-6
UNIT = 2048

U_SSM, U_XM, U_Z, U_GA, U_GB = 0, 4, 16, 28, 44
U_GLU, U_QKV, U_YB, U_WO = 60, 68, 76, 92
U_HEAD = 108
U_FILL = U_HEAD + 6 * PH
U_GATE = U_FILL + 4
U_LAST = U_GATE + 32
U_DOWN = U_LAST + 4
GROUPS_E = 32
N_FILL, N_GATE, N_LAST = 4 * PH, 4 * PH + 4, 4 * PH + 36
EARLY = (N_LAST + 4) // 4
U_PAIR = U_DOWN + 4 * (EARLY - 1)
N_STREAM = U_PAIR + 8 * (GROUPS_E - EARLY) + 4
O_GLU, O_QKV, O_YB, O_WO, O_UP = 60, 92, 132, 148, 164

V_G1, V_G2, V_GF, V_DSKIP, V_CW, V_CB, V_GAIN, V_SKIP = 0, 16, 32, 48, 52, 100, 112, 124
V_LRE, V_LIM, V_LDT, V_BI, V_BF, N_VEC = 136, 152, 168, 184, 185, 186

LOG2E, LN2_HI, LN2_LO = 1.4426950408889634, 0.693359375, -2.12194440e-4
ROUND = 12582912.0
HALF_PI = (1.5703125, 4.837512969970703125e-4, 7.54978995489188216e-8)
NEG_BIG = -3.0e38
S5_STEPS, ML_STEPS, PK_STEPS, PICK_STEPS = 164, 26, 67, 64


def build(nc, a, out_d):
    ctx = ExitStack()
    with ctx:
        base = (nc.sbuf_base + 63) // 64 * 64
        room = nc.sbuf_usable_end - base

        def S(name, shape, dt, kb):
            size = 4 * int(np.prod(shape[1:]))
            assert kb * 1024 + size <= room, (name, kb * 1024 + size, room)
            return nc.alloc_sbuf_tensor_at(name, shape, dt, offset=base + int(kb * 1024))

        def sem(name):
            return ctx.enter_context(nc.semaphore(name))

        raw = S("raw", [P, 2, UNIT], F32, 0)
        whi = S("whi", [P, 2, UNIT], F32R, 16)
        wlo = S("wlo", [P, 2, UNIT], F32R, 32)
        vec = S("vec", [P, N_VEC], F32, 202)
        ones = S("ones", [P, P], F32, 202.75)
        ones_r = S("ones_r", [P, P], F32R, 203.25)
        ident = S("ident", [P, P], F32, 203.75)
        tri = S("tri", [P, P], F32, 204.25)
        iota = S("iota", [P, P], F32, 204.75)
        rs = S("rs", [P, T], F32, 205.25)
        sq = S("sq", [P, 2, T], F32, 176)
        ms = S("ms", [P, T], F32, 180)
        nt = S("nt", [P, T], F32, 182)
        xt = S("xt", [P, 2, T], F32, 184)
        sqf = S("sqf", [P, 2, T], F32, 100)
        sq_sum = S("sq_sum", [P, T], F32, 200)
        hn_hi = S("hn_hi", [P, KC, T], F32R, 48)
        hn_lo = S("hn_lo", [P, KC, T], F32R, 80)
        x = S("x", [P, KC, T], F32, 112)
        uT = S("uT", [P, SC, T], F32, 144)
        stage = S("stage", [P, 2, T], F32, 152)
        cp = S("cp", [P, 2, 16, 32], F32, 156)
        craw = S("craw", [P, 2, 16, 32], F32, 160)
        wif = S("wif", [P, KC, 64], F32, 164)
        bc = S("bc", [P, 2, P], F32, 168)
        cc = S("cc", [P, 2, 4, 32], F32, 169)
        pc = S("pc", [P, 2, 9, 4], F32, 170)
        rc = S("rc", [P, 8], F32, 170.5)
        cw = S("cw", [P, 40, 16], F32, 171)
        ptab = S("ptab", [P, 2, 9, 16], F32, 174)
        gt = S("gt", [P, 4, T], F32, 184)
        gout = S("gout", [P, 3, T], F32, 192)
        tab = S("tab", [P, 2, 2, T], F32, 112)
        bus = S("bus", [P, 2, T], F32, 120)
        rin = S("rin", [P, 2, T], F32, 124)
        wst = S("wst", [P, 2, T], F32, 128)
        rout = S("rout", [P, 2, T], F32, 132)
        dtmp = S("dtmp", [P, 2, T], F32, 136)
        ptmp = S("ptmp", [P, 2, T], F32, 140)
        uc = S("uc", [P, T], F32, 198)
        y_hi = S("y_hi", [P, SC, T], F32R, 176)
        y_lo = S("y_lo", [P, SC, T], F32R, 184)
        sgt = S("sgt", [P, 2, T], F32, 112)
        vt = S("vt", [P, 2, T], F32, 116)
        sa = S("sa", [P, 2, T], F32, 132)
        xc_hi = S("xc_hi", [P, MC, T], F32R, 48)
        xc_lo = S("xc_lo", [P, MC, T], F32R, 72)
        q_hi = S("q_hi", [P, HC, T], F32R, 96)
        q_lo = S("q_lo", [P, HC, T], F32R, 102)
        k_hi = S("k_hi", [P, HC, T], F32R, 108)
        k_lo = S("k_lo", [P, HC, T], F32R, 114)
        v_hi = S("v_hi", [P, TB, HD], F32R, 120)
        v_lo = S("v_lo", [P, TB, HD], F32R, 126)
        p_hi = S("p_hi", [P, TB, T], F32R, 132)
        p_lo = S("p_lo", [P, TB, T], F32R, 140)
        m_bc = S("m_bc", [P, T], F32, 148)
        em_bc = S("em_bc", [P, T], F32, 150)
        xmr = S("xmr", [P, HC, T], F32, 152)
        sz = S("sz", [P, HC, T], F32, 158)
        cv = S("cv", [P, 2, T], F32, 164)
        xcf = S("xcf", [P, 2, T], F32, 168)
        pf = S("pf", [P, 2, T], F32, 172)
        xm_hi = S("xm_hi", [P, HC, T], F32R, 176)
        xm_lo = S("xm_lo", [P, HC, T], F32R, 182)
        ex = S("ex", [P, 2, T], F32, 188)
        hh = S("hh", [P, HC, T], F32, 192)
        rd = S("rd", [P, T], F32, 198)
        gcol = S("gcol", [P, TB], F32, 200)
        mg_hi = S("mg_hi", [P, KC, T], F32R, 96)
        mg_lo = S("mg_lo", [P, KC, T], F32R, 128)
        yal = S("yal", [P, 2, T], F32, 160)
        sbl = S("sbl", [P, 2, T], F32, 164)
        mt = S("mt", [P, 2, T], F32, 168)
        xres = S("xres", [P, 2, T], F32, 172)
        h2 = S("h2", [P, KC, T], F32, 48)
        t_hi = S("t_hi", [P, KC, T], F32R, 96)
        t_lo = S("t_lo", [P, KC, T], F32R, 128)
        key_hi = S("key_hi", [P, PH, 2, NKEY], F32R, 160)
        key_lo = S("key_lo", [P, PH, 2, NKEY], F32R, 168)
        key_raw = S("key_raw", [P, PH, 2, NKEY], F32, 188)
        qq_hi = S("qq_hi", [P, 2, T], F32R, 80)
        qq_lo = S("qq_lo", [P, 2, T], F32R, 84)
        tw = S("tw", [P, 256], F32, 196)
        v12 = S("v12", [P, 2, TB, TOPK], F32, 197)
        i12u = S("i12u", [P, 2, TB, TOPK], U32, 197.5)
        i12 = S("i12", [P, 2, TB, TOPK], F32, 198)
        cand = S("cand", [P, TB, TOPK, TOPK], F32, 88)
        eq = S("eq", [P, TB * TOPK, TOPK], F32, 92)
        tv = S("tv", [P, TB, TOPK], F32, 198.5)
        pos = S("pos", [P, TB, TOPK], U32, 198.75)
        ab_u = S("ab_u", [P, 2, TB, TOPK], U32, 199)
        ab = S("ab", [P, 2, TB, TOPK], F32, 199.5)
        ge = S("ge", [P, TB, TOPK], F32, 200)
        gz = S("gz", [P, 2, TB], F32, 200.25)
        slot = S("slot", [P, 3, TB, PH, TOPK], F32, 176)
        sgl = S("sgl", [P, 2, T], F32, 192)
        slot_t = S("slot_t", [P, 2, T], F32, 82)
        gate_hi = S("gate_hi", [P, T], F32R, 80)
        gate_lo = S("gate_lo", [P, T], F32, 86)
        hot_i = S("hot_i", [P, 2, 8, P], F32R, 48)
        hot_j = S("hot_j", [P, 2, 8, P], F32, 56)
        hot_jg = S("hot_jg", [P, 2, 8, 2, P], F32R, 64)
        gst = S("gst", [P, 2, P, 32], F32, 160)
        gl = S("gl", [P, 2, T], F32, 196)
        gg = S("gg", [P, 2, 16, P], F32, 80)
        act_hi = S("act_hi", [P, 2, 4, T], F32R, 160)
        act_lo = S("act_lo", [P, 2, 4, T], F32R, 176)
        fin = S("fin", [P, KC, T], F32, 104)

        def bank(name):
            return ctx.enter_context(nc.psum_tensor(name, [P, T], F32))

        mm = [bank("mm0"), bank("mm1")]
        sb_ = [bank("sc0"), bank("sc1")]
        dn, st = bank("dn"), bank("st")
        pv = [bank("pv0"), bank("pv1")]
        heads_out = [pv[0], pv[1], st]
        bank_parts = [b[:].rearrange("p (t a j) -> p t a j", t=2, a=2) for b in (pv[0], pv[1], sb_[0], sb_[1])]
        vo = [pv[0], pv[1], sb_[0], sb_[1]]

        hsq = (ex[:, 0, :], ex[:, 1, :], pf[:, 0, :])
        eqs = (eq[:], cand[:].rearrange("p b k a -> p (b k) a"))

        spill = nc.dram_tensor("spill", (56, P, T), F32).ap()
        ya_d = nc.dram_tensor("ya_d", (KC, P, T), F32).ap()
        gates_d = nc.dram_tensor("gates_d", (3, HEADS, T), F32).ap()
        h2_d = nc.dram_tensor("h2_d", (P, KC, T), F32).ap()
        up_d = nc.dram_tensor("up_d", (4 * EARLY, P, T), F32).ap()
        g_d = nc.dram_tensor("g_d", (16, P, P, 32), F32).ap()

        raw_in = [sem("raw_in0"), sem("raw_in1")]
        hi_done, lo_done = sem("hi_done"), sem("lo_done")
        proj_done, proj_free = sem("proj_done"), sem("proj_free")
        vec_in, x_in = sem("vec_in"), [sem(f"x_in{i}") for i in range(4)]
        wif_in, craw_in = sem("wif_in"), sem("craw_in")
        const_done, onesr_done = sem("const_done"), sem("onesr_done")
        sq_done, qsum_done, ssq_done, ln_done, rt_done = sem("sq_done"), sem("qsum_done"), sem("ssq_done"), sem("ln_done"), sem("rt_done")
        xn_done, ahi_done = sem("xn_done"), sem("ahi_done")
        alo_done = [sem("alo_done0"), sem("alo_done1")]
        stage_out = [sem("stage_out0"), sem("stage_out1")]
        if_done, ge_sem, gates_done, gates_out = sem("if_done"), sem("ge_sem"), sem("gates_done"), sem("gates_out")
        coef_done, chunk_done, bc_in = sem("coef_done"), sem("chunk_done"), sem("bc_in")
        bu_done, bus_done, tab_done, rot_done = sem("bu_done"), sem("bus_done"), sem("tab_done"), sem("rot_done")
        prot_done, scan_done, out_r_done, out_i_done = sem("prot_done"), sem("scan_done"), sem("out_r_done"), sem("out_i_done")
        cm_done, yp_done, yg_done, yhi_done, ylo_done = sem("cm_done"), sem("yp_done"), sem("yg_done"), sem("yhi_done"), sem("ylo_done")
        sg_done, ya_done = sem("sg_done"), sem("ya_done")
        sa_in, ya_out = [sem("sa_in0"), sem("sa_in1")], [sem("ya_out0"), sem("ya_out1")]
        xm_in, sz_in, bcst_in = sem("xm_in"), sem("sz_in"), sem("bcst_in")
        cv_done, silu_done, xchi_done, xclo_done = sem("cv_done"), sem("silu_done"), sem("xchi_done"), sem("xclo_done")
        xmhi_done, xmlo_done = sem("xmhi_done"), sem("xmlo_done")
        qkv_hi_done = sem("qkv_hi_done")
        s_done, en_done, ex_done = sem("s_done"), sem("en_done"), sem("ex_done")
        pf_done, phi_done, plo_done = sem("pf_done"), sem("phi_done"), sem("plo_done")
        den_done, pv_done, pv_free, hz_done = sem("den_done"), sem("pv_done"), sem("pv_free"), sem("hz_done")
        mu_done, hc_done, hsq_done, var_done = sem("mu_done"), sem("hc_done"), sem("hsq_done"), sem("var_done")
        vln_done, std_done, xs_done, hf_done, hfhi_done, hflo_done = sem("vln_done"), sem("std_done"), sem("xs_done"), sem("hf_done"), sem("hfhi_done"), sem("hflo_done")
        yl_in = [sem("yl_in0"), sem("yl_in1")]
        mt_done, mghi_done, mglo_done = sem("mt_done"), sem("mghi_done"), sem("mglo_done")
        xr_in = [sem("xr_in0"), sem("xr_in1")]
        key_in, khi_done, klo_done = sem("key_in"), sem("khi_done"), sem("klo_done")
        qp_done, qhi_done, qlo_done = sem("qp_done"), sem("qhi_done"), sem("qlo_done")
        sco_done, sco_free = sem("sco_done"), sem("sco_free")
        gsub_done, gexp_done, eqm_done, slot_done = sem("gsub_done"), sem("gexp_done"), sem("eqm_done"), sem("slot_done")
        eq_done = sem("eq_done")
        tr_done, trc_done = sem("tr_done"), sem("trc_done")
        glo_done, hotj_done, hoth_done, hotl_done = sem("glo_done"), sem("hotj_done"), sem("hoth_done"), sem("hotl_done")
        hot_used, gcopy_done, gps_free = sem("hot_used"), sem("gcopy_done"), sem("gps_free")
        gst_out = [sem("gst_out0"), sem("gst_out1")]
        up_out, up_in = [sem("up_out0"), sem("up_out1")], [sem("up_in0"), sem("up_in1")]
        h2_out, h2_in, g_in = sem("h2_out"), sem("h2_in"), sem("g_in")
        gated_done, acthi_done, actlo_done = sem("gated_done"), sem("acthi_done"), sem("actlo_done")
        v_done, v_free = sem("v_done"), sem("v_free")
        fin_done, fin_out = sem("fin_done"), sem("fin_out")
        dve_step, pool_step = sem("dve_step"), sem("pool_step")
        s5_step, ml_step, pk_step = sem("s5_step"), sem("ml_step"), sem("pk_step")
        waited = sem("waited")
        ms_done, msd_done = sem("ms_done"), sem("msd_done")

        block = ctx.enter_context(nc.Block())

        @block.sync
        def _(sp):
            for i in range(4):
                sp.dma_start(x[:, 4 * i:4 * i + 4, :], a["xT"][:, 4 * i:4 * i + 4, :]).then_inc(x_in[i], 16)
            for k in range(2):
                sp.dma_start(raw[:, k, :], a["stream"][k]).then_inc(raw_in[k], 16)
            with sp.Fori(1, N_STREAM // 2) as m:
                for k in range(2):
                    sp.wait_ge(hi_done, 2 * m + k - 1)
                    sp.wait_ge(lo_done, 2 * m + k - 1)
                    sp.dma_start(raw[:, k, :], a["stream"][2 * m + k]).then_inc(raw_in[k], 16)
            for q in range(4):
                sp.wait_ge(fin_done, 4 * q + 4)
                sp.dma_start(out_d[:, 4 * q:4 * q + 4, :], fin[:, 4 * q:4 * q + 4, :]).then_inc(fin_out, 16)
            sp.wait_ge(fin_out, 16 * 4)

        @block.gpsimd
        def _(pool):
            n = [0]

            def step(ins):
                n[0] += 1
                ins.then_inc(pool_step, 1)
                pool.wait_ge(pool_step, n[0])

            pool.dma_start(vec[:], a["vecs"]).then_inc(vec_in, 16)
            pool.memset(ones[:], 1.0).then_inc(const_done, 1)
            pool.dma_start(wif[:], a["wif"]).then_inc(wif_in, 16)
            pool.dma_start(craw[:], a["c_tab"]).then_inc(craw_in, 16)
            pool.dma_start(bc[:], a["b_tab"][0]).then_inc(bc_in, 16)
            step(pool.memset(ident[:], 0.0))
            step(pool.memset(tri[:], 1.0))
            pool.affine_select(out=ident[:], in_=ident[:], compare_op=ALU.not_equal, fill=1.0, base=0,
                               pattern=[[-1, P]], channel_multiplier=1).then_inc(const_done, 1)
            pool.affine_select(out=tri[:], in_=tri[:], compare_op=ALU.is_ge, fill=0.0, base=0,
                               pattern=[[1, P]], channel_multiplier=-1).then_inc(const_done, 1)
            pool.iota(iota[:], [[1, P]], base=0, channel_multiplier=0,
                      allow_small_or_imprecise_dtypes=True).then_inc(const_done, 1)

            with pool.Fori(0, KC // 2) as p:
                pool.wait_ge(ahi_done, 2 * p + 2)
                pool.tensor_tensor(hn_lo[:, 2 * p + 1, :], x[:, 2 * p + 1, :], hn_hi[:, 2 * p + 1, :].bitcast(F32),
                                   ALU.subtract).then_inc(alo_done[1], 1)

            pool.wait_ge(gates_done, 1)
            pool.dma_start(gates_d.rearrange("g h t -> h g t"), gout[0:HEADS, :, :]).then_inc(gates_out, 16)

            pool.wait_ge(coef_done, 1)
            pool.wait_ge(proj_free, SC)
            with pool.Fori(0, SC) as c:
                pool.wait_ge(cm_done, 4 * c)
                pool.wait_ge(ylo_done, c)
                pool.tensor_copy(uc[:], uT[:, c, :])
                for r in range(2):
                    pool.tensor_copy(cc[:, r, :, :], cp[:, r, :, :].rearrange("p (c k) h -> p c k h", c=4)[:, c, :, :])
                    pool.tensor_copy(pc[:, r, :, :],
                                     ptab[:, r, :, :].rearrange("p n (c k) -> p c n k", c=4)[:, c, :, :])
                pool.tensor_copy(rc[:, 0:4], cw[:, 0, :].rearrange("p (c k) -> p c k", c=4)[:, c, :])
                pool.tensor_copy(rc[:, 4:5], vec[:, V_DSKIP:V_DSKIP + SC].rearrange("p (c k) -> p c k", k=1)[:, c, :])\
                    .then_inc(chunk_done, 1)
                for k in range(4):
                    pool.wait_ge(bus_done, 8 * c + 2 * k + 2)
                    pool.wait_ge(tab_done, 4 * c + k + 1)
                    pool.tensor_tensor(ptmp[:, 0, :], bus[:, 1, :], tab[:, k % 2, 0, :], ALU.mult).then_inc(pool_step, 1)
                    pool.tensor_tensor(ptmp[:, 1, :], bus[:, 0, :], tab[:, k % 2, 1, :], ALU.mult).then_inc(pool_step, 1)
                    pool.wait_ge(pool_step, 2 + 16 * c + 4 * k + 2)
                    pool.wait_ge(scan_done, 8 * c + 2 * k)
                    pool.tensor_tensor(rin[:, 1, :], ptmp[:, 0, :], ptmp[:, 1, :], ALU.subtract).then_inc(prot_done, 1)
                    pool.wait_ge(prot_done, 4 * c + k + 1)
                    pool.wait_ge(scan_done, 8 * c + 2 * k + 2)
                    pool.tensor_tensor(ptmp[:, 0, :], wst[:, 0, :], tab[:, k % 2, 1, :], ALU.mult).then_inc(pool_step, 1)
                    pool.tensor_tensor(ptmp[:, 1, :], wst[:, 1, :], tab[:, k % 2, 0, :], ALU.mult).then_inc(pool_step, 1)
                    pool.wait_ge(pool_step, 2 + 16 * c + 4 * k + 4)
                    pool.wait_ge(cm_done, 4 * c + k)
                    pool.tensor_tensor(rout[:, 1, :], ptmp[:, 0, :], ptmp[:, 1, :], ALU.add).then_inc(out_i_done, 1)
                pool.wait_ge(bu_done, 8 * c + 8)
                pool.dma_start(bc[:], a["b_tab"][c + 1]).then_inc(bc_in, 16)

            pool.wait_ge(cm_done, 16)
            pool.wait_ge(chunk_done, SC)
            for b in range(2):
                pool.wait_ge(stage_out[b], 16 * 28)
            xm_heads, z_heads = (spill[i:i + MC].rearrange("(h c) p t -> h p c t", c=HC) for i in (0, MC))
            pool.dma_start(xmr[:], xm_heads[0]).then_inc(xm_in, 16)
            for b in range(2):
                pool.dma_start(sa[:, b, :], spill[U_GA - U_XM + b]).then_inc(sa_in[b], 16)

            def conv_lo(h, c):
                pool.wait_ge(xchi_done, 3 * h + c + 1)
                pool.tensor_tensor(xc_lo[:, 3 * h + c, :], xcf[:, c % 2, :],
                                   xc_hi[:, 3 * h + c, :].bitcast(F32), ALU.subtract).then_inc(xclo_done, 1)

            for c in range(HC):
                conv_lo(0, c)


            def glu_block(p, b):
                pool.wait_ge(proj_free, O_GLU + 4 * p + 2 * b + 2)
                pool.wait_ge(sa_in[b], 16 * p + 16)
                pool.tensor_tensor(vt[:, b, :], vt[:, b, :], sa[:, b, :], ALU.mult).then_inc(ya_done, 1)
                pool.wait_ge(ya_done, 2 * p + b + 1)
                pool.dma_start(ya_d[2 * p + b], vt[:, b, :]).then_inc(ya_out[b], 16)

            with pool.Fori(0, KC // 2 - 1) as p:
                for b in range(2):
                    glu_block(p, b)
                    pool.dma_start(sa[:, b, :], spill[U_GA - U_XM + 2 * p + b + 2]).then_inc(sa_in[b], 16)
            for b in range(2):
                glu_block(KC // 2 - 1, b)
            for b in range(2):
                pool.wait_ge(ya_out[b], 16 * 8)

            def z_gate(h):
                pool.wait_ge(sz_in, 16 * h + 16)
                for c in range(HC):
                    pool.wait_ge(pv_free, 3 * h + c + 1)
                    pool.tensor_tensor(hh[:, c, :], hh[:, c, :], sz[:, c, :], ALU.mult).then_inc(hz_done, 1)

            def skips(h, blocks):
                for c in blocks:
                    if c >= 2:
                        pool.wait_ge(hf_done, 3 * h + c - 1)
                    pool.tensor_tensor(xcf[:, c % 2, :], xc_hi[:, 3 * h + c, :].bitcast(F32),
                                       xc_lo[:, 3 * h + c, :].bitcast(F32), ALU.add).then_inc(xs_done, 1)

            def key_unit_lo(h):
                m = U_QKV // 2 + h
                pool.wait_ge(lo_done, 2 * m + 1)
                pool.wait_ge(hi_done, 2 * m + 2)
                pool.tensor_tensor(wlo[:, 1, :], raw[:, 1, :], whi[:, 1, :].bitcast(F32), ALU.subtract)\
                    .then_inc(lo_done, 1)

            def xm_low(h):
                for c in range(HC):
                    pool.wait_ge(xmhi_done, 3 * h + c + 1)
                    pool.tensor_tensor(xm_lo[:, c, :], xmr[:, c, :], xm_hi[:, c, :].bitcast(F32), ALU.subtract)\
                        .then_inc(xmlo_done, 1)

            def next_xm(h):
                pool.wait_ge(cv_done, 3 * h + 3)
                pool.wait_ge(xmlo_done, 3 * h + 3)
                pool.dma_start(xmr[:], xm_heads[h + 1]).then_inc(xm_in, 16)

            def head(h, first, last, before_last):
                if not first:
                    z_gate(h - 1)
                pool.wait_ge(en_done, 4 * h)
                pool.wait_ge(pv_free, 3 * h)
                pool.dma_start(m_bc[:], gates_d[1, h].partition_broadcast(P)).then_inc(bcst_in, 16)
                pool.dma_start(em_bc[:], gates_d[2, h].partition_broadcast(P)).then_inc(bcst_in, 16)
                with nc.allow_non_contiguous_dma(reason="one value a partition"):
                    pool.dma_start(gcol[:], gates_d[0, h].rearrange("(s p) -> p s", p=P)).then_inc(bcst_in, 16)
                pool.wait_ge(hz_done, 3 * h)
                pool.dma_start(sz[:], z_heads[h]).then_inc(sz_in, 16)
                if not last:
                    for c in range(HC):
                        conv_lo(h + 1, c)
                if not first:
                    pool.wait_ge(xclo_done, 3 * h + (3 if last else 6))
                    skips(h - 1, (0, 1))
                if not last:
                    key_unit_lo(h + 1)
                    xm_low(h + 1)
                    if not before_last:
                        next_xm(h + 1)
                if not first:
                    skips(h - 1, (2,))

            pool.wait_ge(gates_out, 16)
            xm_low(0)
            next_xm(0)
            head(0, True, False, False)
            with pool.Fori(1, HEADS - 2) as h:
                head(h, False, False, False)
            head(HEADS - 2, False, False, True)
            head(HEADS - 1, False, True, False)
            z_gate(HEADS - 1)
            pool.wait_ge(hf_done, MC - HC)
            skips(HEADS - 1, range(HC))

            pool.wait_ge(hf_done, 12)
            for b in range(2):
                pool.dma_start(yal[:, b, :], ya_d[b]).then_inc(yl_in[b], 16)
                pool.dma_start(sbl[:, b, :], spill[U_GB - U_XM + b]).then_inc(yl_in[b], 16)
            with pool.Fori(1, KC // 2) as p:
                for b in range(2):
                    pool.wait_ge(mt_done, 2 * p + b - 1)
                    pool.dma_start(yal[:, b, :], ya_d[2 * p + b]).then_inc(yl_in[b], 16)
                    pool.dma_start(sbl[:, b, :], spill[U_GB - U_XM + 2 * p + b]).then_inc(yl_in[b], 16)
            pool.wait_ge(hflo_done, MC)
            pool.dma_start(key_raw[:], a["keys"]).then_inc(key_in, 16)
            for b in range(2):
                pool.dma_start(xres[:, b, :], a["xT"][:, b, :]).then_inc(xr_in[b], 16)

            def add_square(r, d, buf, b):
                pool.wait_ge(qsum_done, (KC + 1) * r + d + 1)
                pool.wait_ge(sq_done, KC * (r + 1) + d + 1)
                pool.tensor_tensor(sq_sum[:], sq_sum[:], buf[:, b, :], ALU.add).then_inc(qsum_done, 1)

            pool.wait_ge(pv_free, MC)
            pool.memset(sq_sum[:], 0.0).then_inc(qsum_done, 1)
            with pool.Fori(0, KC // 2 - 1) as p:
                for b in range(2):
                    add_square(0, 2 * p + b, sq, b)
                    pool.wait_ge(proj_free, O_WO + 2 * p + b + 1)
                    pool.dma_start(xres[:, b, :], a["xT"][:, 2 * p + b + 2, :]).then_inc(xr_in[b], 16)
            for b in range(2):
                add_square(0, KC - 2 + b, sq, b)
            def next_lo(m, k):
                nm, nk = (m, 1) if k == 0 else (m + 1, 0)
                pool.wait_ge(hi_done, 2 * nm + nk + 1)
                pool.tensor_tensor(wlo[:, nk, :], raw[:, nk, :], whi[:, nk, :].bitcast(F32), ALU.subtract)\
                    .then_inc(lo_done, 1)

            pool.wait_ge(proj_free, O_UP)
            pool.dma_start(h2_d, h2[:]).then_inc(h2_out, 16)
            pool.wait_ge(khi_done, 1)
            pool.tensor_tensor(key_lo[:], key_raw[:], key_hi[:].bitcast(F32), ALU.subtract).then_inc(klo_done, 1)
            next_lo(U_HEAD // 2, 0)
            with pool.Fori(0, KC // 2) as p:
                pool.wait_ge(ahi_done, KC + 2 * p + 2)
                pool.tensor_tensor(t_lo[:, 2 * p + 1, :], xt[:, 1, :], t_hi[:, 2 * p + 1, :].bitcast(F32),
                                   ALU.subtract).then_inc(alo_done[1], 1)
            def indices(hd):
                for r in range(2):
                    pool.wait_ge(eq_done, 2 * hd + r + 1)
                    for tb in range(TB):
                        e = eqs[r][:, tb * TOPK:(tb + 1) * TOPK, :]
                        last = pool.tensor_tensor(
                            e, e, i12[:, r, tb, :].unsqueeze(1).to_broadcast([P, TOPK, TOPK]), ALU.mult)
                    last.then_inc(eqm_done, 1)

            def head_lo(hd, units):
                for n in units:
                    next_lo(U_HEAD // 2 + 3 * hd + n // 2, n % 2)

            head_lo(0, range(1, 6))
            with pool.Fori(1, PH) as hd:
                head_lo(hd, (0, 1))
                indices(hd - 1)
                head_lo(hd, (2, 3, 4, 5))
            next_lo(U_FILL // 2, 0)
            indices(PH - 1)
            for jj in (1, 2, 3):
                next_lo((U_FILL + jj) // 2, jj % 2)

            pool.wait_ge(glo_done, 1)
            lo_cols = gate_lo[:].rearrange("p (n w) -> p n w", w=8)

            def hot_low(n, b):
                pool.wait_ge(hotj_done, n + 1)
                pool.tensor_tensor(hot_jg[:, b, :, 1, :], hot_j[:, b, :, :],
                                   lo_cols[:, n, :].unsqueeze(2).to_broadcast([P, 8, P]), ALU.mult)\
                    .then_inc(hotl_done, 1)

            with pool.Fori(0, 16) as r:
                for s in range(2):
                    for q in range(2):
                        hot_low(4 * r + 2 * s + q, q)
                    next_lo(U_GATE // 2 + r, s)

            pool.wait_ge(hot_used, 8 + 256)
            pool.dma_start(h2[:], h2_d).then_inc(h2_in, 16)
            for s in range(2):
                pool.wait_ge(gst_out[s], 16 * 8)
            gg_src = g_d.rearrange("n i (g j) t -> g i n (j t)", j=4)
            for k in range(2):
                pool.wait_ge(up_out[k], 16)
                pool.dma_start(gl[:, k, :], up_d[k]).then_inc(up_in[k], 16)
            pool.dma_start(gg[:, 0, :, :], gg_src[0]).then_inc(g_in, 16)
            pool.wait_ge(g_in, 16)
            pool.dma_start(gg[:, 1, :, :], gg_src[1]).then_inc(g_in, 16)
            for k in range(2):
                pool.wait_ge(actlo_done, k + 1)
                pool.dma_start(gl[:, k, :], up_d[2 + k]).then_inc(up_in[k], 16)
            for k in range(2):
                pool.wait_ge(up_out[k], 16 * 2 * EARLY)
            with pool.Fori(1, EARLY) as g:
                for jj in range(4):
                    pool.wait_ge(actlo_done, 4 * g + jj - 1)
                    pool.dma_start(gl[:, jj % 2, :], up_d[4 * g + jj]).then_inc(up_in[jj % 2], 16)
                    if jj == 1:
                        pool.wait_ge(g_in, 16 * g + 16)
                        pool.wait_ge(gated_done, 4 * g)
                        pool.dma_start(gg[:, (g + 1) % 2, :, :], gg_src[g + 1]).then_inc(g_in, 16)
            with pool.Fori(EARLY, GROUPS_E - 1) as g:
                pool.wait_ge(g_in, 16 * g + 16)
                pool.wait_ge(gated_done, 4 * g)
                pool.dma_start(gg[:, (g + 1) % 2, :, :], gg_src[g + 1]).then_inc(g_in, 16)

            pool.wait_ge(gated_done, 4 * GROUPS_E)
            pool.memset(sq_sum[:], 0.0).then_inc(qsum_done, 1)
            for d in range(KC):
                add_square(1, d, sqf, d % 2)

        @block.scalar
        def _(act):
            def met():
                act.wait_ge(const_done, 4)

            def split_hi(m, k, free=None):
                act.wait_ge(raw_in[k], 16 * m + 16)
                if free is not None:
                    act.wait_ge(*free)
                act.activation(whi[:, k, :], raw[:, k, :], ACT.Copy).then_inc(hi_done, 1)

            def next_hi(m, k, free):
                nm, nk = (m, 1) if k == 0 else (m + 1, 0)
                split_hi(nm, nk, free)

            def root(r):
                act.wait_ge(ms_done, r + 1)
                act.activation(rs[:], ms[:], ACT.Ln).then_inc(ln_done, 1)
                act.wait_ge(ln_done, r + 1)
                act.activation(rs[:], rs[:], ACT.Exp, scale=-0.5).then_inc(rt_done, 1)

            act.wait_ge(const_done, 4)
            act.activation(ones_r[:], ones[:], ACT.Copy).then_inc(onesr_done, 1)
            for d in range(KC):
                if d >= 2:
                    act.wait_ge(ssq_done, d - 1)
                if d % 4 == 0:
                    act.wait_ge(x_in[d // 4], 16)
                act.activation(sq[:, d % 2, :], x[:, d, :], ACT.Square).then_inc(sq_done, 1)
            root(0)
            split_hi(0, 0)
            with act.Fori(0, KC) as d:
                met()
                act.wait_ge(xn_done, d + 1)
                act.activation(hn_hi[:, d, :], x[:, d, :], ACT.Copy).then_inc(ahi_done, 1)

            for nu in range(SC):
                next_hi(nu // 2, nu % 2, (proj_done, nu))
                act.wait_ge(proj_done, nu + 1)
                act.activation(uT[:, nu, :], mm[nu % 2][:], ACT.Copy).then_inc(proj_free, 1)

            def spilled(m, k, func):
                next_hi(m, k, (proj_done, 2 * m + k))
                act.wait_ge(proj_done, 2 * m + k + 1)
                act.wait_ge(stage_out[k], 16 * (m - U_XM // 2))
                act.activation(stage[:, k, :], mm[k][:], func).then_inc(proj_free, 1)
                act.wait_ge(proj_free, 2 * m + k + 1)
                act.dma_start(spill[2 * m + k - U_XM], stage[:, k, :]).then_inc(stage_out[k], 16)

            with act.Fori(U_XM // 2, U_Z // 2) as m:
                for k in range(2):
                    spilled(m, k, ACT.Copy)
            act.wait_ge(ge_sem, 1)
            act.activation(gt[0:HEADS, 2, :], gt[0:HEADS, 1, :], ACT.Exp, scale=-1.0).then_inc(ge_sem, 1)
            with act.Fori(U_Z // 2, U_GA // 2 - 1) as m:
                for k in range(2):
                    spilled(m, k, ACT.Sigmoid)
            act.wait_ge(ge_sem, 3)
            act.activation(gout[0:HEADS, 2, :], gt[0:HEADS, 0, :], ACT.Exp, scale=-1.0).then_inc(gates_done, 1)
            for k in range(2):
                spilled(U_GA // 2 - 1, k, ACT.Sigmoid)

            with act.Fori(0, SC) as c:
                for k in range(4):
                    m = U_GA // 2 + 4 * c + k
                    spilled(m, 0, ACT.Sigmoid)
                    for r in range(2):
                        act.wait_ge(bu_done, 8 * c + 2 * k + r + 1)
                        if r == 0:
                            act.wait_ge(prot_done, 4 * c + k)
                            act.wait_ge(rot_done, 4 * c + k)
                        act.activation(bus[:, r, :], sb_[r][:], ACT.Copy).then_inc(bus_done, 1)
                    spilled(m, 1, ACT.Sigmoid)
                act.wait_ge(yp_done, c + 1)
                act.activation(dtmp[:, 0, :], dtmp[:, 0, :], ACT.Gelu_apprx_tanh).then_inc(yg_done, 1)
                met()
                act.wait_ge(yg_done, c + 1)
                act.activation(y_hi[:, c, :], dtmp[:, 0, :], ACT.Copy).then_inc(yhi_done, 1)

            def conv_high(h, c):
                act.wait_ge(cv_done, 3 * h + c + 1)
                if c == 2:
                    act.wait_ge(xclo_done, 3 * h + 1)
                act.activation(xcf[:, c % 2, :], cv[:, c % 2, :], ACT.Silu).then_inc(silu_done, 1)
                met()
                act.wait_ge(silu_done, 3 * h + c + 1)
                act.activation(xc_hi[:, 3 * h + c, :], xcf[:, c % 2, :], ACT.Copy).then_inc(xchi_done, 1)

            act.wait_ge(bc_in, 16 * (SC + 1))
            act.wait_ge(cm_done, 16)
            act.wait_ge(ylo_done, SC)
            split_hi(U_GLU // 2, 1, (proj_done, O_GLU))
            for c in range(HC):
                conv_high(0, c)

            with act.Fori(0, 4) as q:
                for k in range(2):
                    for b in range(2):
                        act.wait_ge(proj_done, O_GLU + 8 * q + 4 * k + 2 * b + 2)
                        act.wait_ge(proj_free, O_GLU + 8 * q + 4 * k + 2 * b - 2)
                        act.activation(sgt[:, b, :], (mm, pv)[b][1][:], ACT.Sigmoid).then_inc(sg_done, 1)
                    split_hi(U_GLU // 2 + q + 1, k, (proj_done, O_GLU + 8 * q + 4 * k + 4))

            def xm_high(h):
                act.wait_ge(xm_in, 16 * h + 16)
                for c in range(HC):
                    act.activation(xm_hi[:, c, :], xmr[:, c, :], ACT.Copy).then_inc(xmhi_done, 1)

            def tail_squares(h):
                for c in range(HC):
                    act.wait_ge(hc_done, 3 * h + c + 1)
                    act.activation(hsq[c], hh[:, c, :], ACT.Square).then_inc(hsq_done, 1)

            def tail_root(h):
                act.wait_ge(msd_done, h + 1)
                act.activation(rs[:], rd[:], ACT.Ln).then_inc(vln_done, 1)
                act.wait_ge(vln_done, h + 1)
                act.activation(rs[:], rs[:], ACT.Exp, scale=-0.5).then_inc(std_done, 1)

            def tail_high(h):
                for c in range(HC):
                    met()
                    act.wait_ge(hf_done, 3 * h + c + 1)
                    act.activation(xc_hi[:, 3 * h + c, :], hh[:, c, :], ACT.Copy).then_inc(hfhi_done, 1)

            def head(h, first, last):
                def qkv(j):
                    act.wait_ge(proj_done, O_QKV + 10 * h + j + 1)
                    src, scale = mm[j % 2][:], HD ** -0.5 if 3 <= j < 6 else 1.0
                    dst = q_hi[:, j, :] if j < 3 else k_hi[:, j - 3, :] if j < 6 else v_hi[:, j - 6, :]
                    act.activation(dst, src if j < 6 else src[:, 0:HD], ACT.Copy, scale=scale).then_inc(qkv_hi_done, 1)

                def weights(s):
                    act.wait_ge(en_done, 4 * h + s + 1)
                    act.activation(ex[:, s % 2, 0:T - P * s], ex[:, s % 2, 0:T - P * s], ACT.Exp).then_inc(ex_done, 1)

                def weighted_high(s):
                    act.wait_ge(pf_done, 4 * h + s + 1)
                    act.activation(p_hi[:, s, P * s:T], pf[:, s % 2, 0:T - P * s], ACT.Copy).then_inc(phi_done, 1)

                for j in range(4 if first else 2):
                    qkv(j)
                if not last:
                    if not first:
                        act.wait_ge(hf_done, 3 * (h - 1))
                    act.wait_ge(xclo_done, 3 * h + 3)
                    conv_high(h + 1, 0)
                if not first:
                    qkv(2)
                    qkv(3)
                if not last:
                    conv_high(h + 1, 1)
                qkv(4)
                qkv(5)
                if not first:
                    tail_squares(h - 1)
                qkv(6)
                if not last:
                    conv_high(h + 1, 2)
                for j in (7, 8, 9):
                    qkv(j)
                split_hi(U_QKV // 2 + h + 1, 0, (proj_done, O_QKV + 10 * h + 10))
                if not first:
                    tail_root(h - 1)
                weights(0)
                weights(1)
                if not last:
                    split_hi(U_QKV // 2 + h + 1, 1)
                    xm_high(h + 1)
                weighted_high(0)
                weighted_high(1)
                weights(2)
                weights(3)
                if not first:
                    tail_high(h - 1)
                weighted_high(2)
                weighted_high(3)

            act.wait_ge(proj_done, O_QKV)
            xm_high(0)
            head(0, True, False)
            with act.Fori(1, HEADS - 1) as h:
                head(h, False, False)
            head(HEADS - 1, False, True)
            tail_squares(HEADS - 1)
            tail_root(HEADS - 1)
            tail_high(HEADS - 1)

            with act.Fori(0, KC // 2) as p:
                for k in range(2):
                    next_hi(U_YB // 2 + p, k, (proj_done, O_YB + 2 * p + k))
                    met()
                    act.wait_ge(mt_done, 2 * p + k + 1)
                    act.activation(mg_hi[:, 2 * p + k, :], mt[:, k, :], ACT.Copy).then_inc(mghi_done, 1)
            act.wait_ge(key_in, 16)
            act.wait_ge(mglo_done, KC)
            act.activation(key_hi[:], key_raw[:], ACT.Copy).then_inc(khi_done, 1)
            with act.Fori(0, KC // 2) as p:
                for k in range(2):
                    next_hi(U_WO // 2 + p, k, (proj_done, O_WO + 2 * p + k))
                    act.wait_ge(qsum_done, 2 * p + k)
                    act.wait_ge(proj_free, O_WO + 2 * p + k + 1)
                    act.activation(sq[:, k, :], h2[:, 2 * p + k, :], ACT.Square).then_inc(sq_done, 1)
            root(1)
            next_hi(U_HEAD // 2, 0, (proj_done, O_UP))
            with act.Fori(0, KC // 2) as p:
                for k in range(2):
                    met()
                    act.wait_ge(xn_done, KC + 2 * p + k + 1)
                    act.activation(t_hi[:, 2 * p + k, :], xt[:, k, :], ACT.Copy).then_inc(ahi_done, 1)


            def stored_up(half, k):
                n = 2 * half + k
                act.wait_ge(proj_done, O_UP + n + 1)
                act.wait_ge(up_out[k], 16 * half)
                act.activation(sgl[:, k, :], mm[k][:], ACT.Gelu_apprx_tanh).then_inc(proj_free, 1)
                act.wait_ge(proj_free, O_UP + n + 1)
                act.dma_start(up_d[n], sgl[:, k, :]).then_inc(up_out[k], 16)

            def queries(hd, first=False):
                m = U_HEAD // 2 + 3 * hd
                for k in range(2):
                    if k or not first:
                        next_hi(m, k, (proj_done, O_UP + 4 * hd) if k == 0 else (qp_done, 2 * hd + 1))
                    act.wait_ge(qp_done, 2 * hd + k + 1)
                    act.wait_ge(sco_done, 2 * hd)
                    act.activation(qq_hi[:, k, :], pv[k][:], ACT.Copy).then_inc(qhi_done, 1)

            def ups(hd):
                m = U_HEAD // 2 + 3 * hd
                for jj in range(4):
                    next_hi(m + 1 + jj // 2, jj % 2,
                            (qp_done, 2 * hd + 2) if jj == 0 else (proj_done, O_UP + 4 * hd + jj))
                    stored_up(2 * hd + jj // 2, jj % 2)

            def softmax_exp(hd):
                act.wait_ge(gsub_done, hd + 1)
                act.activation(ge[:], ge[:], ACT.Exp).then_inc(gexp_done, 1)

            queries(0, first=True)
            act.wait_ge(klo_done, 1)
            ups(0)
            with act.Fori(1, PH) as hd:
                queries(hd)
                softmax_exp(hd - 1)
                ups(hd)
            for jj in range(4):
                next_hi((U_FILL + jj) // 2, jj % 2, (proj_done, O_UP + N_FILL + jj))
                stored_up((N_FILL + jj) // 2, jj % 2)
                if jj == 1:
                    softmax_exp(PH - 1)
                if jj == 2:
                    for v in range(3):
                        act.wait_ge(tr_done, v + 1)
                        act.activation(gate_hi[:] if v == 0 else slot_t[:, v - 1, :], (dn, pv[0], pv[1])[v][:],
                                       ACT.Copy).then_inc(trc_done, 1)

            with act.Fori(0, 8) as r2:
                for s2 in range(2):
                    block_no = 2 * r2 + s2
                    m = U_GATE // 2 + block_no
                    act.wait_ge(gst_out[s2], 16 * r2)
                    for s in range(2):
                        next_hi(m, s, (proj_done, O_UP + N_GATE + 2 * block_no + s))
                        for b in range(8):
                            act.wait_ge(hot_used, 8 + 16 * block_no + 8 * s + b + 1)
                            act.activation(gst[:, s2, :, 16 * s + 2 * b:16 * s + 2 * b + 2],
                                           bank_parts[b % 4][:, :, 0, :].rearrange("p t j -> p j t"), ACT.Copy)\
                                .then_inc(gcopy_done, 1)
                        stored_up(N_GATE // 2 + block_no, s)
                    act.wait_ge(gps_free, 4 + 16 * block_no + 16)
                    act.dma_start(g_d[block_no], gst[:, s2, :, :]).then_inc(gst_out[s2], 16)

            def act_high(par, jj):
                act.activation(act_hi[:, par, jj, :], gl[:, jj % 2, :], ACT.Copy).then_inc(acthi_done, 1)

            for jj in range(4):
                next_hi((U_LAST + jj) // 2, jj % 2, (proj_done, O_UP + N_LAST + jj))
                stored_up((N_LAST + jj) // 2, jj % 2)
                if jj == 2:
                    for j0 in range(4):
                        act.wait_ge(gated_done, j0 + 1)
                        act_high(0, j0)
            with act.Fori(0, EARLY - 1) as g:
                for jj in range(4):
                    m, k = U_DOWN // 2 + 2 * g + jj // 2, jj % 2
                    act.wait_ge(proj_done, O_UP + 4 * EARLY)
                    next_hi(m, k, (v_done, 16 * g + 4 * jj))
                    met()
                    if jj == 0:
                        act.wait_ge(v_done, 16 * g)
                    act.wait_ge(gated_done, 4 * g + jj + 5)
                    act_high((g + 1) % 2, jj)
            with act.Fori(EARLY - 1, GROUPS_E - 1) as g:
                for jj in range(4):
                    m = U_PAIR // 2 + 4 * (g - (EARLY - 1)) + jj
                    split_hi(m, 1, (v_done, 16 * g + 4 * jj))
                    act.wait_ge(proj_done, O_UP + 4 * g + jj + 5)
                    act.wait_ge(actlo_done, 4 * g + jj + 3)
                    act.activation(gl[:, jj % 2, :], mm[jj % 2][:], ACT.Gelu_apprx_tanh).then_inc(proj_free, 1)
                    split_hi(m + 1, 0, (proj_done, O_UP + 4 * g + jj + 5))
                    met()
                    if jj == 0:
                        act.wait_ge(v_done, 16 * g)
                    act.wait_ge(gated_done, 4 * g + jj + 5)
                    act_high((g + 1) % 2, jj)
            for jj in range(4):
                nu = N_STREAM - 4 + jj + 1
                if jj < 3:
                    split_hi(nu // 2, nu % 2, (v_done, 16 * (GROUPS_E - 1) + 4 * jj))
                for d in range(4 * jj, 4 * jj + 4):
                    act.wait_ge(qsum_done, KC + 1 + d)
                    act.wait_ge(v_free, 4 + 16 * (GROUPS_E - 1) + d + 1)
                    act.activation(sqf[:, d % 2, :], h2[:, d, :], ACT.Square).then_inc(sq_done, 1)
            root(2)


        @block.vector
        def _(dve):
            n = [0]

            def step(ins):
                n[0] += 1
                ins.then_inc(dve_step, 1)
                dve.wait_ge(dve_step, n[0])

            def stepper(s, at):
                k = [0]

                def one(ins, wait=True, apart=False):
                    k[0] += 1
                    ins.then_inc(s, 1)
                    if wait:
                        dve.wait_ge(s, at + k[0])
                    if apart:
                        carrier()
                return one, k

            def carrier():
                dve.sem_inc(waited, 1)

            def split_lo(m, k):
                dve.wait_ge(hi_done, 2 * m + k + 1)
                dve.tensor_tensor(wlo[:, k, :], raw[:, k, :], whi[:, k, :].bitcast(F32), ALU.subtract)\
                    .then_inc(lo_done, 1)

            def next_lo(m, k):
                nm, nk = (m, 1) if k == 0 else (m + 1, 0)
                split_lo(nm, nk)

            def newton(one, y, ms_, tmp):
                one(dve.tensor_tensor(tmp, y, y, ALU.mult))
                one(dve.tensor_tensor(tmp, tmp, ms_, ALU.mult))
                one(dve.tensor_scalar(tmp, tmp, -0.5, 1.5, ALU.mult, ALU.add))
                one(dve.tensor_tensor(y, y, tmp, ALU.mult))

            def norm_scale(r):
                dve.wait_ge(ssq_done, KC + r)
                dve.tensor_scalar(ms[:], st[:], 1.0 / D, EPS, ALU.mult, ALU.add).then_inc(ms_done, 1)
                dve.wait_ge(rt_done, r + 1)
                dve.wait_ge(ms_done, r + 1)
                newton(step, rs[:], ms[:], nt[:])

            def cols(v0, nv):
                return vec[:, v0:v0 + nv].rearrange("p (d o) -> p d o", o=1)

            dve.wait_ge(vec_in, 16)
            norm_scale(0)

            def xn(d):
                dve.scalar_tensor_tensor(x[:, d, :], x[:, d, :], cols(V_G1, KC)[:, d, :], rs[:],
                                         ALU.mult, ALU.mult).then_inc(xn_done, 1)

            def xlo(d):
                dve.wait_ge(ahi_done, d + 1)
                dve.tensor_tensor(hn_lo[:, d, :], x[:, d, :], hn_hi[:, d, :].bitcast(F32), ALU.subtract)\
                    .then_inc(alo_done[0], 1)

            split_lo(0, 0)
            for k in range(2):
                xn(k)
            with dve.Fori(1, KC // 2) as p:
                for k in range(2):
                    xn(2 * p + k)
                xlo(2 * p - 2)
            xlo(KC - 2)

            for nu in range(SC):
                next_lo(nu // 2, nu % 2)

            C = {}

            def col(name):
                if name not in C:
                    C[name] = len(C)
                return cw[:, C[name], :]

            def ts(o, i, s1, s2, o1, o2=None):
                step(dve.tensor_scalar(o, i, s1, s2, o1, o2) if o2 is not None else
                     dve.tensor_scalar(o, i, s1, None, o1))

            def tt(o, i, j, op):
                step(dve.tensor_tensor(o, i, j, op))

            def stt(o, i, s, j, o1, o2):
                step(dve.scalar_tensor_tensor(o, i, s, j, o1, o2))

            radius = col("radius")

            def exp_of(o, i):
                xx, nn, rr, qq = col("xx"), col("nn"), col("rr"), col("qq")
                ts(xx, i, -88.02, 89.0, ALU.max, ALU.min)
                ts(nn, xx, LOG2E, ROUND, ALU.mult, ALU.add)
                ts(nn, nn, -ROUND, None, ALU.add)
                stt(rr, nn, -LN2_HI, xx, ALU.mult, ALU.add)
                stt(rr, nn, -LN2_LO, rr, ALU.mult, ALU.add)
                ts(qq, rr, 1.0 / 5040, None, ALU.mult)
                for c in (1.0 / 720, 1.0 / 120, 1.0 / 24, 1.0 / 6, 0.5, 1.0):
                    stt(qq, qq, c, rr, ALU.add, ALU.mult)
                ts(xx.bitcast(I32), nn, 127.0, 8388608.0, ALU.add, ALU.mult)
                stt(o, qq, 1.0, xx, ALU.add, ALU.mult)

            lre, lim, ldt = (vec[:, v:v + 16] for v in (V_LRE, V_LIM, V_LDT))
            dt, th = col("dt"), col("th")
            exp_of(dt, ldt)
            tt(th, lre, dt, ALU.mult)
            exp_of(radius, th)
            tt(th, lim, dt, ALU.mult)
            nn, rr, zz, ss, co = col("nn"), col("rr"), col("zz"), col("ss"), col("co")
            ts(nn, th, 2.0 / np.pi, ROUND, ALU.mult, ALU.add)
            ts(nn, nn, -ROUND, None, ALU.add)
            stt(rr, nn, -HALF_PI[0], th, ALU.mult, ALU.add)
            stt(rr, nn, -HALF_PI[1], rr, ALU.mult, ALU.add)
            stt(rr, nn, -HALF_PI[2], rr, ALU.mult, ALU.add)
            tt(zz, rr, rr, ALU.mult)
            ts(ss, zz, -1.9515295891e-4, None, ALU.mult)
            stt(ss, ss, 8.3321608736e-3, zz, ALU.add, ALU.mult)
            stt(ss, ss, -1.6666654611e-1, zz, ALU.add, ALU.mult)
            stt(ss, ss, 1.0, rr, ALU.add, ALU.mult)
            ts(co, zz, 2.443315711809948e-5, None, ALU.mult)
            stt(co, co, -1.388731625493765e-3, zz, ALU.add, ALU.mult)
            stt(co, co, 4.166664568298827e-2, zz, ALU.add, ALU.mult)
            stt(co, co, -0.5, zz, ALU.add, ALU.mult)
            ts(co, co, 1.0, None, ALU.add)
            ni, bi, b0, b1 = col("ni").bitcast(I32), col("bi").bitcast(I32), col("b0"), col("b1")
            step(dve.tensor_copy(ni, nn))
            ts(bi, ni, 1, None, ALU.bitwise_and)
            step(dve.tensor_copy(b0, bi))
            ts(bi, ni, 1, 1, ALU.arith_shift_right, ALU.bitwise_and)
            step(dve.tensor_copy(b1, bi))
            ts(b1, b1, -2.0, 1.0, ALU.mult, ALU.add)
            d1, d2, e1, e2 = col("d1"), col("d2"), col("e1"), col("e2")
            ts(d2, b0, -1.0, 1.0, ALU.mult, ALU.add)
            tt(e1, ss, d2, ALU.mult)
            tt(e2, co, b0, ALU.mult)
            tt(e1, e1, e2, ALU.add)
            tt(ptab[:, 1, 0, :], e1, b1, ALU.mult)
            tt(e1, co, d2, ALU.mult)
            tt(e2, ss, b0, ALU.mult)
            tt(e1, e1, e2, ALU.subtract)
            tt(ptab[:, 0, 0, :], e1, b1, ALU.mult)
            for i in range(1, 9):
                c0, s0 = ptab[:, 0, i - 1, :], ptab[:, 1, i - 1, :]
                tt(e1, c0, c0, ALU.mult)
                tt(e2, s0, s0, ALU.mult)
                tt(ptab[:, 0, i, :], e1, e2, ALU.subtract)
                stt(ptab[:, 1, i, :], c0, 2.0, s0, ALU.mult, ALU.mult)
            fr, fi = col("fr"), col("fi")
            tt(d1, radius, ptab[:, 0, 0, :], ALU.mult)
            ts(d1, d1, -1.0, None, ALU.add)
            tt(d2, radius, ptab[:, 1, 0, :], ALU.mult)
            tt(e1, lre, lre, ALU.mult)
            tt(e2, lim, lim, ALU.mult)
            tt(zz, e1, e2, ALU.add)
            step(dve.reciprocal(zz, zz))
            tt(e1, d1, lre, ALU.mult)
            tt(e2, d2, lim, ALU.mult)
            tt(e1, e1, e2, ALU.add)
            tt(fr, e1, zz, ALU.mult)
            tt(e1, d2, lre, ALU.mult)
            tt(e2, d1, lim, ALU.mult)
            tt(e1, e1, e2, ALU.subtract)
            tt(fi, e1, zz, ALU.mult)
            dve.wait_ge(craw_in, 16)
            dve.wait_ge(if_done, 1)
            frb = fr.unsqueeze(2).to_broadcast([P, 16, 32])
            fib = fi.unsqueeze(2).to_broadcast([P, 16, 32])
            cr, ci = craw[:, 0, :, :], craw[:, 1, :, :]
            w0 = dtmp[:, 0, :].rearrange("p (q h) -> p q h", q=16)
            tt(w0, cr, frb, ALU.mult)
            tt(cp[:, 0, :, :], ci, fib, ALU.mult)
            tt(cp[:, 0, :, :], w0, cp[:, 0, :, :], ALU.subtract)
            tt(w0, ci, frb, ALU.mult)
            tt(cp[:, 1, :, :], cr, fib, ALU.mult)
            tt(cp[:, 1, :, :], w0, cp[:, 1, :, :], ALU.add)
            dve.tensor_scalar(cp[:, 1, :, :], cp[:, 1, :, :], -1.0, None, ALU.mult).then_inc(coef_done, 1)

            with dve.Fori(U_XM // 2, U_Z // 2) as m:
                for k in range(2):
                    next_lo(m, k)

            gi, g1, g2, gf = (gt[0:HEADS, i, :] for i in range(4))
            go, gm, g5 = (gout[0:HEADS, i, :] for i in range(3))
            ts(gi, pv[0][0:HEADS, :], vec[0:HEADS, V_BI:V_BI + 1], None, ALU.add)
            ts(gf, pv[0][32:32 + HEADS, :], vec[32:32 + HEADS, V_BF:V_BF + 1], None, ALU.add)
            dve.scalar_tensor_tensor(g1, gf, -1.0, gf, ALU.mult, ALU.max).then_inc(ge_sem, 1)
            with dve.Fori(U_Z // 2, U_GA // 2 - 1) as m:
                for k in range(2):
                    next_lo(m, k)
            dve.wait_ge(ge_sem, 2)
            ts(g1, g2, 2.0, None, ALU.add)
            step(dve.reciprocal(g1, g1))
            tt(g1, g2, g1, ALU.mult)
            tt(go, g1, g1, ALU.mult)
            ts(g2, go, 1.0 / 17, None, ALU.mult)
            for d in (15, 13, 11, 9, 7, 5, 3):
                stt(g2, g2, 1.0 / d, go, ALU.add, ALU.mult)
            stt(g2, g2, 1.0, g1, ALU.add, ALU.mult)
            ts(gf, gf, 0.0, None, ALU.min)
            stt(gf, g2, -2.0, gf, ALU.mult, ALU.add)
            one_b = ones[0:HEADS, 0:1].to_broadcast([HEADS, T])
            step(dve.tensor_tensor_scan(g1, one_b, gf, 0.0, ALU.mult, ALU.add))
            tt(go, gi, g1, ALU.subtract)
            step(dve.tensor_tensor_scan(g2, one_b, go, 0.0, ALU.mult, ALU.max))
            ts(gm, g2, -1.0, None, ALU.mult)
            dve.tensor_tensor(gi, g1, g2, ALU.add).then_inc(ge_sem, 1)
            for k in range(2):
                next_lo(U_GA // 2 - 1, k)

            with dve.Fori(0, SC) as c:
                one, count = stepper(s5_step, S5_STEPS * c)
                dve.wait_ge(chunk_done, c + 1)
                for k in range(4):
                    m = U_GA // 2 + 4 * c + k
                    next_lo(m, 0)
                    dve.wait_ge(out_i_done, 4 * c + k - 1 if k else 4 * c)
                    tc_, ts_ = tab[:, k % 2, 0, :], tab[:, k % 2, 1, :]
                    one(dve.memset(tc_[:, 0:1], 1.0), wait=False)
                    one(dve.memset(ts_[:, 0:1], 0.0))
                    for lv in range(9):
                        w = 1 << lv
                        pcos, psin = pc[:, 0, lv, k:k + 1], pc[:, 1, lv, k:k + 1]
                        one(dve.tensor_scalar(dtmp[:, 0, 0:w], ts_[:, 0:w], psin, None, ALU.mult), wait=False)
                        one(dve.tensor_scalar(dtmp[:, 1, 0:w], ts_[:, 0:w], pcos, None, ALU.mult))
                        one(dve.scalar_tensor_tensor(tc_[:, w:2 * w], tc_[:, 0:w], pcos, dtmp[:, 0, 0:w],
                                                     ALU.mult, ALU.subtract), wait=False)
                        ins = dve.scalar_tensor_tensor(ts_[:, w:2 * w], tc_[:, 0:w], psin, dtmp[:, 1, 0:w],
                                                       ALU.mult, ALU.add)
                        if lv < 8:
                            one(ins)
                        else:
                            ins.then_inc(tab_done, 1)
                    dve.wait_ge(tab_done, 4 * c + k + 1)
                    dve.wait_ge(bus_done, 8 * c + 2 * k + 2)
                    one(dve.tensor_tensor(dtmp[:, 0, :], bus[:, 0, :], tc_, ALU.mult), wait=False)
                    one(dve.tensor_tensor(dtmp[:, 1, :], bus[:, 1, :], ts_, ALU.mult))
                    dve.tensor_tensor(rin[:, 0, :], dtmp[:, 0, :], dtmp[:, 1, :], ALU.add).then_inc(rot_done, 1)
                    dve.wait_ge(rot_done, 4 * c + k + 1)
                    dve.wait_ge(out_i_done, 4 * c + k)
                    rb = rc[:, k:k + 1].to_broadcast([P, T])
                    dve.tensor_tensor_scan(wst[:, 0, :], rb, rin[:, 0, :], 0.0, ALU.mult, ALU.add).then_inc(scan_done, 1)
                    dve.wait_ge(prot_done, 4 * c + k + 1)
                    dve.tensor_tensor_scan(wst[:, 1, :], rb, rin[:, 1, :], 0.0, ALU.mult, ALU.add).then_inc(scan_done, 1)
                    next_lo(m, 1)
                    dve.wait_ge(scan_done, 8 * c + 2 * k + 2)
                    one(dve.tensor_tensor(dtmp[:, 0, :], wst[:, 0, :], tc_, ALU.mult), wait=False)
                    one(dve.tensor_tensor(dtmp[:, 1, :], wst[:, 1, :], ts_, ALU.mult))
                    dve.wait_ge(cm_done, 4 * c + k)
                    dve.tensor_tensor(rout[:, 0, :], dtmp[:, 0, :], dtmp[:, 1, :], ALU.subtract).then_inc(out_r_done, 1)
                dve.wait_ge(out_r_done, 4 * c + 4)
                dve.wait_ge(cm_done, 4 * c + 4)
                dve.scalar_tensor_tensor(dtmp[:, 0, :], uc[:], rc[:, 4:5], dn[:], ALU.mult, ALU.add).then_inc(yp_done, 1)
                dve.wait_ge(yhi_done, c + 1)
                dve.tensor_tensor(y_lo[:, c, :], dtmp[:, 0, :], y_hi[:, c, :].bitcast(F32), ALU.subtract)\
                    .then_inc(ylo_done, 1)
                assert count[0] == S5_STEPS, count

            def conv(one, h, c):
                dve.wait_ge(silu_done, 3 * h + 1 if c == 2 else 3 * h)
                o, i = cv[:, c % 2, :], xmr[:, c, :]
                tap = [cols(V_CW + MC * j, MC)[:, 3 * h + c, :] for j in range(4)]
                one(dve.tensor_scalar(o, i, tap[3], cols(V_CB, MC)[:, 3 * h + c, :], ALU.mult, ALU.add))
                for lag in (1, 2, 3):
                    ins = dve.scalar_tensor_tensor(o[:, lag:T], i[:, 0:T - lag], tap[3 - lag], o[:, lag:T],
                                                   ALU.mult, ALU.add)
                    if lag < 3:
                        one(ins)
                    else:
                        ins.then_inc(cv_done, 1)

            split_lo(U_GLU // 2, 1)
            dve.wait_ge(xm_in, 16)
            for c in range(HC):
                conv(step, 0, c)

            with dve.Fori(0, 4) as q:
                for k in range(2):
                    for b in range(2):
                        f = 4 * q + 2 * k + b
                        dve.wait_ge(sg_done, f + 1)
                        dve.wait_ge(ya_out[b], 16 * (2 * q + k))
                        dve.tensor_tensor(vt[:, b, :], (mm, pv)[b][0][:], sgt[:, b, :], ALU.mult).then_inc(proj_free, 2)
                    split_lo(U_GLU // 2 + q + 1, k)

            def centre(h):
                dve.wait_ge(mu_done, h + 1)
                for c in range(HC):
                    dve.scalar_tensor_tensor(hh[:, c, :], st[:], -1.0 / HD, hh[:, c, :], ALU.mult, ALU.add)\
                        .then_inc(hc_done, 1)

            def variance(h):
                dve.wait_ge(var_done, h + 1)
                dve.tensor_scalar(rd[:], dn[:], 1.0 / HD, EPS, ALU.mult, ALU.add).then_inc(msd_done, 1)

            def scale(one, h, last):
                dve.wait_ge(std_done, h + 1)
                dve.wait_ge(silu_done, MC if last else 3 * h + 6)
                newton(one, rs[:], rd[:], cv[:, 1, :])

            def finish(one, h):
                for c in range(HC):
                    one(dve.tensor_tensor(hh[:, c, :], hh[:, c, :], rs[:], ALU.mult), wait=False)
                    dve.wait_ge(xs_done, 3 * h + c + 1)
                    one(dve.tensor_scalar(xcf[:, c % 2, :], xcf[:, c % 2, :], cols(V_SKIP, MC)[:, 3 * h + c, :], None,
                                          ALU.mult))
                    dve.scalar_tensor_tensor(hh[:, c, :], hh[:, c, :], cols(V_GAIN, MC)[:, 3 * h + c, :],
                                             xcf[:, c % 2, :], ALU.mult, ALU.add).then_inc(hf_done, 1)
                for c in range(HC):
                    dve.wait_ge(hfhi_done, 3 * h + c + 1)
                    dve.tensor_tensor(xc_lo[:, 3 * h + c, :], hh[:, c, :], xc_hi[:, 3 * h + c, :].bitcast(F32),
                                      ALU.subtract).then_inc(hflo_done, 1)

            def head(one, h, first, last):
                def qkv(j):
                    dve.wait_ge(qkv_hi_done, 10 * h + j + 1)
                    src = mm[j % 2]
                    if j < 3:
                        ins = dve.tensor_tensor(q_lo[:, j, :], src[:], q_hi[:, j, :].bitcast(F32), ALU.subtract)
                    elif j < 6:
                        ins = dve.scalar_tensor_tensor(k_lo[:, j - 3, :], src[:], HD ** -0.5,
                                                       k_hi[:, j - 3, :].bitcast(F32), ALU.mult, ALU.subtract)
                    else:
                        ins = dve.tensor_tensor(v_lo[:, j - 6, :], src[:, 0:HD], v_hi[:, j - 6, :].bitcast(F32),
                                                ALU.subtract)
                    ins.then_inc(proj_free, 1)

                def exponent(s):
                    dve.tensor_scalar(ex[:, s % 2, 0:T - P * s], m_bc[:, P * s:T], gcol[:, s:s + 1], 0.0,
                                      ALU.add, ALU.min).then_inc(en_done, 1)

                def weighted(s):
                    w = T - P * s
                    dve.wait_ge(ex_done, 4 * h + s + 1)
                    one(dve.tensor_tensor(ex[:, s % 2, 0:P], ex[:, s % 2, 0:P], tri[:], ALU.mult))
                    dve.wait_ge(s_done, 4 * h + s + 1)
                    dve.tensor_tensor(pf[:, s % 2, 0:w], sb_[s % 2][:, 0:w], ex[:, s % 2, 0:w], ALU.mult)\
                        .then_inc(pf_done, 1)

                def weighted_low(s):
                    dve.wait_ge(phi_done, 4 * h + s + 1)
                    dve.tensor_tensor(p_lo[:, s, P * s:T], pf[:, s % 2, 0:T - P * s],
                                      p_hi[:, s, P * s:T].bitcast(F32), ALU.subtract).then_inc(plo_done, 1)

                for j in range(4 if first else 1):
                    qkv(j)
                if not last:
                    dve.wait_ge(xm_in, 16 * h + 32)
                    conv(one, h + 1, 0)
                if not first:
                    for j in (1, 2, 3):
                        qkv(j)
                if not last:
                    conv(one, h + 1, 1)
                qkv(4)
                qkv(5)
                if not first:
                    centre(h - 1)
                if not last:
                    conv(one, h + 1, 2)
                for j in range(6, 10):
                    qkv(j)
                if not first:
                    variance(h - 1)
                dve.wait_ge(bcst_in, 48 * h + 48)
                exponent(0)
                exponent(1)
                dve.wait_ge(lo_done, U_QKV + 2 * h + 2)
                split_lo(U_QKV // 2 + h + 1, 0)
                if not first:
                    scale(one, h - 1, last)
                weighted(0)
                weighted(1)
                weighted_low(0)
                exponent(2)
                weighted_low(1)
                exponent(3)
                if not first:
                    finish(one, h - 1)
                weighted(2)
                weighted(3)
                weighted_low(2)
                weighted_low(3)
                dve.wait_ge(den_done, h + 1)
                one(dve.scalar_tensor_tensor(rd[:], dn[:], -1.0, em_bc[:], ALU.mult, ALU.max))
                one(dve.tensor_tensor(rd[:], dn[:], rd[:], ALU.max))
                one(dve.reciprocal(rd[:], rd[:]))
                dve.wait_ge(hflo_done, 3 * h)
                for c in range(HC):
                    dve.wait_ge(pv_done, 3 * h + c + 1)
                    dve.tensor_tensor(hh[:, c, :], heads_out[c][:], rd[:], ALU.mult).then_inc(pv_free, 1)

            for b in range(2):
                dve.wait_ge(ya_out[b], 16 * 8)
            one, count = stepper(ml_step, 0)
            head(one, 0, True, False)
            steps0 = count[0]
            with dve.Fori(1, HEADS - 1) as h:
                one, count = stepper(ml_step, steps0 + ML_STEPS * (h - 1))
                head(one, h, False, False)
                assert count[0] == ML_STEPS, count
            one, count = stepper(ml_step, steps0 + ML_STEPS * (HEADS - 2))
            head(one, HEADS - 1, False, True)
            centre(HEADS - 1)
            variance(HEADS - 1)
            scale(one, HEADS - 1, True)
            finish(one, HEADS - 1)

            with dve.Fori(0, KC // 2) as p:
                for k in range(2):
                    next_lo(U_YB // 2 + p, k)
                    dve.wait_ge(yl_in[k], 32 * p + 32)
                    dve.wait_ge(proj_done, O_YB + 2 * p + k + 1)
                    dve.tensor_tensor(mt[:, k, :], mm[k][:], sbl[:, k, :], ALU.mult).then_inc(proj_free, 1)
                    dve.wait_ge(proj_free, O_YB + 2 * p + k + 1)
                    dve.tensor_tensor(mt[:, k, :], mt[:, k, :], yal[:, k, :], ALU.add).then_inc(mt_done, 1)
                    dve.wait_ge(mghi_done, 2 * p + k + 1)
                    dve.tensor_tensor(mg_lo[:, 2 * p + k, :], mt[:, k, :], mg_hi[:, 2 * p + k, :].bitcast(F32),
                                      ALU.subtract).then_inc(mglo_done, 1)
            with dve.Fori(0, KC // 2) as p:
                for k in range(2):
                    next_lo(U_WO // 2 + p, k)
                    dve.wait_ge(xr_in[k], 16 * p + 16)
                    dve.wait_ge(proj_done, O_WO + 2 * p + k + 1)
                    dve.tensor_tensor(h2[:, 2 * p + k, :], mm[k][:], xres[:, k, :], ALU.add).then_inc(proj_free, 1)

            norm_scale(1)

            with dve.Fori(0, KC // 2) as p:
                for k in range(2):
                    dve.wait_ge(alo_done[k], KC // 2 + p)
                    dve.scalar_tensor_tensor(xt[:, k, :], h2[:, 2 * p + k, :], cols(V_G2, KC)[:, 2 * p + k, :], rs[:],
                                             ALU.mult, ALU.mult).then_inc(xn_done, 1)
                dve.wait_ge(ahi_done, KC + 2 * p + 1)
                dve.tensor_tensor(t_lo[:, 2 * p, :], xt[:, 0, :], t_hi[:, 2 * p, :].bitcast(F32), ALU.subtract)\
                    .then_inc(alo_done[0], 1)

            def top16(one, vals, vo_, io_):
                width = vals.shape[-1]
                one(dve.max(vo_[:, 0:8], vals), apart=True)
                one(dve.max_index(io_[:, 0:8], vo_[:, 0:8], vals), wait=False)
                one(dve.match_replace(tw[:, 0:width], vo_[:, 0:8], vals, NEG_BIG), apart=True)
                one(dve.max(vo_[:, 8:16], tw[:, 0:width]), apart=True)
                one(dve.max_index(io_[:, 8:16], vo_[:, 8:16], tw[:, 0:width]), apart=True)

            def query_lo(hd):
                for k in range(2):
                    dve.wait_ge(qhi_done, 2 * hd + k + 1)
                    dve.tensor_tensor(qq_lo[:, k, :], pv[k][:], qq_hi[:, k, :].bitcast(F32), ALU.subtract)\
                        .then_inc(qlo_done, 1)

            def picks(one, hd):
                for k in range(2):
                    dve.wait_ge(sco_done, 2 * hd + k + 1)
                    carrier()
                    for tb in range(TB):
                        top16(one, sb_[k][:, tb * NKEY:(tb + 1) * NKEY], v12[:, k, tb, :], i12u[:, k, tb, :])
                    dve.tensor_copy(i12[:, k, :, :], i12u[:, k, :, :]).then_inc(sco_free, 1)
                one(dve.tensor_tensor(cand[:], v12[:, 0, :, :].unsqueeze(3).to_broadcast([P, TB, TOPK, TOPK]),
                                      v12[:, 1, :, :].unsqueeze(2).to_broadcast([P, TB, TOPK, TOPK]), ALU.add),
                    apart=True)
                for tb in range(TB):
                    top16(one, cand[:, tb, :, :].rearrange("p a b -> p (a b)"), tv[:, tb, :], pos[:, tb, :])
                dve.tensor_tensor(ge[:], tv[:], tv[:, :, 0:1].to_broadcast([P, TB, TOPK]), ALU.subtract)\
                    .then_inc(gsub_done, 1)
                one(dve.tensor_scalar(ab_u[:, 0, :, :], pos[:], 4, None, ALU.logical_shift_right), wait=False)
                one(dve.tensor_scalar(ab_u[:, 1, :, :], pos[:], 15, None, ALU.bitwise_and))
                one(dve.tensor_copy(ab[:], ab_u[:]))
                for r in range(2):
                    dve.wait_ge(sco_free, 2 * hd + 2)
                    dve.tensor_tensor(eqs[r], iota[:, 0:TOPK].unsqueeze(1).to_broadcast([P, TB * TOPK, TOPK]),
                                      ab[:, r, :, :].rearrange("p b k -> p (b k)").unsqueeze(2)
                                      .to_broadcast([P, TB * TOPK, TOPK]), ALU.is_equal).then_inc(eq_done, 1)

            def gates(one, hd):
                dve.wait_ge(gexp_done, hd + 1)
                one(dve.tensor_reduce(gz[:, 0, :], ge[:], AX_X, ALU.add))
                one(dve.reciprocal(gz[:, 1, :], gz[:, 0, :]))
                one(dve.tensor_tensor(slot[:, 0, :, hd, :], ge[:], gz[:, 1, :].unsqueeze(2)
                                      .to_broadcast([P, TB, TOPK]), ALU.mult), wait=False)
                for r in range(2):
                    dve.wait_ge(eqm_done, 2 * hd + r + 1)
                    dve.tensor_reduce(slot[:, 1 + r, :, hd, :], eqs[r].rearrange("p (b k) a -> p b k a", b=TB),
                                      AX_X, ALU.add).then_inc(slot_done, 1)

            one, count = stepper(pk_step, 0)
            query_lo(0)
            picks(one, 0)
            assert count[0] == PICK_STEPS, count
            with dve.Fori(1, PH) as hd:
                one, count = stepper(pk_step, PICK_STEPS + PK_STEPS * (hd - 1))
                query_lo(hd)
                gates(one, hd - 1)
                picks(one, hd)
                assert count[0] == PK_STEPS, count
            one, count = stepper(pk_step, PICK_STEPS + PK_STEPS * (PH - 1))
            gates(one, PH - 1)

            dve.wait_ge(trc_done, 3)
            dve.tensor_tensor(gate_lo[:], dn[:], gate_hi[:].bitcast(F32), ALU.subtract).then_inc(glo_done, 1)
            i_cols, j_cols = (slot_t[:, v, :].rearrange("p (n w) -> p n w", w=8) for v in range(2))
            g_cols = gate_hi[:].bitcast(F32).rearrange("p (n w) -> p n w", w=8)
            iota_b = iota[:].unsqueeze(1).to_broadcast([P, 8, P])
            dve.wait_ge(h2_out, 16)

            def hot_rows(n8, b):
                dve.wait_ge(hot_used, 4 * n8 + 4)
                dve.tensor_tensor(hot_j[:, b, :, :], iota_b, j_cols[:, n8, :].unsqueeze(2).to_broadcast([P, 8, P]),
                                  ALU.is_equal).then_inc(hotj_done, 1)
                dve.tensor_tensor(hot_i[:, b, :, :], iota_b, i_cols[:, n8, :].unsqueeze(2).to_broadcast([P, 8, P]),
                                  ALU.is_equal)
                dve.wait_ge(hotj_done, n8 + 1)
                dve.tensor_tensor(hot_jg[:, b, :, 0, :], hot_j[:, b, :, :],
                                  g_cols[:, n8, :].unsqueeze(2).to_broadcast([P, 8, P]), ALU.mult)\
                    .then_inc(hoth_done, 1)

            def gather(n8, i):
                for b in range(4):
                    dve.wait_ge(gcopy_done, 4 * n8 + b + 1)
                    t0 = 8 * (i % 4) + 2 * b
                    part = gst[:, i // 4, :, t0:t0 + 2]
                    dve.tensor_tensor(part, part, bank_parts[b][:, :, 1, :].rearrange("p t j -> p j t"), ALU.add)\
                        .then_inc(gps_free, 1)

            dve.sem_inc(gps_free, 4)
            with dve.Fori(0, 8) as r:
                for i in range(8):
                    hot_rows(8 * r + i, i % 2)
                    if i > 0:
                        gather(8 * r + i - 1, i - 1)
                gather(8 * r + 7, 7)

            def gate(par, jj):
                g3 = gl[:, jj % 2, :].rearrange("p (n t) -> p n t", n=16)
                dve.tensor_tensor(g3, g3, gg[:, par, :, :].rearrange("p n (j t) -> p n j t", j=4)[:, :, jj, :],
                                  ALU.mult).then_inc(gated_done, 1)

            def act_low(par, jj, num):
                dve.wait_ge(acthi_done, num + 1)
                dve.tensor_tensor(act_lo[:, par, jj, :], gl[:, jj % 2, :], act_hi[:, par, jj, :].bitcast(F32),
                                  ALU.subtract).then_inc(actlo_done, 1)

            def add_down(g, jj):
                for b in range(4):
                    dve.wait_ge(v_done, 16 * g + 4 * jj + b + 1)
                    dve.tensor_tensor(h2[:, 4 * jj + b, :], h2[:, 4 * jj + b, :], vo[b][:], ALU.add)\
                        .then_inc(v_free, 1)

            dve.wait_ge(lo_done, U_LAST + 1)
            for jj in range(4):
                next_lo((U_LAST + jj) // 2, jj % 2)
                if jj == 2:
                    dve.wait_ge(g_in, 16)
                    for j0 in range(4):
                        dve.wait_ge(up_in[j0 % 2], 16 * (j0 // 2) + 16)
                        gate(0, j0)
                        act_low(0, j0, j0)
            dve.wait_ge(h2_in, 16)
            for k in range(2):
                dve.wait_ge(up_out[k], 16 * 2 * EARLY)
            with dve.Fori(0, EARLY - 1) as g:
                dve.wait_ge(g_in, 16 * g + 32)
                for jj in range(4):
                    m, k = U_DOWN // 2 + 2 * g + jj // 2, jj % 2
                    next_lo(m, k)
                    dve.wait_ge(up_in[k], 16 * (2 * g + jj // 2) + 48)
                    gate((g + 1) % 2, jj)
                    act_low((g + 1) % 2, jj, 4 * g + 4 + jj)
                    add_down(g, jj)
            with dve.Fori(EARLY - 1, GROUPS_E - 1) as g:
                dve.wait_ge(g_in, 16 * g + 32)
                for jj in range(4):
                    m = U_PAIR // 2 + 4 * (g - (EARLY - 1)) + jj
                    split_lo(m, 1)
                    dve.wait_ge(proj_free, O_UP + 4 * g + jj + 5)
                    gate((g + 1) % 2, jj)
                    split_lo(m + 1, 0)
                    act_low((g + 1) % 2, jj, 4 * g + 4 + jj)
                    add_down(g, jj)
            for jj in range(4):
                nu = N_STREAM - 4 + jj + 1
                if jj < 3:
                    split_lo(nu // 2, nu % 2)
                add_down(GROUPS_E - 1, jj)

            dve.wait_ge(v_free, 4 + 16 * GROUPS_E)
            norm_scale(2)
            for d in range(KC):
                dve.scalar_tensor_tensor(fin[:, d, :], h2[:, d, :], vec[:, V_GF + d:V_GF + d + 1], rs[:],
                                         ALU.mult, ALU.mult).then_inc(fin_done, 1)

        @block.tensor
        def _(pe):
            def mm3(out, lh, ll, rh, rl, start, stop):
                pe.matmul(out, lh, rh, start=start, stop=False)
                pe.matmul(out, lh, rl, start=False, stop=False)
                return pe.matmul(out, ll, rh, start=False, stop=stop)

            def w(k, c0, width=P):
                return whi[:, k, c0:c0 + width], wlo[:, k, c0:c0 + width]

            def proj(m, k, o, rh, rl, kc=KC, b=None, c0=0, wait=True):
                if wait:
                    pe.wait_ge(lo_done, 2 * m + k + 1)
                pe.wait_ge(proj_free, o - 1)
                out = mm[k if b is None else b][:]
                for d in range(kc):
                    last = mm3(out, *w(k, c0 + P * d), rh[:, d, :], rl[:, d, :], d == 0, d == kc - 1)
                last.then_inc(proj_done, 1)

            def sum_squares(r):
                pe.wait_ge(qsum_done, (KC + 1) * r)
                pe.matmul(st[:], ones[:], sq_sum[:], start=True, stop=True).then_inc(ssq_done, 1)

            pe.wait_ge(const_done, 4)
            for d in range(KC):
                pe.wait_ge(sq_done, d + 1)
                pe.matmul(st[:], ones[:], sq[:, d % 2, :], start=(d == 0), stop=(d == KC - 1)).then_inc(ssq_done, 1)
            pe.wait_ge(lo_done, 1)
            for d in range(KC):
                pe.wait_ge(alo_done[d % 2], d // 2 + 1)
                last = mm3(mm[0][:], *w(0, P * d), hn_hi[:, d, :], hn_lo[:, d, :], d == 0, d == KC - 1)
            last.then_inc(proj_done, 1)
            pe.wait_ge(lo_done, 2)
            for d in range(KC):
                last = mm3(mm[1][:], *w(1, P * d), hn_hi[:, d, :], hn_lo[:, d, :], d == 0, d == KC - 1)
            last.then_inc(proj_done, 1)
            for nu in (2, 3):
                proj(nu // 2, nu % 2, nu, hn_hi, hn_lo)
            pe.wait_ge(wif_in, 16)
            for d in range(KC):
                last = pe.matmul(pv[0][0:64, :], wif[:, d, :], x[:, d, :], start=(d == 0), stop=(d == KC - 1))
            last.then_inc(if_done, 1)
            with pe.Fori(U_XM // 2, U_GA // 2) as m:
                for k in range(2):
                    proj(m, k, 2 * m + k, hn_hi, hn_lo)

            def s5_out(c, k):
                pe.wait_ge(out_r_done, 4 * c + k + 1)
                pe.matmul(dn[32 * k:32 * k + 32, :], cc[:, 0, k, :], rout[:, 0, :], start=True, stop=False)
                pe.wait_ge(out_i_done, 4 * c + k + 1)
                pe.matmul(dn[32 * k:32 * k + 32, :], cc[:, 1, k, :], rout[:, 1, :], start=False, stop=True)\
                    .then_inc(cm_done, 1)

            with pe.Fori(0, SC) as c:
                for k in range(4):
                    m = U_GA // 2 + 4 * c + k
                    proj(m, 0, 2 * m, hn_hi, hn_lo)
                    if k:
                        s5_out(c, k - 1)
                    else:
                        pe.wait_ge(chunk_done, c + 1)
                        pe.wait_ge(bc_in, 16 * c + 16)
                        pe.wait_ge(ylo_done, c)
                    rows = slice(32 * k, 32 * k + 32)
                    pe.wait_ge(bus_done, 8 * c + 2 * k)
                    for r in range(2):
                        pe.matmul(sb_[r][:], bc[rows, r, :], uc[rows, :], start=True, stop=True).then_inc(bu_done, 1)
                    proj(m, 1, 2 * m + 1, hn_hi, hn_lo)
                s5_out(c, 3)

            pe.wait_ge(ylo_done, SC)
            pe.wait_ge(proj_free, O_GLU)
            with pe.Fori(0, 4) as q:
                for k in range(2):
                    pe.wait_ge(lo_done, U_GLU + 2 * q + k + 1)
                    for j in range(4):
                        pe.wait_ge(proj_free, O_GLU + 8 * q + 4 * k + 2 * (j // 2) - 2)
                        for d in range(SC):
                            last = mm3((mm, pv)[j // 2][j % 2][:], *w(k, 512 * j + P * d), y_hi[:, d, :], y_lo[:, d, :],
                                       d == 0, d == SC - 1)
                        last.then_inc(proj_done, 1)

            def mean(h):
                pe.wait_ge(pv_free, 3 * h + 3)
                for c in range(HC):
                    pe.wait_ge(hz_done, 3 * h + c + 1)
                    last = pe.matmul(st[:], ones[:], hh[:, c, :], start=(c == 0), stop=(c == HC - 1))
                last.then_inc(mu_done, 1)

            def squares(h):
                for c in range(HC):
                    pe.wait_ge(hsq_done, 3 * h + c + 1)
                    last = pe.matmul(dn[:], ones[:], hsq[c], start=(c == 0), stop=(c == HC - 1))
                last.then_inc(var_done, 1)

            def head(h, first):
                ma = U_QKV // 2 + h
                o = O_QKV + 10 * h

                def qk(j):
                    pe.wait_ge(proj_free, o + j - 1)
                    for d in range(HC):
                        last = mm3(mm[j % 2][:], *w(j // 3, HD * d + P * (j % 3)), xc_hi[:, 3 * h + d, :],
                                   xc_lo[:, 3 * h + d, :], d == 0, d == HC - 1)
                    last.then_inc(proj_done, 1)

                def value(s):
                    pe.wait_ge(proj_free, o + 6 + s - 1)
                    for d in range(HC):
                        vh, vl = w(0, 3 * HD, HD) if d == 0 else w(1, (2 + d) * HD, HD)
                        ts_ = slice(P * s, P * s + P)
                        last = mm3(mm[s % 2][:, 0:HD], xm_hi[:, d, ts_], xm_lo[:, d, ts_], vh, vl, d == 0, d == HC - 1)
                    last.then_inc(proj_done, 1)

                def scores(s):
                    pe.wait_ge(pf_done, 4 * h + s - 1 if s >= 2 else 4 * h)
                    ks = slice(P * s, P * s + P)
                    for d in range(HC):
                        last = mm3(sb_[s % 2][:, 0:T - P * s], k_hi[:, d, ks], k_lo[:, d, ks],
                                   q_hi[:, d, P * s:T], q_lo[:, d, P * s:T], d == 0, d == HC - 1)
                    last.then_inc(s_done, 1)

                def den(s):
                    pe.wait_ge(plo_done, 4 * h + s + 1)
                    pe.matmul(dn[:, P * s:T], ones_r[:], p_hi[:, s, P * s:T], start=(s == 0), stop=False)
                    return pe.matmul(dn[:, P * s:T], ones_r[:], p_lo[:, s, P * s:T], start=False, stop=(s == TB - 1))

                pe.wait_ge(lo_done, 2 * ma + 1)
                pe.wait_ge(xclo_done, 3 * h + 3)
                for j in range(3):
                    qk(j)
                pe.wait_ge(lo_done, 2 * ma + 2)
                for j in range(3, 6):
                    qk(j)
                if not first:
                    mean(h - 1)
                pe.wait_ge(xmlo_done, 3 * h + 3)
                for s in range(TB):
                    value(s)
                if not first:
                    squares(h - 1)
                pe.wait_ge(proj_free, o + 10)
                for s in range(TB):
                    scores(s)
                pe.wait_ge(msd_done, h)
                for s in range(TB):
                    last = den(s)
                last.then_inc(den_done, 1)
                pe.wait_ge(pv_free, 3 * h)
                pe.wait_ge(hc_done, 3 * h)
                for c in range(HC):
                    cs = slice(P * c, P * c + P)
                    for s in range(TB):
                        last = mm3(heads_out[c][:, P * s:T], v_hi[:, s, cs], v_lo[:, s, cs],
                                   p_hi[:, s, P * s:T], p_lo[:, s, P * s:T], s == 0, s == TB - 1)
                    last.then_inc(pv_done, 1)

            pe.wait_ge(onesr_done, 1)
            head(0, True)
            with pe.Fori(1, HEADS) as h:
                head(h, False)
            mean(HEADS - 1)
            squares(HEADS - 1)

            pe.wait_ge(hflo_done, MC)
            with pe.Fori(0, KC // 2) as p:
                for k in range(2):
                    proj(U_YB // 2 + p, k, O_YB + 2 * p + k, xc_hi, xc_lo, MC)
            pe.wait_ge(mglo_done, KC)
            with pe.Fori(0, KC // 2) as p:
                for k in range(2):
                    proj(U_WO // 2 + p, k, O_WO + 2 * p + k, mg_hi, mg_lo)

            sum_squares(1)
            with pe.Fori(0, PH) as hd:
                m = U_HEAD // 2 + 3 * hd
                for k in range(2):
                    pe.wait_ge(lo_done, 2 * m + k + 1)
                    pe.wait_ge(qlo_done, 2 * hd)
                    for d in range(KC):
                        if k == 0:
                            pe.wait_ge(alo_done[d % 2], KC // 2 + d // 2 + 1)
                        last = mm3(pv[k][:], *w(k, P * d), t_hi[:, d, :], t_lo[:, d, :], d == 0, d == KC - 1)
                    last.then_inc(qp_done, 1)
                proj(m + 1, 0, O_UP + 4 * hd, t_hi, t_lo)
                pe.wait_ge(klo_done, 1)
                for k in range(2):
                    pe.wait_ge(qlo_done, 2 * hd + k + 1)
                    pe.wait_ge(sco_free, 2 * hd)
                    for tb in range(TB):
                        ts_ = slice(P * tb, P * tb + P)
                        last = mm3(sb_[k][:, ts_], qq_hi[:, k, ts_], qq_lo[:, k, ts_],
                                   key_hi[:, hd, k, :], key_lo[:, hd, k, :], True, True)
                    last.then_inc(sco_done, 1)
                for jj in (1, 2, 3):
                    proj(m + 1 + jj // 2, jj % 2, O_UP + 4 * hd + jj, t_hi, t_lo)
            for jj in range(4):
                if jj == 3:
                    pe.wait_ge(slot_done, 2 * PH)
                    pe.wait_ge(qlo_done, 2 * PH)
                    for v in range(3):
                        for tb in range(TB):
                            last = pe.transpose((dn, pv[0], pv[1])[v][:, P * tb:P * tb + P],
                                                slot[:, v, tb, :, :].rearrange("p h k -> p (h k)"), ident[:])
                        last.then_inc(tr_done, 1)
                proj((U_FILL + jj) // 2, jj % 2, O_UP + N_FILL + jj, t_hi, t_lo)

            pe.sem_inc(hot_used, 8)
            with pe.Fori(0, 16) as r:
                for s in range(2):
                    m, n = U_GATE // 2 + r, 2 * r + s
                    pe.wait_ge(lo_done, 2 * m + s + 1)
                    pe.wait_ge(proj_free, O_UP + N_GATE + n - 1)
                    for q in range(2):
                        for d in range(8 * q, 8 * q + 8):
                            last = mm3(mm[s][:], *w(s, P * d), t_hi[:, d, :], t_lo[:, d, :], d == 0, d == KC - 1)
                        if q == 1:
                            last.then_inc(proj_done, 1)
                        pe.wait_ge(hoth_done, 2 * n + q + 1)
                        pe.wait_ge(hotl_done, 2 * n + q + 1)
                        for v in range(8):
                            if v % 2 == 0:
                                pe.wait_ge(gps_free, 8 * n + 4 * q + v // 2 + 1)
                            last = pe.matmul(vo[v // 2][:, 2 * P * (v % 2):2 * P * (v % 2) + 2 * P], hot_i[:, q, v, :],
                                             hot_jg[:, q, v, :, :].rearrange("p a j -> p (a j)"), start=True, stop=True)
                            if v % 2 == 1:
                                last.then_inc(hot_used, 1)
            for jj in range(4):
                proj((U_LAST + jj) // 2, jj % 2, O_UP + N_LAST + jj, t_hi, t_lo)

            def down(k, g, par, m, v0):
                pe.wait_ge(lo_done, 2 * m + k + 1)
                pe.wait_ge(actlo_done, 4 * g + 4)
                for b in range(4):
                    pe.wait_ge(v_free, v0 + b + 1)
                    for jj in range(4):
                        last = mm3(vo[b][:], *w(k, 512 * jj + P * b), act_hi[:, par, jj, :],
                                   act_lo[:, par, jj, :], jj == 0, jj == 3)
                    last.then_inc(v_done, 1)

            pe.wait_ge(gps_free, 4 + 256)
            pe.sem_inc(v_free, 4)
            with pe.Fori(0, EARLY - 1) as g:
                for jj in range(4):
                    down(jj % 2, g, g % 2, U_DOWN // 2 + 2 * g + jj // 2, 16 * g + 4 * jj)
            with pe.Fori(EARLY - 1, GROUPS_E - 1) as g:
                for jj in range(4):
                    m = U_PAIR // 2 + 4 * (g - (EARLY - 1)) + jj
                    proj(m, 0, O_UP + 4 * (g + 1) + jj, t_hi, t_lo, b=jj % 2)
                    down(1, g, g % 2, m, 16 * g + 4 * jj)
            for jj in range(4):
                nu = N_STREAM - 4 + jj
                down(nu % 2, GROUPS_E - 1, (GROUPS_E - 1) % 2, nu // 2, 16 * (GROUPS_E - 1) + 4 * jj)

            sum_squares(2)

def _blocks(w):
    din, f = w.shape
    return w.reshape(din // P, P, f // P, P).transpose(2, 1, 0, 3).reshape(f // P, P, din)


def _stream(i):
    s = np.zeros((N_STREAM, P, UNIT), np.float32)
    w_in = i["w_in"][0]
    z1 = SSM_W + 2 * ML_W
    ga = z1 + 2 * HEADS
    s[U_SSM:U_GA] = _blocks(w_in[:, 0:z1])
    s[U_GA:U_GLU] = _blocks(w_in[:, ga:])
    g = i["w_glu"][0].reshape(SC, P, 2, 8, 2, P).transpose(3, 1, 4, 2, 0, 5)
    s[U_GLU:U_QKV] = g.reshape(8, P, UNIT)
    for h in range(HEADS):
        q, k, v = (i[n][0, h].reshape(HC, P, HD).transpose(1, 0, 2) for n in ("w_q", "w_k", "w_v"))
        a, b = s[U_QKV + 2 * h], s[U_QKV + 2 * h + 1]
        a[:, 0:3 * HD], a[:, 3 * HD:4 * HD] = q.reshape(P, -1), v[:, 0]
        b[:, 0:3 * HD], b[:, 3 * HD:5 * HD] = k.reshape(P, -1), v[:, 1:3].reshape(P, -1)
    s[U_YB:U_WO, :, 0:ML_W] = _blocks(i["w_mlstm_out"][0])
    s[U_WO:U_HEAD] = _blocks(i["w_out"][0])
    up = i["expert_u"][0].reshape(P, P, KC, P).transpose(1, 3, 2, 0).reshape(P, P, UNIT)
    down = i["expert_v"][0].reshape(P, GROUPS_E, 4, 4, 512).transpose(1, 3, 0, 2, 4).reshape(4 * GROUPS_E, P, UNIT)
    heads = s[U_HEAD:U_FILL].reshape(PH, 6, P, UNIT)
    heads[:, 0:2] = _blocks(i["w_query"][0]).reshape(PH, 2, P, UNIT)
    heads[:, 2:6] = up[0:N_FILL].reshape(PH, 4, P, UNIT)
    s[U_FILL:U_DOWN] = up[N_FILL:4 * EARLY]
    s[U_DOWN:U_PAIR] = down[0:4 * (EARLY - 1)]
    s[U_PAIR:N_STREAM - 4:2] = up[4 * EARLY:]
    s[U_PAIR + 1:N_STREAM - 4:2] = down[4 * (EARLY - 1):-4]
    s[N_STREAM - 4:] = down[-4:]
    return s


def _vectors(i):
    v = np.zeros((P, N_VEC), np.float32)

    def put(at, x):
        x = x.reshape(-1, P).T
        v[:, at:at + x.shape[1]] = x

    put(V_G1, i["norm1_g"][0])
    put(V_G2, i["norm2_g"][0])
    put(V_GF, i["norm_f_g"])
    put(V_DSKIP, i["d_skip"][0])
    put(V_CW, i["conv_w"][0])
    put(V_CB, i["conv_b"][0])
    put(V_GAIN, i["mh_gain"][0])
    put(V_SKIP, i["mlstm_skip"][0])
    put(V_LRE, i["lam_re"][0])
    put(V_LIM, i["lam_im"][0])
    put(V_LDT, np.repeat(i["log_dt"][0], STATE))
    v[0:HEADS, V_BI] = i["b_i"][0]
    v[32:32 + HEADS, V_BF] = i["b_f"][0]
    return v


def _s5_tables(i):
    b_tab = np.zeros((SC + 1, P, 2, P), np.float32)
    c_tab = np.zeros((P, 2, 16, 32), np.float32)
    for g in range(GROUPS):
        c, k, half = g // 8, g // 2 % 4, g % 2
        ch, st = 32 * k + GROUP * half, STATE * half
        for r, (b, cm) in enumerate((("b_re", "c_re"), ("b_im", "c_im"))):
            b_tab[c, ch:ch + GROUP, r, st:st + STATE] = i[b][0, g].T
            c_tab[st:st + STATE, r, g // 2, GROUP * half:GROUP * half + GROUP] = i[cm][0, g].T
    return b_tab, c_tab


def kernel(**inputs):
    import concourse.bacc as _bacc
    from concourse.bass_utils import run_bass_kernel_spmd as _run

    i = {k: np.asarray(v) for k, v in inputs.items()}
    w_in = i["w_in"][0]
    z1 = SSM_W + 2 * ML_W
    wif = np.zeros((P, KC, 64), np.float32)
    wif[:, :, 0:HEADS] = w_in[:, z1:z1 + HEADS].reshape(KC, P, HEADS).transpose(1, 0, 2)
    wif[:, :, 32:32 + HEADS] = w_in[:, z1 + HEADS:z1 + 2 * HEADS].reshape(KC, P, HEADS).transpose(1, 0, 2)
    b_tab, c_tab = _s5_tables(i)
    keys = np.stack([i["key1"][0], i["key2"][0]], 1)
    arrays = {
        "xT": np.ascontiguousarray(i["x"][0].reshape(T, KC, P).transpose(2, 1, 0)),
        "stream": _stream(i), "vecs": _vectors(i), "wif": wif, "b_tab": b_tab, "c_tab": c_tab,
        "keys": np.ascontiguousarray(keys.transpose(3, 0, 1, 2)),
    }
    nc = _bacc.Bacc("TRN2", target_bir_lowering=False, num_devices=1)
    args = {n: nc.dram_tensor(n, v.shape, F32, kind="ExternalInput").ap() for n, v in arrays.items()}
    out = nc.dram_tensor("out", (P, KC, T), F32, kind="ExternalOutput").ap()
    build(nc, args, out)
    r = _run(nc, [arrays], core_ids=[0])
    y = r.results[0]["out"]
    return np.ascontiguousarray(y.transpose(2, 1, 0)).reshape(1, T, D)
```
